# Optimizing a Trainium2 kernel written in Bass

```python
import jax, jax.numpy as jnp
from jax import lax
import numpy as np

D_MODEL = 1024
BATCH = 1
SEQ = 1024
DEPTH = 1

HEAD_DIM = D_MODEL // 16
ATTN_HEADS = 8
ATTN_KV_HEADS = 2
ATTN_GROUP = ATTN_HEADS // ATTN_KV_HEADS
ATTN_WIDTH = ATTN_HEADS * HEAD_DIM
KV_WIDTH = ATTN_KV_HEADS * HEAD_DIM
WINDOW = 128
BLOCK = 128
ROPE_THETA = 10000.0
POOL_WINDOWS = (2, 4, 8, 16)
POOL_GROUPS = 4
POOL_WIDTH = D_MODEL - ATTN_WIDTH
POOL_CH = POOL_WIDTH // POOL_GROUPS
MIX_WIDTH = ATTN_WIDTH + POOL_WIDTH
IN_WIDTH = ATTN_WIDTH + 2 * KV_WIDTH + POOL_WIDTH
PEER_HEADS = 8
PEER_N_KEYS = 128
PEER_N_EXPERTS = PEER_N_KEYS * PEER_N_KEYS
PEER_TOPK = 16
PEER_QDIM = 256
PEER_HALF = PEER_QDIM // 2
PEER_CHUNK = 128
DEEPNORM_ALPHA = (2.0 * DEPTH) ** 0.25
DEEPNORM_BETA = (8.0 * DEPTH) ** -0.25
LN_EPS = 1e-5

kernel_name = "hybrid_swa_sink_pool_peer_deepnorm_adaln"

def layer_norm(x, g, b):
    x32 = x.astype(jnp.float32)
    mu = jnp.mean(x32, axis=-1, keepdims=True)
    var = jnp.mean(jnp.square(x32 - mu), axis=-1, keepdims=True)
    return ((x32 - mu) * lax.rsqrt(var + LN_EPS) * g + b).astype(x.dtype)

def rope(t, pos):
    half = t.shape[-1] // 2
    freqs = ROPE_THETA ** (-jnp.arange(half, dtype=jnp.float32) / half)
    ang = pos.astype(jnp.float32)[:, None] * freqs[None, :]
    cos = jnp.cos(ang)[None, :, None, :]
    sin = jnp.sin(ang)[None, :, None, :]
    t32 = t.astype(jnp.float32)
    t1, t2 = t32[..., :half], t32[..., half:]
    return jnp.concatenate([t1 * cos - t2 * sin, t2 * cos + t1 * sin], axis=-1).astype(t.dtype)

def sliding_window_gqa_with_sinks(q, k, v, sinks):
    B, S = q.shape[0], q.shape[1]
    nb = S // BLOCK
    qb = q.reshape(B, nb, BLOCK, ATTN_KV_HEADS, ATTN_GROUP, HEAD_DIM)
    kb = k.reshape(B, nb, BLOCK, ATTN_KV_HEADS, HEAD_DIM)
    vb = v.reshape(B, nb, BLOCK, ATTN_KV_HEADS, HEAD_DIM)
    kcat = jnp.concatenate([jnp.concatenate([jnp.zeros_like(kb[:, :1]), kb[:, :-1]], axis=1), kb], axis=2)
    vcat = jnp.concatenate([jnp.concatenate([jnp.zeros_like(vb[:, :1]), vb[:, :-1]], axis=1), vb], axis=2)
    s = jnp.einsum('bnqhgd,bnshd->bnhgqs', qb, kcat).astype(jnp.float32) * (HEAD_DIM ** -0.5)
    q_idx = jnp.arange(BLOCK)[:, None]
    s_idx = jnp.arange(2 * BLOCK)[None, :]
    rel = q_idx + BLOCK - s_idx
    band = (rel >= 0) & (rel < WINDOW)
    blk = jnp.arange(nb)[:, None, None]
    valid = band[None] & ((blk > 0) | (s_idx[None] >= BLOCK))
    s = jnp.where(valid[None, :, None, None], s, -1e30)
    sink_b = sinks.astype(jnp.float32).reshape(1, 1, ATTN_KV_HEADS, ATTN_GROUP, 1, 1)
    m = jnp.maximum(jnp.max(s, axis=-1, keepdims=True), sink_b)
    p = jnp.exp(s - m)
    denom = jnp.sum(p, axis=-1, keepdims=True) + jnp.exp(sink_b - m)
    probs = (p / denom).astype(v.dtype)
    o = jnp.einsum('bnhgqs,bnshd->bnqhgd', probs, vcat)
    return o.reshape(B, S, ATTN_WIDTH)

def multiscale_causal_pool(p, w_pool, pool_scale):
    B, S, _ = p.shape
    p32 = p.astype(jnp.float32).reshape(B, S, POOL_GROUPS, POOL_CH)
    cs = jnp.cumsum(p32, axis=1)
    t = jnp.arange(S)
    outs = []
    for gi, w in enumerate(POOL_WINDOWS):
        csg = cs[:, :, gi]
        lag = jnp.pad(csg, ((0, 0), (w, 0), (0, 0)))[:, :S]
        cnt = jnp.minimum(t + 1, w).astype(jnp.float32)[None, :, None]
        outs.append((csg - lag) / cnt - p32[:, :, gi])
    pooled = jnp.stack(outs, axis=2).astype(p.dtype)
    y = jnp.einsum('bsgc,gce->bsge', pooled, w_pool).reshape(B, S, POOL_WIDTH)
    return y * pool_scale

def peer_ffn(h, w_pq, peer_k1, peer_k2, peer_u, peer_v):
    B, S, D = h.shape
    q = (h @ w_pq).reshape(B, S, PEER_HEADS, 2, PEER_HALF)
    s1 = jnp.einsum('bshc,kc->bshk', q[..., 0, :], peer_k1).astype(jnp.float32)
    s2 = jnp.einsum('bshc,kc->bshk', q[..., 1, :], peer_k2).astype(jnp.float32)
    v1, i1 = lax.top_k(s1, PEER_TOPK)
    v2, i2 = lax.top_k(s2, PEER_TOPK)
    comb = (v1[..., :, None] + v2[..., None, :]).reshape(B, S, PEER_HEADS, PEER_TOPK * PEER_TOPK)
    vals, flat = lax.top_k(comb, PEER_TOPK)
    e = (jnp.take_along_axis(i1, flat // PEER_TOPK, axis=-1) * PEER_N_KEYS
         + jnp.take_along_axis(i2, flat % PEER_TOPK, axis=-1))
    g = jax.nn.softmax(vals, axis=-1).astype(h.dtype)
    n_chunks = (B * S) // PEER_CHUNK
    xs = h.reshape(n_chunks, PEER_CHUNK, D)
    es = e.reshape(n_chunks, PEER_CHUNK, PEER_HEADS * PEER_TOPK)
    gs = g.reshape(n_chunks, PEER_CHUNK, PEER_HEADS * PEER_TOPK)

    def expert_chunk(args):
        xc, ec, gc = args
        hid = jnp.einsum('td,tkd->tk', xc, peer_u[ec])
        act = jax.nn.gelu(hid, approximate=False) * gc
        return jnp.einsum('tk,tkd->td', act, peer_v[ec])

    out = lax.map(expert_chunk, (xs, es, gs))
    return out.reshape(B, S, D)

def setup_inputs(seed: int = 0) -> dict:
    key = jax.random.key(seed)
    ks = jax.random.split(key, 20)

    def nrm(k, shape, s):
        return jax.random.normal(k, shape, jnp.float32) * s

    col_scale = jnp.concatenate([
        jnp.ones((ATTN_WIDTH + KV_WIDTH,), jnp.float32),
        jnp.full((KV_WIDTH + POOL_WIDTH,), DEEPNORM_BETA, jnp.float32)])
    return {
        "x": nrm(ks[0], (BATCH, SEQ, D_MODEL), 1.0),
        "c": nrm(ks[1], (BATCH, D_MODEL), 1.0),
        "w_ada": nrm(ks[2], (DEPTH, D_MODEL, 6 * D_MODEL), 0.1 * D_MODEL ** -0.5),
        "b_ada": nrm(ks[3], (DEPTH, 6 * D_MODEL), 0.02),
        "w_in": nrm(ks[4], (DEPTH, D_MODEL, IN_WIDTH), D_MODEL ** -0.5) * col_scale,
        "attn_sinks": nrm(ks[5], (DEPTH, ATTN_HEADS), 1.0),
        "w_pool": nrm(ks[6], (DEPTH, POOL_GROUPS, POOL_CH, POOL_CH), POOL_CH ** -0.5),
        "pool_scale": 1.0 + nrm(ks[7], (DEPTH, POOL_WIDTH), 0.02),
        "w_out": nrm(ks[8], (DEPTH, MIX_WIDTH, D_MODEL), DEEPNORM_BETA * MIX_WIDTH ** -0.5),
        "ln1_g": 1.0 + nrm(ks[9], (DEPTH, D_MODEL), 0.02),
        "ln1_b": nrm(ks[10], (DEPTH, D_MODEL), 0.02),
        "w_pq": nrm(ks[11], (DEPTH, D_MODEL, PEER_HEADS * PEER_QDIM), D_MODEL ** -0.5),
        "peer_k1": nrm(ks[12], (DEPTH, PEER_N_KEYS, PEER_HALF), PEER_HALF ** -0.5),
        "peer_k2": nrm(ks[13], (DEPTH, PEER_N_KEYS, PEER_HALF), PEER_HALF ** -0.5),
        "peer_u": nrm(ks[14], (DEPTH, PEER_N_EXPERTS, D_MODEL), D_MODEL ** -0.5),
        "peer_v": nrm(ks[15], (DEPTH, PEER_N_EXPERTS, D_MODEL), DEEPNORM_BETA),
        "ln2_g": 1.0 + nrm(ks[16], (DEPTH, D_MODEL), 0.02),
        "ln2_b": nrm(ks[17], (DEPTH, D_MODEL), 0.02),
    }

def reference(x, c, w_ada, b_ada, w_in, attn_sinks, w_pool, pool_scale, w_out, ln1_g, ln1_b,
              w_pq, peer_k1, peer_k2, peer_u, peer_v, ln2_g, ln2_b):
    B, S, _ = x.shape
    pos = jnp.arange(S, dtype=jnp.int32)
    for l in range(DEPTH):
        mod = jax.nn.silu(c) @ w_ada[l] + b_ada[l]
        shift1, scale1, gate1, shift2, scale2, gate2 = [m[:, None, :] for m in jnp.split(mod, 6, axis=-1)]
        h = x * (1.0 + scale1) + shift1
        proj = h @ w_in[l]
        q = proj[..., :ATTN_WIDTH].reshape(B, S, ATTN_HEADS, HEAD_DIM)
        k = proj[..., ATTN_WIDTH:ATTN_WIDTH + KV_WIDTH].reshape(B, S, ATTN_KV_HEADS, HEAD_DIM)
        v = proj[..., ATTN_WIDTH + KV_WIDTH:ATTN_WIDTH + 2 * KV_WIDTH].reshape(B, S, ATTN_KV_HEADS, HEAD_DIM)
        p_in = proj[..., ATTN_WIDTH + 2 * KV_WIDTH:]
        attn = sliding_window_gqa_with_sinks(rope(q, pos), rope(k, pos), v, attn_sinks[l])
        pool = multiscale_causal_pool(p_in, w_pool[l], pool_scale[l])
        mix = jnp.concatenate([attn, pool], axis=-1) @ w_out[l]
        x = layer_norm(DEEPNORM_ALPHA * x + (1.0 + gate1) * mix, ln1_g[l], ln1_b[l])
        h2 = x * (1.0 + scale2) + shift2
        y = peer_ffn(h2, w_pq[l], peer_k1[l], peer_k2[l], peer_u[l], peer_v[l])
        x = layer_norm(DEEPNORM_ALPHA * x + (1.0 + gate2) * y, ln2_g[l], ln2_b[l])
    return x


_drawn_inputs = setup_inputs


def setup_inputs(seed=0):
    import zlib

    import numpy as np

    out = dict(_drawn_inputs(seed))
    spreads = {}
    factors = {'attn_sinks': 8.0, 'pool_scale': 3.447, 'ln2_g': 2.86, 'ln2_b': 2.874}
    for name, (base, spread) in spreads.items():
        noise = np.random.default_rng([zlib.crc32(name.encode()), seed]).standard_normal(out[name].shape)
        drawn = base * np.exp(spread * noise) if base else spread * noise
        out[name] = __import__('jax').numpy.asarray(drawn.astype(out[name].dtype))
    for name, factor in factors.items():
        out[name] = (out[name] * factor).astype(out[name].dtype)
    return out
```

```python
from contextlib import ExitStack

import concourse.bass as bass
from concourse import mybir

ALU = mybir.AluOpType
ACT = mybir.ActivationFunctionType
AX = mybir.AxisListType
F32 = mybir.dt.float32
F32R = mybir.dt.float32r
BF16 = mybir.dt.bfloat16
U32 = mybir.dt.uint32

P = 128
D = 1024
DC = D // P
SEQ = 1024
TILES = SEQ // P
HD = 64
HALF = HD // 2
HEADS, KV_HEADS = 8, 2
QW, KVW = HEADS * HD, KV_HEADS * HD
POOLS = (2, 4, 8, 16)
PG = len(POOLS)
PW = D - QW
PEER_HEADS, KEYS, TOPK = 8, 128, 16
NQ = 2 * PEER_HEADS
EXPERTS = KEYS * KEYS
ALPHA = 2.0 ** 0.25
EPS = 1e-5
NEG = -1e30
LOWEST = -3.0e38
NB = 512

RECTS = ((0, 2, 16), (2, 8, 5), (8, 16, 1))
CAND = sum((a1 - a0) * w for a0, a1, w in RECTS)
ROW_START = [sum((min(a, a1) - a0) * w for a0, a1, w in RECTS if a > a0) for a in range(TOPK)]
NTH = TOPK - 1

HALF_T = 64
PIECES = SEQ // HALF_T
G2 = 2
GROUPS = KEYS // G2

C_IDENT = 0
C_MASK = C_IDENT + P
C_BAND = C_MASK + 4 * P
C_IOTA = C_BAND + PG * 3 * P
C_START = C_IOTA + P
C_DSTART = C_START + NTH
C_COS = C_DSTART + NTH
C_SIN = C_COS + TILES * HALF
C_WIDTH = C_SIN + TILES * HALF


class Chain:

    def __init__(self, eng, sem):
        self.eng, self.sem, self.n = eng, sem, 0

    def step(self, ins):
        ins.then_inc(self.sem, 1)
        self.n += 1

    def wait(self):
        self.eng.wait_ge(self.sem, self.n)

    def link(self, ins):
        self.step(ins)
        self.wait()

    def clear(self):
        self.wait()
        self.eng.sem_clear(self.sem)
        self.n = 0


def modulation(nc, d, keep):
    CH = 6 * D // NB
    RING = 4
    with ExitStack() as ctx:
        sb = lambda n, s, t=F32: ctx.enter_context(nc.sbuf_tensor(n, s, t))
        sem = lambda n: ctx.enter_context(nc.semaphore(n))
        c_col = sb("c_col", [P, DC])
        c_act = sb("c_act", [P, DC])
        c_rep = sb("c_rep", [P, DC, P])
        ones = sb("ones", [1, P])
        bias = sb("bias", [1, 6 * D])
        wada = sb("wada", [P, RING, DC, NB])
        pool_row = sb("pool_row", [PG, P])
        ps = [ctx.enter_context(nc.psum_tensor(f"ps_mod{i}", [P, NB], F32)) for i in range(2)]
        ps_turn = ctx.enter_context(nc.psum_tensor("ps_turn", [P, PG], F32))
        c_in, const_in, bias_in, silu_done = sem("c_in"), sem("const_in"), sem("bias_in"), sem("silu_done")
        ones_set, rep_ready = sem("ones_set"), sem("rep_ready")
        w_in = [sem(f"wada_in{i}") for i in range(RING)]
        mod_sum, mod_out = sem("mod_sum"), sem("mod_out")
        gate2_out, turned = sem("gate2_out"), sem("pool_turned")
        pool_ready, rows_in = sem("pool_ready"), sem("ada_rows_in")
        block = ctx.enter_context(nc.Block())
        w_view = d["w_ada"].rearrange("a (p j) n -> (a p) j n", j=DC)

        @block.sync
        def _(sp):
            sp.dma_start(c_col[:, :], d["c"].rearrange("a (p j) -> (a p) j", j=DC)).then_inc(c_in, 16)
            sp.dma_start(bias[:, :], d["b_ada"]).then_inc(bias_in, 16)
            for n in range(CH):
                if n >= RING:
                    sp.wait_ge(mod_sum, n - RING + 1)
                sp.dma_start(wada[:, n % RING, :, :],
                             w_view[:, :, n * NB:(n + 1) * NB]).then_inc(w_in[n % RING], 16)
            sp.wait_ge(mod_out, CH)
            sp.dma_start(d["gate2_keep"], keep["mod"][:, 5, :]).then_inc(gate2_out, 16)
            sp.wait_ge(gate2_out, 16)

        @block.gpsimd
        def _(pool):
            nc.gpsimd.memset(ones[:, :], 1.0).then_inc(ones_set, 1)

        @block.scalar
        def _(act):
            act.dma_start(keep["const"][:, :], d["const"]).then_inc(const_in, 16)
            act.dma_start(pool_row[:, :], d["pool_scale"].rearrange("a (g p) -> (a g) p", p=P)).then_inc(rows_in, 16)
            act.wait_ge(c_in, 16)
            nc.scalar.activation(c_act[:, :], c_col[:, :], ACT.Silu).then_inc(silu_done, 1)

        @block.tensor
        def _(pe):
            pe.wait_ge(const_in, 16)
            pe.wait_ge(rows_in, 16)
            nc.tensor.transpose(ps_turn[:, 0:PG], pool_row[:, :], keep["const"][0:PG, 0:PG]).then_inc(turned, 1)
            pe.wait_ge(rep_ready, 1)
            pe.wait_ge(ones_set, 1)
            pe.wait_ge(bias_in, 16)
            for n in range(CH):
                pe.wait_ge(w_in[n % RING], 16 * (n // RING + 1))
                if n >= 2:
                    pe.wait_ge(mod_out, n - 1)
                for j in range(DC):
                    nc.tensor.matmul(ps[n % 2][:, :], c_rep[:, j, :], wada[:, n % RING, j, :], start=(j == 0), stop=False)
                nc.tensor.matmul(ps[n % 2][:, :], ones[:, :], bias[:, n * NB:(n + 1) * NB],
                                 start=False, stop=True).then_inc(mod_sum, 1)

        @block.vector
        def _(dve):
            dve.wait_ge(silu_done, 1)
            for j in range(DC):
                last = nc.vector.tensor_copy(c_rep[:, j, :], c_act[:, j:j + 1].to_broadcast([P, P]))
            last.then_inc(rep_ready, 1)
            dve.wait_ge(turned, 1)
            nc.vector.tensor_copy(keep["pool_col"][:, :], ps_turn[:, :]).then_inc(pool_ready, 1)
            for n in range(CH):
                dve.wait_ge(mod_sum, n + 1)
                kind = n * NB // D
                one = 0.0 if kind in (0, 3) else 1.0
                at = (n * NB) % D
                nc.vector.tensor_scalar_add(keep["mod"][:, kind, at:at + NB], ps[n % 2][:, :], one).then_inc(mod_out, 1)


def mixing(nc, d, keep):
    with ExitStack() as ctx:
        sb = lambda n, s, t=F32: ctx.enter_context(nc.sbuf_tensor(n, s, t))
        sem = lambda n: ctx.enter_context(nc.semaphore(n))
        ps = lambda n, w: ctx.enter_context(nc.psum_tensor(n, [P, w], F32))
        const, mod, h2T = keep["const"], keep["mod"], keep["h2T"]
        ident = const[:, C_IDENT:C_IDENT + P]
        w_in = sb("w_in", [P, DC, QW + 2 * KVW + PW])
        w_out = sb("w_out", [P, DC, D])
        w_pool = sb("w_pool", [P, PG, P])
        ln_g, ln_b = sb("ln1_gain", [P, D]), sb("ln1_bias", [P, D])
        sink = sb("sink", [P, HEADS])
        xt = sb("x_tile", [P, D])
        h = sb("h_tile", [P, D])
        hT = sb("hT", [P, DC, P])
        rot_a, rot_b = sb("rot_a", [P, 10 * HD]), sb("rot_b", [P, 10 * HD])
        qk = sb("qk", [P, 10 * HD])
        qT = sb("qT", [P, 4, P])
        kT = sb("kT", [P, 2, P])
        v = sb("v", [P, 2, KVW])
        pin = sb("pool_in", [P, 2, PW])
        s = sb("scores", [P, 4, 2 * P])
        pT = sb("probsT", [P, 8, P])
        small = sb("small", [P, 5, HEADS])
        pooledT = rot_a
        mixT = sb("mixT", [P, DC, P])
        y = h
        stats, mv, rstd = sb("stats", [P, 2, 6]), sb("mean_var", [P, 2]), sb("rstd", [P, 2])
        power = sb("power", [P, 1])
        h2 = sb("h2", [P, D])
        ps_t, ps_p, ps_s, ps_o = ps("ps_t", 2 * NB), ps("ps_p", 3 * NB), ps("ps_s", 2 * NB), ps("ps_o", NB)

        w_ready, x_in, x1_out = sem("mix_weights_in"), sem("x_in"), sem("x1_out")
        zeroed = sem("zeroed")
        h_ready, h_turned, hT_ready, proj_done = sem("h_ready"), sem("h_turned"), sem("hT_ready"), sem("proj_done")
        rope_done, qk_turned, qkT_ready, vp_ready = sem("rope_done"), sem("qk_turned"), sem("qkT_ready"), sem("vp_ready")
        scores_done, s_ready, negm_ready, exp_done = sem("scores_done"), sem("s_ready"), sem("negm_ready"), sem("exp_done")
        rden_ready, probs_ready, pT_done, pT_ready = sem("rden_ready"), sem("probs_ready"), sem("pT_done"), sem("pT_ready")
        pv_done, mixa_ready, pooled_done, pooledT_ready = sem("pv_done"), sem("mixa_ready"), sem("pooled_done"), sem("pooledT_ready")
        y_done, mixb_ready, out_done, res_done = sem("y_done"), sem("mixb_ready"), sem("out_done"), sem("res_done")
        var_ready, rstd_ready, x1_ready, h2_ready = sem("var_ready"), sem("rstd_ready"), sem("x1_ready"), sem("h2_ready")
        h2_turned, h2T_ready = sem("h2_turned"), sem("h2T_ready")
        dve_chain, act_chain, pool_chain = sem("dve_chain1"), sem("act_chain1"), sem("pool_chain1")
        block = ctx.enter_context(nc.Block())
        x_view = d["x"].rearrange("a (t p) n -> (a t) p n", p=P)

        def over_tiles(eng, body):
            body(0, True)
            with eng.Fori(1, TILES) as i:
                body(i, False)

        @block.sync
        def _(sp):
            sp.dma_start(w_in[:, :, :], d["w_in"].rearrange("a (j p) n -> (a p) j n", p=P)).then_inc(w_ready, 16)
            sp.dma_start(w_pool[:, :, :], d["w_pool"].rearrange("a g p n -> (a p) g n")).then_inc(w_ready, 16)
            sp.dma_start(w_out[:, :, :], d["w_out"].rearrange("a (j p) n -> (a p) j n", p=P)).then_inc(w_ready, 16)

            def body(i, first):
                if not first:
                    sp.wait_ge(res_done, i)
                sp.dma_start(xt[:, :], x_view[i]).then_inc(x_in, 16)
                sp.wait_ge(h2_ready, i + 1)
                sp.dma_start(d["x1_keep"][i], s_x1).then_inc(x1_out, 16)
            s_x1 = y[:, :]
            over_tiles(sp, body)
            sp.wait_ge(x1_out, 16 * TILES)

        @block.gpsimd
        def _(pool):
            nc.gpsimd.memset(kT[:, 0, :], 0.0).then_inc(zeroed, 1)
            nc.gpsimd.memset(v[:, 0, :], 0.0).then_inc(zeroed, 1)
            nc.gpsimd.memset(pin[:, 0, :], 0.0).then_inc(zeroed, 1)
            nc.gpsimd.memset(power[:, :], -0.5).then_inc(zeroed, 1)
            pool.wait_ge(zeroed, 4)
            chain = Chain(pool, pool_chain)

            def body(i, first):
                pool.wait_ge(var_ready, i + 1)
                pool.wait_ge(zeroed, 4)
                nc.gpsimd.tensor_tensor(rstd[:, 0:1], rstd[:, 1:2], power[:, :], ALU.pow).then_inc(rstd_ready, 1)
                pool.wait_ge(x1_ready, i + 1)
                if not first:
                    pool.wait_ge(h2_turned, i)
                pool.wait_ge(zeroed, 4)
                chain.link(nc.gpsimd.tensor_tensor(h2[:, :], y[:, :], mod[:, 4, :], ALU.mult))
                nc.gpsimd.tensor_tensor(h2[:, :], h2[:, :], mod[:, 3, :], ALU.add).then_inc(h2_ready, 1)
                chain.clear()
            over_tiles(pool, body)

        @block.scalar
        def _(act):
            for dst, name in ((ln_g, "ln1_g"), (ln_b, "ln1_b")):
                act.dma_start(dst[:, :], d[name].to_broadcast([P, D])).then_inc(w_ready, 16)
            act.dma_start(sink[:, :], d["attn_sinks"].to_broadcast([P, HEADS])).then_inc(w_ready, 16)
            chain = Chain(act, act_chain)

            def body(i, first):
                act.wait_ge(h_turned, i + 1)
                nc.scalar.activation(hT[:, :, :], ps_t[:, :].rearrange("p (j t) -> p j t", t=P), ACT.Copy).then_inc(hT_ready, 1)
                if not first:
                    act.wait_ge(out_done, i)
                    nc.scalar.activation(kT[:, 0, :], kT[:, 1, :], ACT.Copy)
                    nc.scalar.activation(v[:, 0, :], v[:, 1, :], ACT.Copy)
                    chain.link(nc.scalar.activation(pin[:, 0, :], pin[:, 1, :], ACT.Copy))
                    chain.clear()
                act.wait_ge(proj_done, i + 1)
                nc.scalar.activation(pin[:, 1, :], ps_p[:, 2 * NB:3 * NB], ACT.Copy)
                act.wait_ge(rope_done, i + 1)
                nc.scalar.activation(v[:, 1, :], ps_p[:, QW + KVW:QW + 2 * KVW], ACT.Copy).then_inc(vp_ready, 1)
                act.wait_ge(qk_turned, i + 1)
                nc.scalar.activation(qT[:, :, :], ps_t[:, 0:4 * P].rearrange("p (j t) -> p j t", t=P), ACT.Copy)
                nc.scalar.activation(kT[:, 1, :], ps_t[:, 4 * P:5 * P], ACT.Copy).then_inc(qkT_ready, 1)
                for r in range(2):
                    act.wait_ge(negm_ready, 2 * i + r + 1)
                    for n in range(4):
                        hd = 4 * r + n
                        nc.scalar.activation(s[:, n, :], s[:, n, :], ACT.Exp, bias=small[:, 1, hd:hd + 1],
                                             accum_out=small[:, 2, hd:hd + 1])
                    last = nc.scalar.activation(small[:, 3, 4 * r:4 * r + 4], small[:, 3, 4 * r:4 * r + 4], ACT.Exp)
                    last.then_inc(exp_done, 1)
                    act.wait_ge(exp_done, 2 * i + r + 1)
                    act.wait_ge(rden_ready, 2 * i + r + 1)
                    for n in range(4):
                        hd = 4 * r + n
                        last = nc.scalar.activation(s[:, n, :], s[:, n, :], ACT.Copy, scale=small[:, 4, hd:hd + 1])
                    last.then_inc(probs_ready, 1)
                    act.wait_ge(pT_done, 2 * i + r + 1)
                    if r or not first:
                        act.wait_ge(pv_done, 2 * i + r)
                    nc.scalar.activation(pT[:, :, :], ps_t[:, :].rearrange("p (j t) -> p j t", t=P), ACT.Copy).then_inc(pT_ready, 1)
                act.wait_ge(pv_done, 2 * i + 2)
                nc.scalar.activation(mixT[:, 0:4, :], ps_o[:, :].rearrange("p (j t) -> p j t", t=P), ACT.Copy).then_inc(mixa_ready, 1)
                act.wait_ge(h2_turned, i + 1)
                nc.scalar.activation(h2T[:, :, bass.ds(i * P, P)], ps_t[:, :].rearrange("p (j t) -> p j t", t=P), ACT.Copy).then_inc(h2T_ready, 1)
            over_tiles(act, body)

        @block.tensor
        def _(pe):
            pe.wait_ge(zeroed, 4)

            def body(i, first):
                pe.wait_ge(h_ready, i + 1)
                if not first:
                    pe.wait_ge(h2T_ready, i)
                for j in range(DC):
                    last = nc.tensor.transpose(ps_t[:, j * P:(j + 1) * P], h[:, j * P:(j + 1) * P], ident)
                last.then_inc(h_turned, 1)
                if first:
                    pe.wait_ge(w_ready, 16 * 6)
                pe.wait_ge(hT_ready, i + 1)
                if not first:
                    pe.wait_ge(mixb_ready, i)
                for at, src, width in ((0, 0, QW), (QW, QW, 2 * KVW), (2 * NB, QW + 2 * KVW, PW)):
                    for j in range(DC):
                        last = nc.tensor.matmul(ps_p[:, at:at + width], hT[:, j, :], w_in[:, j, src:src + width],
                                                start=(j == 0), stop=(j == DC - 1))
                last.then_inc(proj_done, 1)
                pe.wait_ge(rope_done, i + 1)
                for j in range(4):
                    nc.tensor.transpose(ps_t[:, j * P:(j + 1) * P], qk[:, j * P:(j + 1) * P], ident)
                nc.tensor.transpose(ps_t[:, 4 * P:5 * P], qk[:, QW:QW + KVW], ident).then_inc(qk_turned, 1)
                pe.wait_ge(qkT_ready, i + 1)
                if not first:
                    pe.wait_ge(res_done, i)

                def score_round(r):
                    for n in range(4):
                        last = nc.tensor.matmul(ps_s[:, n * 2 * P:(n + 1) * 2 * P], qT[HD * r:HD * r + HD, n, :],
                                                kT[HD * r:HD * r + HD, :, :], start=True, stop=True)
                    last.then_inc(scores_done, 1)

                score_round(0)
                pe.wait_ge(vp_ready, i + 1)
                for g in range(PG):
                    own = C_BAND + (3 * g + (0 if first else 1)) * P
                    prev = C_BAND + (3 * g + 2) * P
                    out = ps_p[:, g * P:(g + 1) * P]
                    nc.tensor.matmul(out, pin[:, 1, g * P:(g + 1) * P], const[:, own:own + P], start=True, stop=False)
                    last = nc.tensor.matmul(out, pin[:, 0, g * P:(g + 1) * P], const[:, prev:prev + P], start=False, stop=True)
                last.then_inc(pooled_done, 1)
                pe.wait_ge(s_ready, 2 * i + 1)
                score_round(1)
                pe.wait_ge(pooledT_ready, i + 1)
                for g in range(PG):
                    last = nc.tensor.matmul(ps_p[:, NB + g * P:NB + (g + 1) * P], w_pool[:, g, :],
                                            pooledT[:, g * P:(g + 1) * P], start=True, stop=True)
                last.then_inc(y_done, 1)
                for r in range(2):
                    pe.wait_ge(probs_ready, 2 * i + r + 1)
                    if r:
                        pe.wait_ge(pT_ready, 2 * i + 1)
                    for n in range(8):
                        last = nc.tensor.transpose(ps_t[:, n * P:(n + 1) * P], s[:, n // 2, (n % 2) * P:(n % 2 + 1) * P], ident)
                    last.then_inc(pT_done, 1)
                    pe.wait_ge(pT_ready, 2 * i + r + 1)
                    if r == 0 and not first:
                        pe.wait_ge(mixa_ready, i)
                    for n in range(4):
                        hd = 4 * r + n
                        at = HD * (hd % 2)
                        out = ps_o[at:at + HD, (hd // 2) * P:(hd // 2 + 1) * P]
                        for k in range(2):
                            last = nc.tensor.matmul(out, v[:, k, r * HD:(r + 1) * HD], pT[:, 2 * n + k, :],
                                                    start=(k == 0), stop=(k == 1))
                    last.then_inc(pv_done, 1)
                pe.wait_ge(mixa_ready, i + 1)
                pe.wait_ge(mixb_ready, i + 1)
                for half in range(2):
                    for j in range(DC):
                        last = nc.tensor.matmul(ps_s[:, half * NB:(half + 1) * NB], mixT[:, j, :],
                                                w_out[:, j, half * NB:(half + 1) * NB], start=(j == 0), stop=(j == DC - 1))
                last.then_inc(out_done, 1)
                pe.wait_ge(h2_ready, i + 1)
                for j in range(DC):
                    last = nc.tensor.transpose(ps_t[:, j * P:(j + 1) * P], h2[:, j * P:(j + 1) * P], ident)
                last.then_inc(h2_turned, 1)
            over_tiles(pe, body)

        @block.vector
        def _(dve):
            chain = Chain(dve, dve_chain)
            V = nc.vector
            dve.wait_ge(w_ready, 16 * 6)

            def body(i, first):
                dve.wait_ge(x_in, 16 * i + 16)
                if not first:
                    dve.wait_ge(x1_out, 16 * i)
                chain.link(V.tensor_tensor(h[:, :], xt[:, :], mod[:, 1, :], ALU.mult))
                V.tensor_tensor(h[:, :], h[:, :], mod[:, 0, :], ALU.add).then_inc(h_ready, 1)
                dve.wait_ge(proj_done, i + 1)
                src = ps_p[:, 0:10 * HD].rearrange("p (n a c) -> p n a c", a=2, c=HALF)
                cos = const[:, bass.ds(i * HALF + C_COS, HALF)]
                sin = const[:, bass.ds(i * HALF + C_SIN, HALF)]
                ra = rot_a[:, :].rearrange("p (n a c) -> p n a c", a=2, c=HALF)
                rb = rot_b[:, :].rearrange("p (n a c) -> p n a c", a=2, c=HALF)
                qk4 = qk[:, :].rearrange("p (n a c) -> p n a c", a=2, c=HALF)
                for a in range(2):
                    V.tensor_tensor(ra[:, :, a, :], src[:, :, a, :], cos.unsqueeze(1).to_broadcast([P, 10, HALF]), ALU.mult)
                    last = V.tensor_tensor(rb[:, :, a, :], src[:, :, 1 - a, :], sin.unsqueeze(1).to_broadcast([P, 10, HALF]), ALU.mult)
                chain.link(last)
                for a, op in ((0, ALU.subtract), (1, ALU.add)):
                    by_pair = lambda t: t[:, 0:HEADS, a, :].rearrange("p (g j) c -> p g j c", g=2)
                    V.tensor_tensor(qk4[:, 0:HEADS, a, :].rearrange("p (j g) c -> p g j c", g=2), by_pair(ra), by_pair(rb), op)
                    last = V.tensor_tensor(qk4[:, HEADS:, a, :], ra[:, HEADS:, a, :], rb[:, HEADS:, a, :], op)
                last.then_inc(rope_done, 1)

                def scores_and_max(r):
                    hs = slice(4 * r, 4 * r + 4)
                    dve.wait_ge(scores_done, 2 * i + r + 1)
                    if r:
                        dve.wait_ge(pT_done, 2 * i + 1)
                    mask = const[:, C_MASK:C_MASK + 2 * P] if first else const[:, C_MASK + 2 * P:C_MASK + 4 * P]
                    V.scalar_tensor_tensor(s[:, :, :], ps_s[:, :].rearrange("p (n k) -> p n k", n=4), HD ** -0.5,
                                           mask.unsqueeze(1).to_broadcast([P, 4, 2 * P]), ALU.mult, ALU.add).then_inc(s_ready, 1)
                    dve.wait_ge(s_ready, 2 * i + r + 1)
                    chain.link(V.tensor_reduce(small[:, 0, hs], s[:, :, :], AX.X, ALU.max))
                    chain.link(V.tensor_tensor(small[:, 0, hs], small[:, 0, hs], sink[:, hs], ALU.max))
                    V.tensor_tensor(small[:, 3, hs], sink[:, hs], small[:, 0, hs], ALU.subtract)
                    V.tensor_scalar(small[:, 1, hs], small[:, 0, hs], -1.0, None, ALU.mult).then_inc(negm_ready, 1)

                def denominators(r):
                    hs = slice(4 * r, 4 * r + 4)
                    dve.wait_ge(exp_done, 2 * i + r + 1)
                    chain.link(V.tensor_tensor(small[:, 0, hs], small[:, 2, hs], small[:, 3, hs], ALU.add))
                    V.reciprocal(small[:, 4, hs], small[:, 0, hs]).then_inc(rden_ready, 1)

                scores_and_max(0)
                dve.wait_ge(pooled_done, i + 1)
                V.tensor_copy(pooledT[:, 0:PW], ps_p[:, 0:PW]).then_inc(pooledT_ready, 1)
                denominators(0)
                dve.wait_ge(y_done, i + 1)
                V.tensor_tensor(mixT[:, 4:8, :], ps_p[:, NB:2 * NB].rearrange("p (g t) -> p g t", g=PG),
                                keep["pool_col"][:, :].unsqueeze(2).to_broadcast([P, PG, P]), ALU.mult).then_inc(mixb_ready, 1)
                scores_and_max(1)
                denominators(1)
                dve.wait_ge(out_done, i + 1)
                chain.link(V.tensor_tensor(y[:, :], ps_s[:, :], mod[:, 2, :], ALU.mult))
                V.scalar_tensor_tensor(y[:, :], xt[:, :], ALPHA, y[:, :], ALU.mult, ALU.add).then_inc(res_done, 1)
                dve.wait_ge(res_done, i + 1)
                chain.wait()
                V.bn_stats(stats[:, 0, :], y[:, 0:NB])
                chain.link(V.bn_stats(stats[:, 1, :], y[:, NB:D]))
                chain.link(V.bn_aggr(mv[:, :], stats[:, :, :]))
                V.tensor_scalar_add(rstd[:, 1:2], mv[:, 1:2], EPS).then_inc(var_ready, 1)
                chain.link(V.scalar_tensor_tensor(y[:, :], y[:, :], mv[:, 0:1], ln_g[:, :], ALU.subtract, ALU.mult))
                dve.wait_ge(rstd_ready, i + 1)
                V.scalar_tensor_tensor(y[:, :], y[:, :], rstd[:, 0:1], ln_b[:, :], ALU.mult, ALU.add).then_inc(x1_ready, 1)
                chain.clear()
            over_tiles(dve, body)


def routing(nc, d, keep):
    SLOTS = 8
    with ExitStack() as ctx:
        sb = lambda n, s, t=F32: ctx.enter_context(nc.sbuf_tensor(n, s, t))
        sem = lambda n: ctx.enter_context(nc.semaphore(n))
        ps = lambda n, w: ctx.enter_context(nc.psum_tensor(n, [P, w], F32))
        const, h2T = keep["const"], keep["h2T"]
        ident = const[:, C_IDENT:C_IDENT + P]
        iota = const[:, C_IOTA:C_IOTA + P]
        w_pq = sb("w_pq", [P, DC, NQ * P])
        k_rows = sb("key_rows", [P, 2, P])
        keysT = sb("keysT", [P, 2, P])
        qT = sb("queriesT", [P, 8, P])
        gates = sb("gates", [P, 2, KEYS, HALF_T])
        vals = sb("vals", [P, NQ, TOPK])
        idx_u = sb("idx_u", [P, NQ, TOPK], U32)
        idx = sb("idx", [P, NQ, TOPK], BF16)
        rest = sb("rest", [P, NQ, P])
        cand = sb("cand", [P, PEER_HEADS, CAND])
        cand_rest = rest[:, 0:PEER_HEADS, 0:CAND]
        top = sb("top", [P, PEER_HEADS, TOPK])
        pos_u = sb("pos_u", [P, PEER_HEADS, TOPK], U32)
        pos = sb("pos", [P, PEER_HEADS, TOPK], BF16)
        col = sb("col", [P, PEER_HEADS, TOPK], BF16)
        starts = sb("starts", [P, 2 * NTH + TOPK], BF16)
        step1 = sb("step1", [P, PEER_HEADS, NTH], BF16)
        past = sb("past", [P, PEER_HEADS, TOPK, TOPK], BF16)
        prod = rest[:, PEER_HEADS:NQ, :].rearrange("p n k -> p (n k)").bitcast(BF16).rearrange(
            "p (h k r) -> p h k r", h=PEER_HEADS, k=TOPK)
        red = sb("red", [P, PEER_HEADS, TOPK])
        route = sb("route", [P, 3, P])
        stand = sb("stand", [P, 1])
        gsum = sb("gsum", [P, 2, PEER_HEADS])
        routeT = sb("routeT", [P, 3, P])
        hot1, hot2 = sb("hot1", [P, SLOTS, P]), sb("hot2", [P, SLOTS, P])
        ps_q, ps_s, ps_g = ps("ps_q", 2 * NB), ps("ps_key", 4 * NB), ps("ps_gate", 2 * NB)

        w_ready, keys_turned, keysT_ready = sem("route_weights_in"), sem("keys_turned"), sem("keysT_ready")
        q_done, qT_ready, s_done, s_used = sem("q_done"), sem("qT_ready"), sem("s_done"), sem("s_used")
        top_done, exp_done, route_ready, route_turned, routeT_ready = (
            sem("top_done"), sem("gate_exp_done"), sem("route_ready"), sem("route_turned"), sem("routeT_ready"))
        hot_ready, gate_done, gate_out = sem("hot_ready"), sem("gate_done"), sem("gate_out")
        stored = [sem("gates_stored0"), sem("gates_stored1")]
        starts_ready = sem("starts_ready")
        dve_chain = sem("dve_chain2")
        block = ctx.enter_context(nc.Block())
        GPT = P // SLOTS
        GPH = GPT // 2

        @block.sync
        def _(sp):
            sp.dma_start(k_rows[:, 0, :], d["peer_k1"].rearrange("a k c -> (a k) c")).then_inc(w_ready, 16)
            sp.dma_start(k_rows[:, 1, :], d["peer_k2"].rearrange("a k c -> (a k) c")).then_inc(w_ready, 16)
            sp.dma_start(w_pq[:, :, :], d["w_pq"].rearrange("a (j p) n -> (a p) j n", p=P)).then_inc(w_ready, 16)
            with sp.Fori(0, TILES) as i:
                for half in range(2):
                    sp.wait_ge(gate_out, i * (2 * GPT) + (half + 1) * 2 * GPH)
                    sp.dma_start(d["gates_keep"][2 * i + half], gates[:, half, :, :].rearrange("p k t -> p (k t)")).then_inc(stored[half], 16)
            for half in range(2):
                sp.wait_ge(stored[half], 16 * TILES)

        @block.scalar
        def _(act):
            act.wait_ge(keys_turned, 1)
            nc.scalar.activation(keysT[:, :, :], ps_q[:, 0:2 * P].rearrange("p (a k) -> p a k", a=2), ACT.Copy).then_inc(keysT_ready, 1)

            def body(i, first):
                for r in range(2):
                    act.wait_ge(q_done, 2 * i + r + 1)
                    if r or not first:
                        act.wait_ge(s_done, 2 * i + r)
                    nc.scalar.activation(qT[:, :, :], ps_q[:, :].rearrange("p (n t) -> p n t", t=P), ACT.Copy).then_inc(qT_ready, 1)
                act.wait_ge(top_done, i + 1)
                nc.scalar.activation(red[:, :, :], red[:, :, :], ACT.Exp).then_inc(exp_done, 1)
                act.wait_ge(route_turned, i + 1)
                nc.scalar.activation(routeT[:, :, :], ps_q[:, 0:3 * P].rearrange("p (n t) -> p n t", t=P), ACT.Copy).then_inc(routeT_ready, 1)
                for half in range(2):
                    if not first:
                        act.wait_ge(stored[half], 16 * i)
                    def group(g):
                        for b in range(2):
                            act.wait_ge(gate_done, i * (2 * GPT) + half * 2 * GPH + 2 * g + b + 1)
                            act.wait_ge(keysT_ready, 1)
                            dst = gates[:, half, :, bass.ds(g * SLOTS + 4 * b, 4)]
                            nc.scalar.activation(dst, ps_g[:, b * NB:(b + 1) * NB].rearrange("p (t k) -> p k t", k=KEYS), ACT.Copy).then_inc(gate_out, 1)
                    with act.Fori(0, GPH) as g:
                        group(g)
            body(0, True)
            with act.Fori(1, TILES) as i:
                body(i, False)

        @block.tensor
        def _(pe):
            pe.wait_ge(w_ready, 48)
            for a in range(2):
                last = nc.tensor.transpose(ps_q[:, a * P:(a + 1) * P], k_rows[:, a, :], ident)
            last.then_inc(keys_turned, 1)
            pe.wait_ge(keysT_ready, 1)

            def body(i, first):
                for r in range(2):
                    if r:
                        pe.wait_ge(qT_ready, 2 * i + 1)
                    elif not first:
                        pe.wait_ge(routeT_ready, i)
                    for n in range(8):
                        for j in range(DC):
                            last = nc.tensor.matmul(ps_q[:, n * P:(n + 1) * P], w_pq[:, j, (8 * r + n) * P:(8 * r + n + 1) * P],
                                                    h2T[:, j, bass.ds(i * P, P)], start=(j == 0), stop=(j == DC - 1))
                    last.then_inc(q_done, 1)
                    pe.wait_ge(qT_ready, 2 * i + r + 1)
                    if not first:
                        pe.wait_ge(s_used, i)
                    for n in range(8):
                        at = (8 * r + n) * P
                        last = nc.tensor.matmul(ps_s[:, at:at + P], qT[:, n, :], keysT[:, n % 2, :], start=True, stop=True)
                    last.then_inc(s_done, 1)
                pe.wait_ge(route_ready, i + 1)
                for n in range(3):
                    last = nc.tensor.transpose(ps_q[:, n * P:(n + 1) * P], route[:, n, :], ident)
                last.then_inc(route_turned, 1)

                def group(g, fresh):
                    for b in range(2):
                        pe.wait_ge(hot_ready, i * (2 * GPT) + 2 * g + b + 1)
                        if not fresh:
                            pe.wait_ge(gate_out, i * (2 * GPT) + 2 * g + b - 1)
                        for t in range(4):
                            k = 4 * b + t
                            last = nc.tensor.matmul(ps_g[:, k * P:(k + 1) * P], hot1[:, k, :], hot2[:, k, :], start=True, stop=True)
                        last.then_inc(gate_done, 1)
                group(0, first)
                with pe.Fori(1, GPT) as g:
                    group(g, False)
            body(0, True)
            with pe.Fori(1, TILES) as i:
                body(i, False)

        @block.vector
        def _(dve):
            V = nc.vector
            chain = Chain(dve, dve_chain)
            V.tensor_copy(starts[:, 0:2 * NTH], const[:, C_START:C_START + 2 * NTH]).then_inc(starts_ready, 1)
            V.tensor_copy(starts[:, 2 * NTH:2 * NTH + TOPK], const[:, C_IOTA:C_IOTA + TOPK]).then_inc(starts_ready, 1)
            dve.wait_ge(starts_ready, 2)
            th = starts[:, 0:NTH].unsqueeze(1).to_broadcast([P, P, NTH])
            dth = starts[:, NTH:2 * NTH].unsqueeze(1).to_broadcast([P, P, NTH])
            cols = starts[:, 2 * NTH:].unsqueeze(1).to_broadcast([P, P, TOPK])
            heads4 = [P, PEER_HEADS, TOPK, TOPK]

            def body(i, first):
                dve.wait_ge(s_done, 2 * i + 2)
                V.memset(stand[:, :], 0.0)
                sc = [ps_s[:, n * P:(n + 1) * P] for n in range(NQ)]
                for n in range(NQ):
                    last = V.max(vals[:, n, 0:8], sc[n])
                chain.link(last)
                for n in range(NQ):
                    V.max_index(idx_u[:, n, 0:8], vals[:, n, 0:8], sc[n])
                    last = V.match_replace(rest[:, n, :], vals[:, n, 0:8], sc[n], LOWEST)
                chain.link(last)
                V.memset(stand[:, :], 0.0).then_inc(s_used, 1)
                for n in range(NQ):
                    last = V.max(vals[:, n, 8:16], rest[:, n, :])
                chain.link(last)
                for n in range(NQ):
                    last = V.max_index(idx_u[:, n, 8:16], vals[:, n, 8:16], rest[:, n, :])
                pair = vals[:, :, :].rearrange("p (h a) k -> p h a k", a=2)
                at = 0
                for a0, a1, w in RECTS:
                    m = (a1 - a0) * w
                    shape = [P, PEER_HEADS, a1 - a0, w]
                    last = V.tensor_tensor(cand[:, :, at:at + m].rearrange("p h (a b) -> p h a b", b=w),
                                           pair[:, :, 0, a0:a1].unsqueeze(3).to_broadcast(shape),
                                           pair[:, :, 1, 0:w].unsqueeze(2).to_broadcast(shape), ALU.add)
                    at += m
                chain.link(last)
                V.tensor_copy(idx[:, :, :], idx_u[:, :, :])
                for n in range(PEER_HEADS):
                    last = V.max(top[:, n, 0:8], cand[:, n, :])
                chain.link(last)
                for n in range(PEER_HEADS):
                    V.max_index(pos_u[:, n, 0:8], top[:, n, 0:8], cand[:, n, :])
                    last = V.match_replace(cand_rest[:, n, :], top[:, n, 0:8], cand[:, n, :], LOWEST)
                chain.link(last)
                for n in range(PEER_HEADS):
                    last = V.max(top[:, n, 8:16], cand_rest[:, n, :])
                chain.link(last)
                for n in range(PEER_HEADS):
                    last = V.max_index(pos_u[:, n, 8:16], top[:, n, 8:16], cand_rest[:, n, :])
                V.tensor_tensor(red[:, :, :], top[:, :, :], top[:, :, 0:1].to_broadcast([P, PEER_HEADS, TOPK]), ALU.subtract).then_inc(top_done, 1)
                dve.wait_ge(top_done, i + 1)
                chain.wait()
                pidx = idx[:, :, :].rearrange("p (h a) k -> p h a k", a=2)
                V.tensor_tensor(step1[:, :, :], pidx[:, :, 0, 1:TOPK], pidx[:, :, 0, 0:NTH], ALU.subtract)
                chain.link(V.tensor_copy(pos[:, :, :], pos_u[:, :, :]))
                flat = lambda t: t.rearrange("p h k -> p (h k)")
                deep = past[:, :, :, 0:NTH].rearrange("p h k r -> p (h k) r")
                chain.link(V.tensor_tensor(deep, flat(pos[:, :, :]).unsqueeze(2).to_broadcast([P, P, NTH]), th, ALU.is_ge))
                pdeep = prod[:, :, :, 0:NTH]
                chain.link(V.tensor_tensor(pdeep, past[:, :, :, 0:NTH], step1[:, :, :].unsqueeze(2).to_broadcast([P, PEER_HEADS, TOPK, NTH]), ALU.mult))
                dve.wait_ge(exp_done, i + 1)
                chain.wait()
                V.tensor_reduce(gsum[:, 0, :], red[:, :, :], AX.X, ALU.add)
                r1 = route[:, 0, :].rearrange("p (h k) -> p h k", h=PEER_HEADS)
                r2 = route[:, 1, :].rearrange("p (h k) -> p h k", h=PEER_HEADS)
                rg = route[:, 2, :].rearrange("p (h k) -> p h k", h=PEER_HEADS)
                chain.link(V.tensor_reduce(r1, pdeep, AX.X, ALU.add))
                V.reciprocal(gsum[:, 1, :], gsum[:, 0, :])
                chain.link(V.tensor_tensor(prod[:, :, :, 0:NTH].rearrange("p h k r -> p (h k) r"), deep, dth, ALU.mult))
                V.tensor_tensor(rg, red[:, :, :], gsum[:, 1, :].unsqueeze(2).to_broadcast([P, PEER_HEADS, TOPK]), ALU.mult)
                V.tensor_tensor(r1, r1, pidx[:, :, 0, 0:1].to_broadcast([P, PEER_HEADS, TOPK]), ALU.add)
                chain.link(V.tensor_reduce(r2, pdeep, AX.X, ALU.add))
                chain.link(V.tensor_tensor(col[:, :, :], pos[:, :, :], r2, ALU.subtract))
                chain.link(V.tensor_tensor(past[:, :, :, :].rearrange("p h k r -> p (h k) r"),
                                           flat(col[:, :, :]).unsqueeze(2).to_broadcast([P, P, TOPK]), cols, ALU.is_equal))
                chain.link(V.tensor_tensor(prod[:, :, :, :], past[:, :, :, :], pidx[:, :, 1, :].unsqueeze(2).to_broadcast(heads4), ALU.mult))
                V.tensor_reduce(r2, prod[:, :, :, :], AX.X, ALU.add).then_inc(route_ready, 1)
                chain.clear()
                dve.wait_ge(routeT_ready, i + 1)

                def group(g, fresh):
                    for b in range(2):
                        if not fresh:
                            dve.wait_ge(gate_done, i * (2 * GPT) + 2 * g + b - 1)
                        dve.wait_ge(starts_ready, 2)
                        for t in range(4):
                            k = 4 * b + t
                            tok = bass.ds(g * SLOTS + k, 1)
                            V.tensor_scalar(hot1[:, k, :], iota, routeT[:, 0, tok], routeT[:, 2, tok], ALU.is_equal, ALU.mult)
                            last = V.tensor_scalar(hot2[:, k, :], iota, routeT[:, 1, tok], None, ALU.is_equal)
                        last.then_inc(hot_ready, 1)
                group(0, first)
                with dve.Fori(1, GPT) as g:
                    group(g, False)
            body(0, True)
            with dve.Fori(1, TILES) as i:
                body(i, False)


def split_h2(nc, d, keep):
    with ExitStack() as ctx:
        sem = lambda n: ctx.enter_context(nc.semaphore(n))
        hi_ready, lo_ready = sem("h2_hi_ready"), sem("h2_lo_ready")
        block = ctx.enter_context(nc.Block())
        h2T, hi, lo = keep["h2T"], keep["h_hi"], keep["h_lo"]

        @block.scalar
        def _(act):
            for j in range(DC):
                nc.scalar.activation(hi[:, j, :], h2T[:, j, :], ACT.Copy).then_inc(hi_ready, 1)

        @block.vector
        def _(dve):
            for j in range(DC):
                dve.wait_ge(hi_ready, j + 1)
                nc.vector.tensor_tensor(lo[:, j, :], h2T[:, j, :], hi[:, j, :].bitcast(F32), ALU.subtract).then_inc(lo_ready, 1)


def experts(nc, d, keep):
    with ExitStack() as ctx:
        sb = lambda n, s, t=F32: ctx.enter_context(nc.sbuf_tensor(n, s, t))
        sem = lambda n: ctx.enter_context(nc.semaphore(n))
        ps = lambda n, w: ctx.enter_context(nc.psum_tensor(n, [P, w], F32))
        h_part = (keep["h_hi"], keep["h_lo"])
        acc = keep["acc"]
        ident = keep["ident"][:, :]
        u_raw = sb("u_raw", [P, 2, D])
        v_raw = sb("v_raw", [P, 2, D])
        gate = sb("gate", [P, 2, PIECES, HALF_T])
        uT = [sb("uT_hi", [P, G2, DC, P], F32R), sb("uT_lo", [P, G2, DC, P], F32R)]
        a_part = [sb("act_hi", [P, 2, G2, SEQ], F32R), sb("act_lo", [P, 2, G2, SEQ], F32R)]
        v_part = [sb("v_hi", [P, 2, G2, D], F32R), sb("v_lo", [P, 2, G2, D], F32R)]
        ps_u = ps("ps_u", 2 * NB)
        ps_h = [ps(f"ps_h{b}", 2 * NB) for b in range(2)]
        ps_y = [ps(f"ps_y{b}", NB) for b in range(2)]
        u_in = [sem(f"u_in{b}") for b in range(2)]
        v_in = [sem(f"v_in{b}") for b in range(2)]
        g_in = [sem(f"gate_in{b}") for b in range(2)]
        u_turned, uhi_ready, ulo_ready = sem("u_turned"), sem("uhi_ready"), sem("ulo_ready")
        vhi_ready, vlo_ready = sem("vhi_ready"), sem("vlo_ready")
        hid_done, gelu_done, gated, ahi_ready, alo_ready = sem("hid_done"), sem("gelu_done"), sem("gated"), sem("ahi_ready"), sem("alo_ready")
        y_done, y_added, group_used = sem("y_done2"), sem("y_added"), sem("group_used")
        acc_zero = sem("acc_zero")
        block = ctx.enter_context(nc.Block())
        u_view = d["peer_u"].rearrange("a (k1 k2) n -> (a k1) k2 n", k2=KEYS)
        v_view = d["peer_v"].rearrange("a (k1 k2) n -> (a k1) k2 n", k2=KEYS)
        g_view = d["gates_keep"].rearrange("c p (k t) -> p k c t", t=HALF_T)
        YP = 2 * TILES

        def over_groups(eng, body):
            body(0, 0, True)
            body(1, 1, True)
            with eng.Fori(1, GROUPS // 2) as m:
                body(2 * m, 0, False)
                body(2 * m + 1, 1, False)

        @block.sync
        def _(sp):
            def body(g, slot, first):
                for e in range(G2):
                    step = 2 * g + e
                    fresh = first and slot == 0
                    if not fresh:
                        sp.wait_ge(u_turned, step - 1)
                    sp.dma_start(u_raw[:, e, :], u_view[:, step, :] if isinstance(step, int) else u_view[:, bass.ds(step, 1), :].rearrange("p a n -> p (a n)")).then_inc(u_in[e], 16)
                    if not fresh:
                        sp.wait_ge(gated, step - 1)
                    sp.dma_start(gate[:, e, :, :], g_view[:, step, :, :] if isinstance(step, int) else g_view[:, bass.ds(step, 1), :, :].rearrange("p a c t -> p (a c) t")).then_inc(g_in[e], 16)
                    if not fresh:
                        sp.wait_ge(vlo_ready, step - 1)
                    sp.dma_start(v_raw[:, e, :], v_view[:, step, :] if isinstance(step, int) else v_view[:, bass.ds(step, 1), :].rearrange("p a n -> p (a n)")).then_inc(v_in[e], 16)
            over_groups(sp, body)

        @block.gpsimd
        def _(pool):
            nc.gpsimd.memset(acc[:, :, :], 0.0).then_inc(acc_zero, 1)

            def body(g, slot, first):
                for e in range(G2):
                    step = 2 * g + e
                    pool.wait_ge(vhi_ready, step + 1)
                    pool.wait_ge(acc_zero, 1)
                    nc.gpsimd.tensor_tensor(v_part[1][:, slot, e, :], v_raw[:, e, :], v_part[0][:, slot, e, :].bitcast(F32), ALU.subtract).then_inc(vlo_ready, 1)
            over_groups(pool, body)

        @block.scalar
        def _(act):
            def u_hi(e, step, fresh):
                act.wait_ge(u_turned, step + 1)
                if not fresh:
                    act.wait_ge(hid_done, step - 1)
                nc.scalar.activation(uT[0][:, e, :, :], ps_u[:, :].rearrange("p (j k) -> p j k", k=P), ACT.Copy).then_inc(uhi_ready, 1)

            def body(g, slot, first):
                for e in range(G2):
                    step = 2 * g + e
                    if first and slot == 0:
                        u_hi(e, step, True)
                    act.wait_ge(v_in[e], 16 * g + 16)
                    if not first:
                        act.wait_ge(group_used, g - 1)
                    nc.scalar.activation(v_part[0][:, slot, e, :], v_raw[:, e, :], ACT.Copy).then_inc(vhi_ready, 1)
                for e in range(G2):
                    step = 2 * g + e
                    act.wait_ge(hid_done, step + 1)
                    nc.scalar.activation(ps_h[e][:, :], ps_h[e][:, :], ACT.Gelu).then_inc(gelu_done, 1)
                    next_u(g, e, step)
                    act.wait_ge(gated, step + 1)
                    nc.scalar.activation(a_part[0][:, slot, e, :], ps_h[e][:, :], ACT.Copy).then_inc(ahi_ready, 1)

            def next_u(g, e, step):
                if isinstance(g, int) and g == GROUPS - 1:
                    return
                u_hi(e, step + 2, False)
            body(0, 0, True)
            body(1, 1, True)
            with act.Fori(1, GROUPS // 2 - 1) as m:
                body(2 * m, 0, False)
                body(2 * m + 1, 1, False)
            body(GROUPS - 2, 0, False)
            body(GROUPS - 1, 1, False)

        @block.tensor
        def _(pe):
            def turn(e, step, fresh):
                pe.wait_ge(u_in[e], 8 * (step - e) + 16)
                if not fresh:
                    pe.wait_ge(ulo_ready, step)
                for j in range(DC):
                    last = nc.tensor.transpose(ps_u[:, j * P:(j + 1) * P], u_raw[:, e, j * P:(j + 1) * P], ident)
                last.then_inc(u_turned, 1)

            def hidden(e, step, fresh):
                pe.wait_ge(ulo_ready, step + 1)
                if not fresh:
                    pe.wait_ge(alo_ready, step - 1)
                for half in range(2):
                    n = 0
                    for a, b in ((0, 0), (0, 1), (1, 0)):
                        for j in range(DC):
                            last = nc.tensor.matmul(ps_h[e][:, half * NB:(half + 1) * NB], uT[a][:, e, j, :],
                                                    h_part[b][:, j, half * NB:(half + 1) * NB],
                                                    start=(n == 0), stop=(n == 3 * DC - 1))
                            n += 1
                last.then_inc(hid_done, 1)

            def output(g, slot, fresh):
                pe.wait_ge(alo_ready, 2 * g + 2)
                pe.wait_ge(vlo_ready, 2 * g + 2)
                for q in range(YP):
                    t, half = q // 2, q % 2
                    if not fresh or q >= 2:
                        pe.wait_ge(y_added, g * YP + q - 1)
                    n = 0
                    for e in range(G2):
                        for a, b in ((0, 0), (0, 1), (1, 0)):
                            last = nc.tensor.matmul(ps_y[q % 2][:, :], a_part[a][:, slot, e, t * P:(t + 1) * P],
                                                    v_part[b][:, slot, e, half * NB:(half + 1) * NB],
                                                    start=(n == 0), stop=(n == 3 * G2 - 1))
                            n += 1
                    last.then_inc(y_done, 1)
                pe.wait_ge(y_done, (g + 1) * YP)
                nc.tensor.nop().then_inc(group_used, 1)

            def body(g, slot, first, last=False):
                for e in range(G2):
                    hidden(e, 2 * g + e, first and slot == 0)
                    if not last:
                        turn(e, 2 * g + 2 + e, False)
                if not (first and slot == 0):
                    output(g - 1, 1 - slot, first)

            turn(0, 0, True)
            turn(1, 1, False)
            body(0, 0, True)
            body(1, 1, True)
            with pe.Fori(1, GROUPS // 2 - 1) as m:
                body(2 * m, 0, False)
                body(2 * m + 1, 1, False)
            body(GROUPS - 2, 0, False)
            body(GROUPS - 1, 1, False, last=True)
            output(GROUPS - 1, 1, False)

        @block.vector
        def _(dve):
            V = nc.vector

            def u_lo(e, step):
                dve.wait_ge(uhi_ready, step + 1)
                V.tensor_tensor(uT[1][:, e, :, :], ps_u[:, :].rearrange("p (j k) -> p j k", k=P), uT[0][:, e, :, :].bitcast(F32), ALU.subtract).then_inc(ulo_ready, 1)

            def add_out(g, fresh):
                for q in range(YP):
                    t, half = q // 2, q % 2
                    dve.wait_ge(y_done, g * YP + q + 1)
                    if not fresh and q == 0:
                        dve.wait_ge(y_added, g * YP)
                    dst = acc[:, t, half * NB:(half + 1) * NB]
                    V.tensor_tensor(dst, ps_y[q % 2][:, :], dst, ALU.add).then_inc(y_added, 1)

            def body(g, slot, first, last=False):
                for e in range(G2):
                    step = 2 * g + e
                    dve.wait_ge(g_in[e], 16 * g + 16)
                    dve.wait_ge(gelu_done, step + 1)
                    V.tensor_tensor(ps_h[e][:, :], ps_h[e][:, :], gate[:, e, :, :].rearrange("p c t -> p (c t)"), ALU.mult).then_inc(gated, 1)
                    if not last:
                        u_lo(e, step + 2)
                    dve.wait_ge(ahi_ready, step + 1)
                    V.tensor_tensor(a_part[1][:, slot, e, :], ps_h[e][:, :], a_part[0][:, slot, e, :].bitcast(F32), ALU.subtract).then_inc(alo_ready, 1)
                if not (first and slot == 0):
                    add_out(g - 1, first)

            dve.wait_ge(acc_zero, 1)
            u_lo(0, 0)
            u_lo(1, 1)
            body(0, 0, True)
            body(1, 1, True)
            with dve.Fori(1, GROUPS // 2 - 1) as m:
                body(2 * m, 0, False)
                body(2 * m + 1, 1, False)
            body(GROUPS - 2, 0, False)
            body(GROUPS - 1, 1, False, last=True)
            add_out(GROUPS - 1, False)


def final(nc, d, keep):
    with ExitStack() as ctx:
        sb = lambda n, s, t=F32: ctx.enter_context(nc.sbuf_tensor(n, s, t))
        sem = lambda n: ctx.enter_context(nc.semaphore(n))
        acc = keep["acc"]
        gate2, ln_g, ln_b = sb("gate2", [P, D]), sb("ln2_gain", [P, D]), sb("ln2_bias", [P, D])
        x1 = sb("x1", [P, TILES, D])
        stats, mv = sb("stats2", [P, TILES, 2, 6]), sb("mean_var2", [P, TILES, 2])
        rstd, power = sb("rstd2", [P, TILES, 2]), sb("power2", [P, 1])
        rows_in, x1_in, power_set = sem("final_rows_in"), sem("x1_in"), sem("power_set")
        var_ready, rstd_ready, out_ready, out_stored = sem("var2_ready"), sem("rstd2_ready"), sem("out_ready"), sem("out_stored")
        dve_chain = sem("dve_chain4")
        block = ctx.enter_context(nc.Block())

        @block.sync
        def _(sp):
            sp.dma_start(gate2[:, :], d["gate2_keep"]).then_inc(rows_in, 16)
            sp.dma_start(x1[:, :, :], d["x1_keep"].rearrange("t p n -> p t n")).then_inc(x1_in, 16)
            for t in range(TILES):
                sp.wait_ge(out_ready, t + 1)
                sp.dma_start(d["out"].rearrange("a (t p) n -> (a t) p n", p=P)[t], acc[:, t, :]).then_inc(out_stored, 16)
            sp.wait_ge(out_stored, 16 * TILES)

        @block.gpsimd
        def _(pool):
            nc.gpsimd.memset(power[:, :], -0.5).then_inc(power_set, 1)
            pool.wait_ge(power_set, 1)
            for t in range(TILES):
                pool.wait_ge(var_ready, t + 1)
                nc.gpsimd.tensor_tensor(rstd[:, t, 0:1], rstd[:, t, 1:2], power[:, :], ALU.pow).then_inc(rstd_ready, 1)

        @block.scalar
        def _(act):
            act.dma_start(ln_g[:, :], d["ln2_g"].to_broadcast([P, D])).then_inc(rows_in, 16)
            act.dma_start(ln_b[:, :], d["ln2_b"].to_broadcast([P, D])).then_inc(rows_in, 16)

        @block.vector
        def _(dve):
            V = nc.vector
            chain = Chain(dve, dve_chain)
            dve.wait_ge(rows_in, 48)
            dve.wait_ge(x1_in, 16)
            for t in range(TILES):
                y = acc[:, t, :]
                chain.link(V.tensor_tensor(y, y, gate2[:, :], ALU.mult))
                chain.link(V.scalar_tensor_tensor(y, x1[:, t, :], ALPHA, y, ALU.mult, ALU.add))
                V.bn_stats(stats[:, t, 0, :], acc[:, t, 0:NB])
                chain.link(V.bn_stats(stats[:, t, 1, :], acc[:, t, NB:D]))
                chain.link(V.bn_aggr(mv[:, t, :], stats[:, t, :, :]))
                V.tensor_scalar_add(rstd[:, t, 1:2], mv[:, t, 1:2], EPS).then_inc(var_ready, 1)
                chain.link(V.scalar_tensor_tensor(y, y, mv[:, t, 0:1], ln_g[:, :], ALU.subtract, ALU.mult))
                dve.wait_ge(rstd_ready, t + 1)
                V.scalar_tensor_tensor(y, y, rstd[:, t, 0:1], ln_b[:, :], ALU.mult, ALU.add).then_inc(out_ready, 1)


def build(nc, d):
    d["gate2_keep"] = nc.dram_tensor("gate2_keep", [P, D], F32, kind="Internal").ap()
    d["x1_keep"] = nc.dram_tensor("x1_keep", [TILES, P, D], F32, kind="Internal").ap()
    d["gates_keep"] = nc.dram_tensor("gates_keep", [PIECES, P, KEYS * HALF_T], F32, kind="Internal").ap()
    keep = {}
    with ExitStack() as ctx:
        sb = lambda n, s, t=F32: ctx.enter_context(nc.sbuf_tensor(n, s, t))
        keep["h2T"] = keep["acc"] = sb("h2T_then_sums", [P, DC, SEQ])
        with nc.sbuf_tensor("const", [P, C_WIDTH], F32) as const:
            keep["const"] = const
            with nc.sbuf_tensor("mod", [P, 6, D], F32) as mod, nc.sbuf_tensor("pool_col", [P, PG], F32) as pool_col:
                keep["mod"], keep["pool_col"] = mod, pool_col
                modulation(nc, d, keep)
                mixing(nc, d, keep)
            routing(nc, d, keep)
        keep["ident"] = sb("ident", [P, P])
        with nc.sbuf_tensor("h_hi", [P, DC, SEQ], F32R) as h_hi, nc.sbuf_tensor("h_lo", [P, DC, SEQ], F32R) as h_lo:
            keep["h_hi"], keep["h_lo"] = h_hi, h_lo
            load_ident(nc, d, keep)
            split_h2(nc, d, keep)
            experts(nc, d, keep)
        final(nc, d, keep)


def load_ident(nc, d, keep):
    with nc.semaphore("ident_in") as ident_in, nc.Block() as block:
        @block.sync
        def _(sp):
            sp.dma_start(keep["ident"][:, :], d["const"][:, C_IDENT:C_IDENT + P]).then_inc(ident_in, 16)
            sp.wait_ge(ident_in, 16)


_INS = ['x', 'c', 'w_ada', 'b_ada', 'w_in', 'attn_sinks', 'w_pool', 'pool_scale', 'w_out', 'ln1_g', 'ln1_b',
        'w_pq', 'peer_k1', 'peer_k2', 'peer_u', 'peer_v', 'ln2_g', 'ln2_b']


def shape_constants():
    import numpy as np
    k = np.zeros((P, C_WIDTH), np.float32)
    k[:, C_IDENT:C_IDENT + P] = np.eye(P)
    q, s = np.arange(P)[:, None], np.arange(2 * P)[None, :]
    rel = q + P - s
    band = (rel >= 0) & (rel < P)
    k[:, C_MASK:C_MASK + 2 * P] = np.where(band & (s >= P), 0.0, NEG)
    k[:, C_MASK + 2 * P:C_MASK + 4 * P] = np.where(band, 0.0, NEG)
    s, t = np.arange(P)[:, None], np.arange(P)[None, :]
    for g, w in enumerate(POOLS):
        own = (s <= t) & (t - s < w)
        prev = t + P - s < w
        first = np.where(own, 1.0 / np.minimum(t + 1, w), 0.0) - (s == t)
        for n, m in enumerate((first, own / w - (s == t), prev / w)):
            at = C_BAND + (3 * g + n) * P
            k[:, at:at + P] = m
    k[:, C_IOTA:C_IOTA + P] = np.arange(P)
    starts = np.array(ROW_START, np.float32)
    k[:, C_START:C_START + NTH] = starts[1:]
    k[:, C_DSTART:C_DSTART + NTH] = starts[1:] - starts[:-1]
    freqs = np.float32(10000.0) ** (-np.arange(HALF, dtype=np.float32) / np.float32(HALF))
    ang = np.arange(SEQ, dtype=np.float32)[:, None] * freqs[None, :]
    for at, f in ((C_COS, np.cos), (C_SIN, np.sin)):
        tab = f(ang).astype(np.float32).reshape(TILES, P, HALF).transpose(1, 0, 2)
        k[:, at:at + TILES * HALF] = tab.reshape(P, TILES * HALF)
    return k


def kernel(**inputs):
    import numpy as _np
    import concourse.bacc as _bacc
    from concourse import mybir as _mybir
    from concourse.bass_utils import run_bass_kernel_spmd as _run

    nc = _bacc.Bacc("TRN2", target_bir_lowering=False, num_devices=1)
    arrays, d = {}, {}
    for name in _INS:
        a = _np.ascontiguousarray(inputs[name])
        arrays[f"in_{name}_dram"] = a
        d[name] = nc.dram_tensor(f"in_{name}_dram", a.shape, _mybir.dt.from_np(a.dtype), kind="ExternalInput").ap()
    arrays["const_dram"] = shape_constants()
    d["const"] = nc.dram_tensor("const_dram", arrays["const_dram"].shape, F32, kind="ExternalInput").ap()
    d["out"] = nc.dram_tensor("out_0_dram", (1, SEQ, D), F32, kind="ExternalOutput").ap()
    build(nc, d)
    r = _run(nc, [arrays], core_ids=[0])
    return r.results[0]["out_0_dram"]
```

```python
from contextlib import ExitStack

import concourse.bass as bass
from concourse import mybir

ALU = mybir.AluOpType
ACT = mybir.ActivationFunctionType
AX = mybir.AxisListType
F32 = mybir.dt.float32
F32R = mybir.dt.float32r
BF16 = mybir.dt.bfloat16
U32 = mybir.dt.uint32

P = 128
D = 1024
DC = D // P
SEQ = 1024
TILES = SEQ // P
HD = 64
HALF = HD // 2
HEADS, KV_HEADS = 8, 2
QW, KVW = HEADS * HD, KV_HEADS * HD
POOLS = (2, 4, 8, 16)
PG = len(POOLS)
PW = D - QW
PEER_HEADS, KEYS, TOPK = 8, 128, 16
NQ = 2 * PEER_HEADS
EXPERTS = KEYS * KEYS
ALPHA = 2.0 ** 0.25
EPS = 1e-5
NEG = -1e30
LOWEST = -3.0e38
NB = 512

RECTS = ((0, 2, 16), (2, 8, 5), (8, 16, 1))
CAND = sum((a1 - a0) * w for a0, a1, w in RECTS)
ROW_START = [sum((min(a, a1) - a0) * w for a0, a1, w in RECTS if a > a0) for a in range(TOPK)]
NTH = TOPK - 1

HALF_T = 64
PIECES = SEQ // HALF_T

C_IDENT = 0
C_MASK = C_IDENT + P
C_BAND = C_MASK + 4 * P
C_IOTA = C_BAND + PG * 3 * P
C_START = C_IOTA + P
C_DSTART = C_START + NTH
C_COS = C_DSTART + NTH
C_SIN = C_COS + TILES * HALF
C_WIDTH = C_SIN + TILES * HALF


class Chain:

    def __init__(self, eng, sem):
        self.eng, self.sem, self.n = eng, sem, 0

    def step(self, ins):
        ins.then_inc(self.sem, 1)
        self.n += 1

    def wait(self):
        self.eng.wait_ge(self.sem, self.n)

    def link(self, ins):
        self.step(ins)
        self.wait()

    def clear(self):
        self.wait()
        self.eng.sem_clear(self.sem)
        self.n = 0


def modulation(nc, d, keep):
    CH = 6 * D // NB
    RING = 4
    with ExitStack() as ctx:
        sb = lambda n, s, t=F32: ctx.enter_context(nc.sbuf_tensor(n, s, t))
        sem = lambda n: ctx.enter_context(nc.semaphore(n))
        c_col = sb("c_col", [P, DC])
        c_act = sb("c_act", [P, DC])
        c_rep = sb("c_rep", [P, DC, P])
        ones = sb("ones", [1, P])
        bias = sb("bias", [1, 6 * D])
        wada = sb("wada", [P, RING, DC, NB])
        pool_row = sb("pool_row", [PG, P])
        ps = [ctx.enter_context(nc.psum_tensor(f"ps_mod{i}", [P, NB], F32)) for i in range(2)]
        ps_turn = ctx.enter_context(nc.psum_tensor("ps_turn", [P, PG], F32))
        c_in, const_in, bias_in, silu_done = sem("c_in"), sem("const_in"), sem("bias_in"), sem("silu_done")
        ones_set, rep_ready = sem("ones_set"), sem("rep_ready")
        w_in = [sem(f"wada_in{i}") for i in range(RING)]
        mod_sum, mod_out = sem("mod_sum"), sem("mod_out")
        gate2_out, turned = sem("gate2_out"), sem("pool_turned")
        pool_ready, rows_in = sem("pool_ready"), sem("ada_rows_in")
        block = ctx.enter_context(nc.Block())
        w_view = d["w_ada"].rearrange("a (p j) n -> (a p) j n", j=DC)

        @block.sync
        def _(sp):
            sp.dma_start(c_col[:, :], d["c"].rearrange("a (p j) -> (a p) j", j=DC)).then_inc(c_in, 16)
            sp.dma_start(bias[:, :], d["b_ada"]).then_inc(bias_in, 16)
            for n in range(CH):
                if n >= RING:
                    sp.wait_ge(mod_sum, n - RING + 1)
                sp.dma_start(wada[:, n % RING, :, :],
                             w_view[:, :, n * NB:(n + 1) * NB]).then_inc(w_in[n % RING], 16)
            sp.wait_ge(mod_out, CH)
            sp.dma_start(d["gate2_keep"], keep["mod"][:, 5, :]).then_inc(gate2_out, 16)
            sp.wait_ge(gate2_out, 16)

        @block.gpsimd
        def _(pool):
            nc.gpsimd.memset(ones[:, :], 1.0).then_inc(ones_set, 1)

        @block.scalar
        def _(act):
            act.dma_start(keep["const"][:, :], d["const"]).then_inc(const_in, 16)
            act.dma_start(pool_row[:, :], d["pool_scale"].rearrange("a (g p) -> (a g) p", p=P)).then_inc(rows_in, 16)
            act.wait_ge(c_in, 16)
            nc.scalar.activation(c_act[:, :], c_col[:, :], ACT.Silu).then_inc(silu_done, 1)

        @block.tensor
        def _(pe):
            pe.wait_ge(const_in, 16)
            pe.wait_ge(rows_in, 16)
            nc.tensor.transpose(ps_turn[:, 0:PG], pool_row[:, :], keep["const"][0:PG, 0:PG]).then_inc(turned, 1)
            pe.wait_ge(rep_ready, 1)
            pe.wait_ge(ones_set, 1)
            pe.wait_ge(bias_in, 16)
            for n in range(CH):
                pe.wait_ge(w_in[n % RING], 16 * (n // RING + 1))
                if n >= 2:
                    pe.wait_ge(mod_out, n - 1)
                for j in range(DC):
                    nc.tensor.matmul(ps[n % 2][:, :], c_rep[:, j, :], wada[:, n % RING, j, :], start=(j == 0), stop=False)
                nc.tensor.matmul(ps[n % 2][:, :], ones[:, :], bias[:, n * NB:(n + 1) * NB],
                                 start=False, stop=True).then_inc(mod_sum, 1)

        @block.vector
        def _(dve):
            dve.wait_ge(silu_done, 1)
            for j in range(DC):
                last = nc.vector.tensor_copy(c_rep[:, j, :], c_act[:, j:j + 1].to_broadcast([P, P]))
            last.then_inc(rep_ready, 1)
            dve.wait_ge(turned, 1)
            nc.vector.tensor_copy(keep["pool_col"][:, :], ps_turn[:, :]).then_inc(pool_ready, 1)
            for n in range(CH):
                dve.wait_ge(mod_sum, n + 1)
                kind = n * NB // D
                one = 0.0 if kind in (0, 3) else 1.0
                at = (n * NB) % D
                nc.vector.tensor_scalar_add(keep["mod"][:, kind, at:at + NB], ps[n % 2][:, :], one).then_inc(mod_out, 1)


def mixing(nc, d, keep):
    with ExitStack() as ctx:
        sb = lambda n, s, t=F32: ctx.enter_context(nc.sbuf_tensor(n, s, t))
        sem = lambda n: ctx.enter_context(nc.semaphore(n))
        ps = lambda n, w: ctx.enter_context(nc.psum_tensor(n, [P, w], F32))
        const, mod, h2T = keep["const"], keep["mod"], keep["h2T"]
        ident = const[:, C_IDENT:C_IDENT + P]
        w_in = sb("w_in", [P, DC, QW + 2 * KVW + PW])
        w_out = sb("w_out", [P, DC, D])
        w_pool = sb("w_pool", [P, PG, P])
        ln_g, ln_b = sb("ln1_gain", [P, D]), sb("ln1_bias", [P, D])
        sink = sb("sink", [P, HEADS])
        xt = sb("x_tile", [P, D])
        h = sb("h_tile", [P, D])
        hT = sb("hT", [P, DC, P])
        rot_a, rot_b = sb("rot_a", [P, 10 * HD]), sb("rot_b", [P, 10 * HD])
        qk = sb("qk", [P, 10 * HD])
        qT = sb("qT", [P, 4, P])
        kT = sb("kT", [P, 2, P])
        v = sb("v", [P, 2, KVW])
        pin = sb("pool_in", [P, 2, PW])
        s = sb("scores", [P, 4, 2 * P])
        pT = sb("probsT", [P, 8, P])
        small = sb("small", [P, 5, HEADS])
        pooledT = rot_a
        mixT = sb("mixT", [P, DC, P])
        y = h
        stats, mv, rstd = sb("stats", [P, 2, 6]), sb("mean_var", [P, 2]), sb("rstd", [P, 2])
        power = sb("power", [P, 1])
        h2 = sb("h2", [P, D])
        ps_t, ps_p, ps_s, ps_o = ps("ps_t", 2 * NB), ps("ps_p", 3 * NB), ps("ps_s", 2 * NB), ps("ps_o", NB)

        w_ready, x_in, x1_out = sem("mix_weights_in"), sem("x_in"), sem("x1_out")
        zeroed = sem("zeroed")
        h_ready, h_turned, hT_ready, proj_done = sem("h_ready"), sem("h_turned"), sem("hT_ready"), sem("proj_done")
        rope_done, qk_turned, qkT_ready, vp_ready = sem("rope_done"), sem("qk_turned"), sem("qkT_ready"), sem("vp_ready")
        scores_done, s_ready, negm_ready, exp_done = sem("scores_done"), sem("s_ready"), sem("negm_ready"), sem("exp_done")
        rden_ready, probs_ready, pT_done, pT_ready = sem("rden_ready"), sem("probs_ready"), sem("pT_done"), sem("pT_ready")
        pv_done, mixa_ready, pooled_done, pooledT_ready = sem("pv_done"), sem("mixa_ready"), sem("pooled_done"), sem("pooledT_ready")
        y_done, mixb_ready, out_done, res_done = sem("y_done"), sem("mixb_ready"), sem("out_done"), sem("res_done")
        var_ready, rstd_ready, x1_ready, h2_ready = sem("var_ready"), sem("rstd_ready"), sem("x1_ready"), sem("h2_ready")
        h2_turned, h2T_ready = sem("h2_turned"), sem("h2T_ready")
        dve_chain, act_chain, pool_chain = sem("dve_chain1"), sem("act_chain1"), sem("pool_chain1")
        block = ctx.enter_context(nc.Block())
        x_view = d["x"].rearrange("a (t p) n -> (a t) p n", p=P)

        def over_tiles(eng, body):
            body(0, True)
            with eng.Fori(1, TILES) as i:
                body(i, False)

        @block.sync
        def _(sp):
            sp.dma_start(w_in[:, :, :], d["w_in"].rearrange("a (j p) n -> (a p) j n", p=P)).then_inc(w_ready, 16)
            sp.dma_start(w_pool[:, :, :], d["w_pool"].rearrange("a g p n -> (a p) g n")).then_inc(w_ready, 16)
            sp.dma_start(w_out[:, :, :], d["w_out"].rearrange("a (j p) n -> (a p) j n", p=P)).then_inc(w_ready, 16)

            def body(i, first):
                if not first:
                    sp.wait_ge(res_done, i)
                sp.dma_start(xt[:, :], x_view[i]).then_inc(x_in, 16)
                sp.wait_ge(h2_ready, i + 1)
                sp.dma_start(d["x1_keep"][i], s_x1).then_inc(x1_out, 16)
            s_x1 = y[:, :]
            over_tiles(sp, body)
            sp.wait_ge(x1_out, 16 * TILES)

        @block.gpsimd
        def _(pool):
            nc.gpsimd.memset(kT[:, 0, :], 0.0).then_inc(zeroed, 1)
            nc.gpsimd.memset(v[:, 0, :], 0.0).then_inc(zeroed, 1)
            nc.gpsimd.memset(pin[:, 0, :], 0.0).then_inc(zeroed, 1)
            nc.gpsimd.memset(power[:, :], -0.5).then_inc(zeroed, 1)
            pool.wait_ge(zeroed, 4)
            chain = Chain(pool, pool_chain)

            def body(i, first):
                pool.wait_ge(var_ready, i + 1)
                pool.wait_ge(zeroed, 4)
                nc.gpsimd.tensor_tensor(rstd[:, 0:1], rstd[:, 1:2], power[:, :], ALU.pow).then_inc(rstd_ready, 1)
                pool.wait_ge(x1_ready, i + 1)
                if not first:
                    pool.wait_ge(h2_turned, i)
                pool.wait_ge(zeroed, 4)
                chain.link(nc.gpsimd.tensor_tensor(h2[:, :], y[:, :], mod[:, 4, :], ALU.mult))
                nc.gpsimd.tensor_tensor(h2[:, :], h2[:, :], mod[:, 3, :], ALU.add).then_inc(h2_ready, 1)
                chain.clear()
            over_tiles(pool, body)

        @block.scalar
        def _(act):
            for dst, name in ((ln_g, "ln1_g"), (ln_b, "ln1_b")):
                act.dma_start(dst[:, :], d[name].to_broadcast([P, D])).then_inc(w_ready, 16)
            act.dma_start(sink[:, :], d["attn_sinks"].to_broadcast([P, HEADS])).then_inc(w_ready, 16)
            chain = Chain(act, act_chain)

            def body(i, first):
                act.wait_ge(h_turned, i + 1)
                nc.scalar.activation(hT[:, :, :], ps_t[:, :].rearrange("p (j t) -> p j t", t=P), ACT.Copy).then_inc(hT_ready, 1)
                if not first:
                    act.wait_ge(out_done, i)
                    nc.scalar.activation(kT[:, 0, :], kT[:, 1, :], ACT.Copy)
                    nc.scalar.activation(v[:, 0, :], v[:, 1, :], ACT.Copy)
                    chain.link(nc.scalar.activation(pin[:, 0, :], pin[:, 1, :], ACT.Copy))
                    chain.clear()
                act.wait_ge(proj_done, i + 1)
                nc.scalar.activation(pin[:, 1, :], ps_p[:, 2 * NB:3 * NB], ACT.Copy)
                act.wait_ge(rope_done, i + 1)
                nc.scalar.activation(v[:, 1, :], ps_p[:, QW + KVW:QW + 2 * KVW], ACT.Copy).then_inc(vp_ready, 1)
                act.wait_ge(qk_turned, i + 1)
                nc.scalar.activation(qT[:, :, :], ps_t[:, 0:4 * P].rearrange("p (j t) -> p j t", t=P), ACT.Copy)
                nc.scalar.activation(kT[:, 1, :], ps_t[:, 4 * P:5 * P], ACT.Copy).then_inc(qkT_ready, 1)
                for r in range(2):
                    act.wait_ge(negm_ready, 2 * i + r + 1)
                    for n in range(4):
                        hd = 4 * r + n
                        nc.scalar.activation(s[:, n, :], s[:, n, :], ACT.Exp, bias=small[:, 1, hd:hd + 1],
                                             accum_out=small[:, 2, hd:hd + 1])
                    last = nc.scalar.activation(small[:, 3, 4 * r:4 * r + 4], small[:, 3, 4 * r:4 * r + 4], ACT.Exp)
                    last.then_inc(exp_done, 1)
                    act.wait_ge(exp_done, 2 * i + r + 1)
                    act.wait_ge(rden_ready, 2 * i + r + 1)
                    for n in range(4):
                        hd = 4 * r + n
                        last = nc.scalar.activation(s[:, n, :], s[:, n, :], ACT.Copy, scale=small[:, 4, hd:hd + 1])
                    last.then_inc(probs_ready, 1)
                    act.wait_ge(pT_done, 2 * i + r + 1)
                    if r or not first:
                        act.wait_ge(pv_done, 2 * i + r)
                    nc.scalar.activation(pT[:, :, :], ps_t[:, :].rearrange("p (j t) -> p j t", t=P), ACT.Copy).then_inc(pT_ready, 1)
                act.wait_ge(pv_done, 2 * i + 2)
                nc.scalar.activation(mixT[:, 0:4, :], ps_o[:, :].rearrange("p (j t) -> p j t", t=P), ACT.Copy).then_inc(mixa_ready, 1)
                act.wait_ge(h2_turned, i + 1)
                nc.scalar.activation(h2T[:, :, bass.ds(i * P, P)], ps_t[:, :].rearrange("p (j t) -> p j t", t=P), ACT.Copy).then_inc(h2T_ready, 1)
            over_tiles(act, body)

        @block.tensor
        def _(pe):
            pe.wait_ge(zeroed, 4)

            def body(i, first):
                pe.wait_ge(h_ready, i + 1)
                if not first:
                    pe.wait_ge(h2T_ready, i)
                for j in range(DC):
                    last = nc.tensor.transpose(ps_t[:, j * P:(j + 1) * P], h[:, j * P:(j + 1) * P], ident)
                last.then_inc(h_turned, 1)
                if first:
                    pe.wait_ge(w_ready, 16 * 6)
                pe.wait_ge(hT_ready, i + 1)
                if not first:
                    pe.wait_ge(mixb_ready, i)
                for at, src, width in ((0, 0, QW), (QW, QW, 2 * KVW), (2 * NB, QW + 2 * KVW, PW)):
                    for j in range(DC):
                        last = nc.tensor.matmul(ps_p[:, at:at + width], hT[:, j, :], w_in[:, j, src:src + width],
                                                start=(j == 0), stop=(j == DC - 1))
                last.then_inc(proj_done, 1)
                pe.wait_ge(rope_done, i + 1)
                for j in range(4):
                    nc.tensor.transpose(ps_t[:, j * P:(j + 1) * P], qk[:, j * P:(j + 1) * P], ident)
                nc.tensor.transpose(ps_t[:, 4 * P:5 * P], qk[:, QW:QW + KVW], ident).then_inc(qk_turned, 1)
                pe.wait_ge(qkT_ready, i + 1)
                if not first:
                    pe.wait_ge(res_done, i)

                def score_round(r):
                    for n in range(4):
                        last = nc.tensor.matmul(ps_s[:, n * 2 * P:(n + 1) * 2 * P], qT[HD * r:HD * r + HD, n, :],
                                                kT[HD * r:HD * r + HD, :, :], start=True, stop=True)
                    last.then_inc(scores_done, 1)

                score_round(0)
                pe.wait_ge(vp_ready, i + 1)
                for g in range(PG):
                    own = C_BAND + (3 * g + (0 if first else 1)) * P
                    prev = C_BAND + (3 * g + 2) * P
                    out = ps_p[:, g * P:(g + 1) * P]
                    nc.tensor.matmul(out, pin[:, 1, g * P:(g + 1) * P], const[:, own:own + P], start=True, stop=False)
                    last = nc.tensor.matmul(out, pin[:, 0, g * P:(g + 1) * P], const[:, prev:prev + P], start=False, stop=True)
                last.then_inc(pooled_done, 1)
                pe.wait_ge(s_ready, 2 * i + 1)
                score_round(1)
                pe.wait_ge(pooledT_ready, i + 1)
                for g in range(PG):
                    last = nc.tensor.matmul(ps_p[:, NB + g * P:NB + (g + 1) * P], w_pool[:, g, :],
                                            pooledT[:, g * P:(g + 1) * P], start=True, stop=True)
                last.then_inc(y_done, 1)
                for r in range(2):
                    pe.wait_ge(probs_ready, 2 * i + r + 1)
                    if r:
                        pe.wait_ge(pT_ready, 2 * i + 1)
                    for n in range(8):
                        last = nc.tensor.transpose(ps_t[:, n * P:(n + 1) * P], s[:, n // 2, (n % 2) * P:(n % 2 + 1) * P], ident)
                    last.then_inc(pT_done, 1)
                    pe.wait_ge(pT_ready, 2 * i + r + 1)
                    if r == 0 and not first:
                        pe.wait_ge(mixa_ready, i)
                    for n in range(4):
                        hd = 4 * r + n
                        at = HD * (hd % 2)
                        out = ps_o[at:at + HD, (hd // 2) * P:(hd // 2 + 1) * P]
                        for k in range(2):
                            last = nc.tensor.matmul(out, v[:, k, r * HD:(r + 1) * HD], pT[:, 2 * n + k, :],
                                                    start=(k == 0), stop=(k == 1))
                    last.then_inc(pv_done, 1)
                pe.wait_ge(mixa_ready, i + 1)
                pe.wait_ge(mixb_ready, i + 1)
                for half in range(2):
                    for j in range(DC):
                        last = nc.tensor.matmul(ps_s[:, half * NB:(half + 1) * NB], mixT[:, j, :],
                                                w_out[:, j, half * NB:(half + 1) * NB], start=(j == 0), stop=(j == DC - 1))
                last.then_inc(out_done, 1)
                pe.wait_ge(h2_ready, i + 1)
                for j in range(DC):
                    last = nc.tensor.transpose(ps_t[:, j * P:(j + 1) * P], h2[:, j * P:(j + 1) * P], ident)
                last.then_inc(h2_turned, 1)
            over_tiles(pe, body)

        @block.vector
        def _(dve):
            chain = Chain(dve, dve_chain)
            V = nc.vector
            dve.wait_ge(w_ready, 16 * 6)

            def body(i, first):
                dve.wait_ge(x_in, 16 * i + 16)
                if not first:
                    dve.wait_ge(x1_out, 16 * i)
                chain.link(V.tensor_tensor(h[:, :], xt[:, :], mod[:, 1, :], ALU.mult))
                V.tensor_tensor(h[:, :], h[:, :], mod[:, 0, :], ALU.add).then_inc(h_ready, 1)
                dve.wait_ge(proj_done, i + 1)
                src = ps_p[:, 0:10 * HD].rearrange("p (n a c) -> p n a c", a=2, c=HALF)
                cos = const[:, bass.ds(i * HALF + C_COS, HALF)]
                sin = const[:, bass.ds(i * HALF + C_SIN, HALF)]
                ra = rot_a[:, :].rearrange("p (n a c) -> p n a c", a=2, c=HALF)
                rb = rot_b[:, :].rearrange("p (n a c) -> p n a c", a=2, c=HALF)
                qk4 = qk[:, :].rearrange("p (n a c) -> p n a c", a=2, c=HALF)
                for a in range(2):
                    V.tensor_tensor(ra[:, :, a, :], src[:, :, a, :], cos.unsqueeze(1).to_broadcast([P, 10, HALF]), ALU.mult)
                    last = V.tensor_tensor(rb[:, :, a, :], src[:, :, 1 - a, :], sin.unsqueeze(1).to_broadcast([P, 10, HALF]), ALU.mult)
                chain.link(last)
                for a, op in ((0, ALU.subtract), (1, ALU.add)):
                    by_pair = lambda t: t[:, 0:HEADS, a, :].rearrange("p (g j) c -> p g j c", g=2)
                    V.tensor_tensor(qk4[:, 0:HEADS, a, :].rearrange("p (j g) c -> p g j c", g=2), by_pair(ra), by_pair(rb), op)
                    last = V.tensor_tensor(qk4[:, HEADS:, a, :], ra[:, HEADS:, a, :], rb[:, HEADS:, a, :], op)
                last.then_inc(rope_done, 1)

                def scores_and_max(r):
                    hs = slice(4 * r, 4 * r + 4)
                    dve.wait_ge(scores_done, 2 * i + r + 1)
                    if r:
                        dve.wait_ge(pT_done, 2 * i + 1)
                    mask = const[:, C_MASK:C_MASK + 2 * P] if first else const[:, C_MASK + 2 * P:C_MASK + 4 * P]
                    V.scalar_tensor_tensor(s[:, :, :], ps_s[:, :].rearrange("p (n k) -> p n k", n=4), HD ** -0.5,
                                           mask.unsqueeze(1).to_broadcast([P, 4, 2 * P]), ALU.mult, ALU.add).then_inc(s_ready, 1)
                    dve.wait_ge(s_ready, 2 * i + r + 1)
                    chain.link(V.tensor_reduce(small[:, 0, hs], s[:, :, :], AX.X, ALU.max))
                    chain.link(V.tensor_tensor(small[:, 0, hs], small[:, 0, hs], sink[:, hs], ALU.max))
                    V.tensor_tensor(small[:, 3, hs], sink[:, hs], small[:, 0, hs], ALU.subtract)
                    V.tensor_scalar(small[:, 1, hs], small[:, 0, hs], -1.0, None, ALU.mult).then_inc(negm_ready, 1)

                def denominators(r):
                    hs = slice(4 * r, 4 * r + 4)
                    dve.wait_ge(exp_done, 2 * i + r + 1)
                    chain.link(V.tensor_tensor(small[:, 0, hs], small[:, 2, hs], small[:, 3, hs], ALU.add))
                    V.reciprocal(small[:, 4, hs], small[:, 0, hs]).then_inc(rden_ready, 1)

                scores_and_max(0)
                dve.wait_ge(pooled_done, i + 1)
                V.tensor_copy(pooledT[:, 0:PW], ps_p[:, 0:PW]).then_inc(pooledT_ready, 1)
                denominators(0)
                dve.wait_ge(y_done, i + 1)
                V.tensor_tensor(mixT[:, 4:8, :], ps_p[:, NB:2 * NB].rearrange("p (g t) -> p g t", g=PG),
                                keep["pool_col"][:, :].unsqueeze(2).to_broadcast([P, PG, P]), ALU.mult).then_inc(mixb_ready, 1)
                scores_and_max(1)
                denominators(1)
                dve.wait_ge(out_done, i + 1)
                chain.link(V.tensor_tensor(y[:, :], ps_s[:, :], mod[:, 2, :], ALU.mult))
                V.scalar_tensor_tensor(y[:, :], xt[:, :], ALPHA, y[:, :], ALU.mult, ALU.add).then_inc(res_done, 1)
                dve.wait_ge(res_done, i + 1)
                chain.wait()
                V.bn_stats(stats[:, 0, :], y[:, 0:NB])
                chain.link(V.bn_stats(stats[:, 1, :], y[:, NB:D]))
                chain.link(V.bn_aggr(mv[:, :], stats[:, :, :]))
                V.tensor_scalar_add(rstd[:, 1:2], mv[:, 1:2], EPS).then_inc(var_ready, 1)
                chain.link(V.scalar_tensor_tensor(y[:, :], y[:, :], mv[:, 0:1], ln_g[:, :], ALU.subtract, ALU.mult))
                dve.wait_ge(rstd_ready, i + 1)
                V.scalar_tensor_tensor(y[:, :], y[:, :], rstd[:, 0:1], ln_b[:, :], ALU.mult, ALU.add).then_inc(x1_ready, 1)
                chain.clear()
            over_tiles(dve, body)


def in_pairs(eng, count, body):
    body(0, 0)
    body(1, 1)
    with eng.Fori(1, count // 2 - 1) as m:
        body(2 * m, 0)
        body(2 * m + 1, 1)
    body(count - 2, 0)
    body(count - 1, 1)


def at_least(n, k):
    return not isinstance(n, int) or n >= k


def one(view, n):
    if isinstance(n, int):
        return view[:, n]
    return view[:, bass.ds(n, 1)].rearrange("p m j n -> p (m j) n")


def queries(nc, d, keep):
    with ExitStack() as ctx:
        sb = lambda n, s, t=F32: ctx.enter_context(nc.sbuf_tensor(n, s, t))
        sem = lambda n: ctx.enter_context(nc.semaphore(n))
        ps = lambda n, w: ctx.enter_context(nc.psum_tensor(n, [P, w], F32))
        const, h2T, h_part = keep["const"], keep["h2T"], (keep["h_hi"], keep["h_lo"])
        ident = const[:, C_IDENT:C_IDENT + P]
        k_rows, keysT = sb("key_rows", [P, 2, P]), sb("keysT", [P, 2, P])
        w_raw = sb("wq_raw", [P, 2, DC, P])
        w_part = (sb("wq_hi", [P, 2, DC, P], F32R), sb("wq_lo", [P, 2, DC, P], F32R))
        qT = sb("queriesT", [P, 2, SEQ])
        score = sb("score_rows", [P, 2, TILES, P])
        ps_q = [ps(f"ps_q{e}", 2 * NB) for e in range(2)]
        ps_s = [ps(f"ps_s{e}", 2 * NB) for e in range(2)]
        keys_in, keys_turned, keysT_ready = sem("keys_in"), sem("keys_turned"), sem("keysT_ready")
        hi_ready, lo_ready = sem("h2_hi_ready"), sem("h2_lo_ready")
        w_in = [sem(f"wq_in{e}") for e in range(2)]
        whi_ready, wlo_ready = sem("wq_hi_ready"), sem("wq_lo_ready")
        q_done, qT_ready, s_done, s_ready = sem("q_done"), sem("qT_ready"), sem("s_done"), sem("s_rows_ready")
        stored = [sem(f"scores_stored{e}") for e in range(2)]
        block = ctx.enter_context(nc.Block())
        w_view = d["w_pq"].rearrange("a (j p) (m n) -> (a p) m j n", p=P, n=P)
        s_view = d["scores_keep"].rearrange("t p (m k) -> p m t k", k=KEYS)

        @block.sync
        def _(sp):
            sp.dma_start(k_rows[:, 0, :], d["peer_k1"].rearrange("a k c -> (a k) c")).then_inc(keys_in, 16)
            sp.dma_start(k_rows[:, 1, :], d["peer_k2"].rearrange("a k c -> (a k) c")).then_inc(keys_in, 16)

            def body(n, e):
                if at_least(n, 2):
                    sp.wait_ge(wlo_ready, n - 1)
                sp.dma_start(w_raw[:, e, :, :], one(w_view, n)).then_inc(w_in[e], 16)
            in_pairs(sp, NQ, body)

        @block.gpsimd
        def _(pool):
            def body(n, e):
                pool.wait_ge(s_ready, n + 1)
                pool.wait_ge(keys_in, 32)
                pool.dma_start(one(s_view, n), score[:, e, :, :]).then_inc(stored[e], 16)
            in_pairs(pool, NQ, body)
            for e in range(2):
                pool.wait_ge(stored[e], 16 * PEER_HEADS)

        @block.scalar
        def _(act):
            def w_hi(n, e):
                act.wait_ge(w_in[e], 8 * (n - e) + 16)
                if at_least(n, 2):
                    act.wait_ge(q_done, n - 1)
                nc.scalar.activation(w_part[0][:, e, :, :], w_raw[:, e, :, :], ACT.Copy).then_inc(whi_ready, 1)

            def body(n, e):
                if not isinstance(n, int) or n < NQ - 1:
                    w_hi(n + 1, 1 - e)
                act.wait_ge(q_done, n + 1)
                if at_least(n, 2):
                    act.wait_ge(s_done, n - 1)
                nc.scalar.activation(qT[:, e, :], ps_q[e][:, :], ACT.Copy).then_inc(qT_ready, 1)

            act.wait_ge(keys_turned, 1)
            nc.scalar.activation(keysT[:, :, :], ps_s[0][:, 0:2 * P].rearrange("p (a k) -> p a k", a=2), ACT.Copy).then_inc(keysT_ready, 1)
            w_hi(0, 0)
            for j in range(DC):
                nc.scalar.activation(h_part[0][:, j, :], h2T[:, j, :], ACT.Copy).then_inc(hi_ready, 1)
            in_pairs(act, NQ, body)

        @block.tensor
        def _(pe):
            pe.wait_ge(keys_in, 32)
            for a in range(2):
                last = nc.tensor.transpose(ps_s[0][:, a * P:(a + 1) * P], k_rows[:, a, :], ident)
            last.then_inc(keys_turned, 1)
            pe.wait_ge(keysT_ready, 1)

            def key_scores(n, e):
                pe.wait_ge(qT_ready, n + 1)
                if at_least(n, 2):
                    pe.wait_ge(s_ready, n - 1)
                for t in range(TILES):
                    last = nc.tensor.matmul(ps_s[e][:, t * P:(t + 1) * P], qT[:, e, t * P:(t + 1) * P], keysT[:, e, :], start=True, stop=True)
                last.then_inc(s_done, 1)

            def body(n, e):
                fresh = isinstance(n, int) and n == 0
                pe.wait_ge(whi_ready, n + 1)
                if not fresh:
                    pe.wait_ge(wlo_ready, n + 1)
                if at_least(n, 2):
                    pe.wait_ge(qT_ready, n - 1)
                for half in range(2):
                    k = 0
                    for a, b in ((0, 0), (1, 0), (0, 1)):
                        if fresh and half == 0 and a == 1:
                            pe.wait_ge(wlo_ready, 1)
                        for j in range(DC):
                            if fresh and half == 0 and (a, b) != (1, 0):
                                pe.wait_ge(hi_ready if b == 0 else lo_ready, j + 1)
                            last = nc.tensor.matmul(ps_q[e][:, half * NB:(half + 1) * NB], w_part[a][:, e, j, :],
                                                    h_part[b][:, j, half * NB:(half + 1) * NB], start=(k == 0), stop=(k == 3 * DC - 1))
                            k += 1
                last.then_inc(q_done, 1)
                if not fresh:
                    key_scores(n - 1, 1 - e)
            in_pairs(pe, NQ, body)
            key_scores(NQ - 1, 1)

        @block.vector
        def _(dve):
            V = nc.vector

            def w_lo(n, e):
                dve.wait_ge(whi_ready, n + 1)
                if at_least(n, 2):
                    dve.wait_ge(q_done, n - 1)
                V.tensor_tensor(w_part[1][:, e, :, :], w_raw[:, e, :, :], w_part[0][:, e, :, :].bitcast(F32), ALU.subtract).then_inc(wlo_ready, 1)

            def rows_out(n, e):
                dve.wait_ge(s_done, n + 1)
                if at_least(n, 2):
                    dve.wait_ge(stored[e], 8 * (n - e))
                V.tensor_copy(score[:, e, :, :], ps_s[e][:, :].rearrange("p (t k) -> p t k", k=P)).then_inc(s_ready, 1)

            def body(n, e):
                if not isinstance(n, int) or n < NQ - 1:
                    w_lo(n + 1, 1 - e)
                rows_out(n, e)

            w_lo(0, 0)
            for j in range(DC):
                dve.wait_ge(hi_ready, j + 1)
                V.tensor_tensor(h_part[1][:, j, :], h2T[:, j, :], h_part[0][:, j, :].bitcast(F32), ALU.subtract).then_inc(lo_ready, 1)
            in_pairs(dve, NQ, body)


def routing(nc, d, keep):
    UNIT = 4
    UNITS = P // UNIT
    HEAD_STEPS = KEYS // (2 * TILES)
    TILE_STEPS = KEYS // TILES
    with ExitStack() as ctx:
        sb = lambda n, s, t=F32: ctx.enter_context(nc.sbuf_tensor(n, s, t))
        sem = lambda n: ctx.enter_context(nc.semaphore(n))
        ps = lambda n, w: ctx.enter_context(nc.psum_tensor(n, [P, w], F32))
        const, h_part = keep["const"], (keep["h_hi"], keep["h_lo"])
        ident = const[:, C_IDENT:C_IDENT + P]
        iota = const[:, C_IOTA:C_IOTA + P]
        sc = sb("score_tile", [P, NQ, P])
        gates = [keep["h2T"][:, :, :].rearrange("p j n -> p (j n)").rearrange("p (k t) -> p k t", t=HALF_T),
                 sb("gates1", [P, KEYS, HALF_T])[:, :, :]]
        vals = sb("vals", [P, NQ, TOPK])
        idx_u = sb("idx_u", [P, NQ, TOPK], U32)
        idx = sb("idx", [P, NQ, TOPK], BF16)
        rest = sb("rest", [P, NQ, P])
        wide = sb("wide", [P, PEER_HEADS * TOPK * TOPK], BF16)
        cand = wide[:, 0:2 * PEER_HEADS * CAND].bitcast(F32).rearrange("p (h n) -> p h n", h=PEER_HEADS)
        cand_rest = rest[:, 0:PEER_HEADS, 0:CAND]
        top = sb("top", [P, PEER_HEADS, TOPK])
        pos_u = sb("pos_u", [P, PEER_HEADS, TOPK], U32)
        pos = sb("pos", [P, PEER_HEADS, TOPK], BF16)
        col = sb("col", [P, PEER_HEADS, TOPK], BF16)
        starts = sb("starts", [P, 2 * NTH + TOPK], BF16)
        step1 = sb("step1", [P, PEER_HEADS, NTH], BF16)
        past = wide[:, :].rearrange("p (h k r) -> p h k r", h=PEER_HEADS, k=TOPK)
        prod = rest[:, PEER_HEADS:NQ, :].rearrange("p n k -> p (n k)").bitcast(BF16).rearrange(
            "p (h k r) -> p h k r", h=PEER_HEADS, k=TOPK)
        red = sb("red", [P, PEER_HEADS, TOPK])
        route = sb("route", [P, 3, P])
        stand = sb("stand", [P, 1])
        gsum = sb("gsum", [P, 2, PEER_HEADS])
        routeT = sb("routeT", [P, 3, P])
        hot1, hot2 = sb("hot1", [P, 2, UNIT, P]), sb("hot2", [P, 2, UNIT, P])
        u_raw = sb("u_raw", [P, 2, D])
        uT = (sb("uT_hi", [P, 2, DC, P], F32R), sb("uT_lo", [P, 2, DC, P], F32R))
        hid = sb("hid", [P, 2, SEQ])
        ps_u, ps_g = ps("ps_u", 2 * NB), ps("ps_gate", 2 * NB)
        ps_h = [ps(f"ps_h{e}", 2 * NB) for e in range(2)]

        scores_in, s_used = sem("scores_in"), sem("s_used")
        top_done, exp_done, route_ready, route_turned, routeT_ready = (
            sem("top_done"), sem("gate_exp_done"), sem("route_ready"), sem("route_turned"), sem("routeT_ready"))
        hot_ready, gate_done, gate_out = sem("hot_ready"), sem("gate_done"), sem("gate_out")
        stored = [sem("gates_stored0"), sem("gates_stored1")]
        starts_ready = sem("starts_ready")
        u_in = [sem(f"u_in{b}") for b in range(2)]
        u_turned, uhi_ready, ulo_ready = sem("u_turned"), sem("uhi_ready"), sem("ulo_ready")
        hid_done, gelu_done = sem("hid_done"), sem("gelu_done")
        hid_stored = [sem(f"hid_stored{b}") for b in range(2)]
        dve_chain = sem("dve_chain2")
        block = ctx.enter_context(nc.Block())
        u_view = d["peer_u"].rearrange("a (k1 k2) n -> (a k1) k2 n", k2=KEYS)
        hid_view = d["hid_keep"].rearrange("k2 p t -> p k2 t")

        def over_rounds(eng, pair, end=None):
            for c in range(HEAD_STEPS // 2):
                pair(0, c, 2 * c, None, 0, 0)
            if end:
                end(0)

            def middle(i):
                for c in range(TILE_STEPS // 2):
                    pair(i, c, HEAD_STEPS + TILE_STEPS * (i - 1) + 2 * c, i - 1, UNITS // TILE_STEPS, 2 * c * (UNITS // TILE_STEPS))
                if end:
                    end(i)
            middle(1)
            with eng.Fori(2, TILES) as i:
                middle(i)
            for c in range(HEAD_STEPS // 2):
                pair(TILES, c, KEYS - HEAD_STEPS + 2 * c, TILES - 1, UNITS // HEAD_STEPS, 2 * c * (UNITS // HEAD_STEPS))

        def has_next(step):
            return not isinstance(step, int) or step + 2 < KEYS

        @block.sync
        def _(sp):
            for e in range(2):
                sp.dma_start(u_raw[:, e, :], one2(u_view, e)).then_inc(u_in[e], 16)

            def pair(i, c, step0, tile, units, unit0):
                for e in range(2):
                    step = step0 + e
                    if has_next(step):
                        sp.wait_ge(u_turned, step + 1)
                        sp.dma_start(u_raw[:, e, :], one2(u_view, step + 2)).then_inc(u_in[e], 16)
                    sp.wait_ge(gelu_done, step + 1)
                    sp.dma_start(one2(hid_view, step), hid[:, e, :]).then_inc(hid_stored[e], 16)
            over_rounds(sp, pair)
            for e in range(2):
                sp.wait_ge(hid_stored[e], 16 * KEYS // 2)

        @block.gpsimd
        def _(pool):
            pool.dma_start(sc[:, :, :].rearrange("p n k -> p (n k)"), d["scores_keep"][0]).then_inc(scores_in, 16)
            with pool.Fori(1, TILES) as i:
                pool.wait_ge(s_used, i)
                pool.wait_ge(scores_in, 16 * i)
                pool.dma_start(sc[:, :, :].rearrange("p n k -> p (n k)"), d["scores_keep"][i]).then_inc(scores_in, 16)

        @block.scalar
        def _(act):
            def u_hi(e, step, fresh=False):
                act.wait_ge(u_turned, step + 1)
                nc.scalar.activation(uT[0][:, e, :, :], ps_u[:, :].rearrange("p (j k) -> p j k", k=P), ACT.Copy).then_inc(uhi_ready, 1)

            def gate_unit(tile, unit):
                half, slot = unit // (UNITS // 2), unit % 2
                if unit % (UNITS // 2) == 0 and at_least(tile, 1):
                    act.wait_ge(stored[half], 16 * tile)
                n = tile * UNITS + unit
                act.wait_ge(gate_done, n + 1)
                at = (unit * UNIT) % HALF_T
                nc.scalar.activation(gates[half][:, :, at:at + UNIT],
                                     ps_g[:, slot * NB:(slot + 1) * NB].rearrange("p (t k) -> p k t", k=KEYS), ACT.Copy).then_inc(gate_out, 1)
                if (unit + 1) % (UNITS // 2) == 0:
                    act.wait_ge(gate_out, n + 1)
                    act.dma_start(d["gates_keep"][2 * tile + half], gates[half].rearrange("p k t -> p (k t)")).then_inc(stored[half], 16)

            def pair(i, c, step0, tile, units, unit0):
                for e in range(2):
                    step = step0 + e
                    act.wait_ge(hid_done, step + 1)
                    if at_least(step, 2):
                        act.wait_ge(hid_stored[e], 8 * (step - e))
                    nc.scalar.activation(hid[:, e, :], ps_h[e][:, :], ACT.Gelu).then_inc(gelu_done, 1)
                    if has_next(step):
                        u_hi(e, step + 2)
                    for k in range(units):
                        gate_unit(tile, unit0 + e * units + k)
                if c == (1 if tile is None else 3) and not (isinstance(i, int) and i == TILES):
                    act.wait_ge(top_done, i + 1)
                    nc.scalar.activation(red[:, :, :], red[:, :, :], ACT.Exp).then_inc(exp_done, 1)

            def end(i):
                act.wait_ge(route_turned, i + 1)
                nc.scalar.activation(routeT[:, :, :], ps_g[:, 0:3 * P].rearrange("p (n t) -> p n t", t=P), ACT.Copy).then_inc(routeT_ready, 1)

            for e in range(2):
                u_hi(e, e)
            over_rounds(act, pair, end)
            for half in range(2):
                act.wait_ge(stored[half], 16 * TILES)

        @block.tensor
        def _(pe):
            def turn(e, step):
                pe.wait_ge(u_in[e], 8 * (step - e) + 16)
                if at_least(step, 1):
                    pe.wait_ge(ulo_ready, step)
                for j in range(DC):
                    last = nc.tensor.transpose(ps_u[:, j * P:(j + 1) * P], u_raw[:, e, j * P:(j + 1) * P], ident)
                last.then_inc(u_turned, 1)

            def hidden(e, step):
                pe.wait_ge(ulo_ready, step + 1)
                if at_least(step, 2):
                    pe.wait_ge(gelu_done, step - 1)
                for half in range(2):
                    n = 0
                    for a, b in ((0, 0), (0, 1), (1, 0)):
                        for j in range(DC):
                            last = nc.tensor.matmul(ps_h[e][:, half * NB:(half + 1) * NB], uT[a][:, e, j, :],
                                                    h_part[b][:, j, half * NB:(half + 1) * NB],
                                                    start=(n == 0), stop=(n == 3 * DC - 1))
                            n += 1
                last.then_inc(hid_done, 1)

            def gate_unit(tile, unit):
                slot = unit % 2
                n = tile * UNITS + unit
                pe.wait_ge(hot_ready, n + 1)
                if at_least(n, 2):
                    pe.wait_ge(gate_out, n - 1)
                for t in range(UNIT):
                    k = slot * UNIT + t
                    last = nc.tensor.matmul(ps_g[:, k * P:(k + 1) * P], hot1[:, slot, t, :], hot2[:, slot, t, :], start=True, stop=True)
                last.then_inc(gate_done, 1)

            def pair(i, c, step0, tile, units, unit0):
                for e in range(2):
                    hidden(e, step0 + e)
                    if has_next(step0 + e):
                        turn(e, step0 + e + 2)
                    for k in range(units):
                        gate_unit(tile, unit0 + e * units + k)

            def end(i):
                pe.wait_ge(route_ready, i + 1)
                if at_least(i, 1):
                    pe.wait_ge(gate_out, i * UNITS)
                for n in range(3):
                    last = nc.tensor.transpose(ps_g[:, n * P:(n + 1) * P], route[:, n, :], ident)
                last.then_inc(route_turned, 1)

            for e in range(2):
                turn(e, e)
            over_rounds(pe, pair, end)

        @block.vector
        def _(dve):
            V = nc.vector
            chain = Chain(dve, dve_chain)
            V.tensor_copy(starts[:, 0:2 * NTH], const[:, C_START:C_START + 2 * NTH]).then_inc(starts_ready, 1)
            V.tensor_copy(starts[:, 2 * NTH:2 * NTH + TOPK], const[:, C_IOTA:C_IOTA + TOPK]).then_inc(starts_ready, 1)
            dve.wait_ge(starts_ready, 2)
            th = starts[:, 0:NTH].unsqueeze(1).to_broadcast([P, P, NTH])
            dth = starts[:, NTH:2 * NTH].unsqueeze(1).to_broadcast([P, P, NTH])
            cols = starts[:, 2 * NTH:].unsqueeze(1).to_broadcast([P, P, TOPK])
            heads4 = [P, PEER_HEADS, TOPK, TOPK]
            pair_vals = vals[:, :, :].rearrange("p (h a) k -> p h a k", a=2)
            pidx = idx[:, :, :].rearrange("p (h a) k -> p h a k", a=2)
            flat = lambda t: t.rearrange("p h k -> p (h k)")
            deep = past[:, :, :, 0:NTH].rearrange("p h k r -> p (h k) r")
            pdeep = prod[:, :, :, 0:NTH]
            by_rank = lambda n: route[:, n, :].rearrange("p (h k) -> p h k", h=PEER_HEADS)
            r1, r2, rg = by_rank(0), by_rank(1), by_rank(2)
            ranks = [P, PEER_HEADS, TOPK]

            def first_keys(i):
                dve.wait_ge(scores_in, 16 * i + 16)
                V.memset(stand[:, :], 0.0)
                for n in range(NQ):
                    last = V.max(vals[:, n, 0:8], sc[:, n, :])
                chain.link(last)
                for n in range(NQ // 2):
                    V.max_index(idx_u[:, n, 0:8], vals[:, n, 0:8], sc[:, n, :])
                    last = V.match_replace(rest[:, n, :], vals[:, n, 0:8], sc[:, n, :], LOWEST)
                chain.step(last)

            def more_keys(i):
                for n in range(NQ // 2, NQ):
                    V.max_index(idx_u[:, n, 0:8], vals[:, n, 0:8], sc[:, n, :])
                    last = V.match_replace(rest[:, n, :], vals[:, n, 0:8], sc[:, n, :], LOWEST)
                chain.link(last)
                V.memset(stand[:, :], 0.0).then_inc(s_used, 1)
                for n in range(NQ):
                    last = V.max(vals[:, n, 8:16], rest[:, n, :])
                chain.step(last)

            def candidates(i):
                chain.wait()
                for n in range(NQ):
                    last = V.max_index(idx_u[:, n, 8:16], vals[:, n, 8:16], rest[:, n, :])
                at = 0
                for a0, a1, w in RECTS:
                    m = (a1 - a0) * w
                    shape = [P, PEER_HEADS, a1 - a0, w]
                    last = V.tensor_tensor(cand[:, :, at:at + m].rearrange("p h (a b) -> p h a b", b=w),
                                           pair_vals[:, :, 0, a0:a1].unsqueeze(3).to_broadcast(shape),
                                           pair_vals[:, :, 1, 0:w].unsqueeze(2).to_broadcast(shape), ALU.add)
                    at += m
                chain.link(last)
                V.tensor_copy(idx[:, :, :], idx_u[:, :, :])
                for n in range(PEER_HEADS):
                    last = V.max(top[:, n, 0:8], cand[:, n, :])
                chain.step(last)

            def tops(i):
                chain.wait()
                for n in range(PEER_HEADS):
                    V.max_index(pos_u[:, n, 0:8], top[:, n, 0:8], cand[:, n, :])
                    last = V.match_replace(cand_rest[:, n, :], top[:, n, 0:8], cand[:, n, :], LOWEST)
                chain.link(last)
                for n in range(PEER_HEADS):
                    last = V.max(top[:, n, 8:16], cand_rest[:, n, :])
                chain.link(last)
                for n in range(PEER_HEADS):
                    last = V.max_index(pos_u[:, n, 8:16], top[:, n, 8:16], cand_rest[:, n, :])
                V.tensor_tensor(red[:, :, :], top[:, :, :], top[:, :, 0:1].to_broadcast(ranks), ALU.subtract).then_inc(top_done, 1)
                dve.wait_ge(top_done, i + 1)
                V.tensor_tensor(step1[:, :, :], pidx[:, :, 0, 1:TOPK], pidx[:, :, 0, 0:NTH], ALU.subtract)
                chain.step(V.tensor_copy(pos[:, :, :], pos_u[:, :, :]))

            def rows(i):
                chain.wait()
                chain.link(V.tensor_tensor(deep, flat(pos[:, :, :]).unsqueeze(2).to_broadcast([P, P, NTH]), th, ALU.is_ge))
                chain.link(V.tensor_tensor(pdeep, past[:, :, :, 0:NTH], step1[:, :, :].unsqueeze(2).to_broadcast([P, PEER_HEADS, TOPK, NTH]), ALU.mult))
                chain.link(V.tensor_reduce(r1, pdeep, AX.X, ALU.add))
                chain.step(V.tensor_tensor(pdeep.rearrange("p h k r -> p (h k) r"), deep, dth, ALU.mult))

            def columns(i):
                dve.wait_ge(exp_done, i + 1)
                V.tensor_reduce(gsum[:, 0, :], red[:, :, :], AX.X, ALU.add)
                chain.link(V.tensor_tensor(r1, r1, pidx[:, :, 0, 0:1].to_broadcast(ranks), ALU.add))
                V.reciprocal(gsum[:, 1, :], gsum[:, 0, :])
                chain.link(V.tensor_reduce(r2, pdeep, AX.X, ALU.add))
                V.tensor_tensor(rg, red[:, :, :], gsum[:, 1, :].unsqueeze(2).to_broadcast(ranks), ALU.mult)
                chain.link(V.tensor_tensor(col[:, :, :], pos[:, :, :], r2, ALU.subtract))
                chain.step(V.tensor_tensor(past[:, :, :, :].rearrange("p h k r -> p (h k) r"),
                                           flat(col[:, :, :]).unsqueeze(2).to_broadcast([P, P, TOPK]), cols, ALU.is_equal))

            def route_out(i):
                chain.wait()
                chain.link(V.tensor_tensor(prod[:, :, :, :], past[:, :, :, :], pidx[:, :, 1, :].unsqueeze(2).to_broadcast(heads4), ALU.mult))
                V.tensor_reduce(r2, prod[:, :, :, :], AX.X, ALU.add).then_inc(route_ready, 1)
                chain.clear()

            parts = (first_keys, more_keys, candidates, tops, rows, columns, route_out)

            def u_lo(e, step):
                dve.wait_ge(uhi_ready, step + 1)
                V.tensor_tensor(uT[1][:, e, :, :], ps_u[:, :].rearrange("p (j k) -> p j k", k=P), uT[0][:, e, :, :].bitcast(F32), ALU.subtract).then_inc(ulo_ready, 1)

            def gate_unit(tile, unit):
                slot = unit % 2
                n = tile * UNITS + unit
                if at_least(n, 2):
                    dve.wait_ge(gate_done, n - 1)
                for t in range(UNIT):
                    tok = slice(unit * UNIT + t, unit * UNIT + t + 1)
                    V.tensor_scalar(hot1[:, slot, t, :], iota, routeT[:, 0, tok], routeT[:, 2, tok], ALU.is_equal, ALU.mult)
                    last = V.tensor_scalar(hot2[:, slot, t, :], iota, routeT[:, 1, tok], None, ALU.is_equal)
                last.then_inc(hot_ready, 1)

            def pair(i, c, step0, tile, units, unit0):
                if tile is None:
                    for part in parts[2 * c:2 * c + 2]:
                        part(i)
                elif not isinstance(i, int) or i < TILES:
                    for part in parts[c:c + 1]:
                        part(i)
                for e in range(2):
                    for k in range(units):
                        gate_unit(tile, unit0 + e * units + k)
                    if has_next(step0 + e):
                        u_lo(e, step0 + e + 2)

            def end(i):
                dve.wait_ge(routeT_ready, i + 1)

            for e in range(2):
                u_lo(e, e)
            over_rounds(dve, pair, end)


def outputs(nc, d, keep):
    G4 = 4
    GROUPS = KEYS // G4
    with ExitStack() as ctx:
        sb = lambda n, s, t=F32: ctx.enter_context(nc.sbuf_tensor(n, s, t))
        sem = lambda n: ctx.enter_context(nc.semaphore(n))
        ps = lambda n, w: ctx.enter_context(nc.psum_tensor(n, [P, w], F32))
        acc = keep["acc"]
        v_raw = sb("v_raw", [P, 2, D])
        hid = sb("hid_back", [P, 2, SEQ])
        gate = sb("gate", [P, 2, PIECES, 2, HALF_T])
        a_part = (sb("act_hi", [P, 2, G4, SEQ], F32R), sb("act_lo", [P, 2, G4, SEQ], F32R))
        v_part = (sb("v_hi", [P, 2, G4, D], F32R), sb("v_lo", [P, 2, G4, D], F32R))
        ps_a = [ps(f"ps_a{e}", 2 * NB) for e in range(2)]
        ps_y = [ps(f"ps_y{b}", NB) for b in range(4)]
        v_in = [sem(f"v_in{b}") for b in range(2)]
        h_in = [sem(f"hid_in{b}") for b in range(2)]
        g_in = [sem(f"gate_in{b}") for b in range(2)]
        vhi_ready, vlo_ready = sem("vhi_ready"), sem("vlo_ready")
        gated, ahi_ready, alo_ready = sem("gated"), sem("ahi_ready"), sem("alo_ready")
        y_done, y_added = sem("y_done2"), sem("y_added")
        acc_zero = sem("acc_zero")
        block = ctx.enter_context(nc.Block())
        v_view = d["peer_v"].rearrange("a (k1 k2) n -> (a k1) k2 n", k2=KEYS)
        g_view = d["gates_keep"].rearrange("c p (m k t) -> p m c k t", k=2, t=HALF_T)
        hid_view = d["hid_keep"].rearrange("k2 p t -> p k2 t")
        YP = 2 * TILES
        YS = YP // G4

        @block.sync
        def _(sp):
            def body(g, slot):
                for e in range(G4):
                    step, raw, pr = G4 * g + e, e % 2, e // 2
                    if at_least(step, 2):
                        sp.wait_ge(gated, step - 1)
                    sp.dma_start(hid[:, raw, :], one2(hid_view, step)).then_inc(h_in[raw], 16)
                    if e % 2 == 0:
                        if at_least(g, 1):
                            sp.wait_ge(gated, G4 * (g - 1) + e + 2)
                        sp.dma_start(gate[:, pr, :, :, :].rearrange("p c k t -> p c (k t)"),
                                     one_pair(g_view, 2 * g + pr)).then_inc(g_in[pr], 16)
                    if at_least(step, 2):
                        sp.wait_ge(vlo_ready, step - 1)
                    sp.dma_start(v_raw[:, raw, :], one2(v_view, step)).then_inc(v_in[raw], 16)
            in_pairs(sp, GROUPS, body)

        @block.gpsimd
        def _(pool):
            nc.gpsimd.memset(acc[:, :, :], 0.0).then_inc(acc_zero, 1)

            def body(g, slot):
                for e in range(G4):
                    step = G4 * g + e
                    pool.wait_ge(vhi_ready, step + 1)
                    nc.gpsimd.tensor_tensor(v_part[1][:, slot, e, :], v_raw[:, e % 2, :], v_part[0][:, slot, e, :].bitcast(F32), ALU.subtract).then_inc(vlo_ready, 1)
            in_pairs(pool, GROUPS, body)

        @block.scalar
        def _(act):
            def body(g, slot):
                for e in range(G4):
                    step, raw = G4 * g + e, e % 2
                    act.wait_ge(v_in[raw], 16 * (2 * g + e // 2) + 16)
                    if at_least(g, 2) and e == 0:
                        act.wait_ge(y_done, (g - 1) * YP)
                    nc.scalar.activation(v_part[0][:, slot, e, :], v_raw[:, raw, :], ACT.Copy).then_inc(vhi_ready, 1)
                    act.wait_ge(gated, step + 1)
                    nc.scalar.activation(a_part[0][:, slot, e, :], ps_a[raw][:, :], ACT.Copy).then_inc(ahi_ready, 1)
            in_pairs(act, GROUPS, body)

        @block.tensor
        def _(pe):
            def body(g, slot):
                pe.wait_ge(alo_ready, G4 * g + G4)
                pe.wait_ge(vlo_ready, G4 * g + G4)
                for q in range(YP):
                    t, half = q // 2, q % 2
                    if q >= 4 or at_least(g, 1):
                        pe.wait_ge(y_added, g * YP + q - 3)
                    n = 0
                    for e in range(G4):
                        for a, b in ((0, 0), (0, 1), (1, 0)):
                            last = nc.tensor.matmul(ps_y[q % 4][:, :], a_part[a][:, slot, e, t * P:(t + 1) * P],
                                                    v_part[b][:, slot, e, half * NB:(half + 1) * NB],
                                                    start=(n == 0), stop=(n == 3 * G4 - 1))
                            n += 1
                    last.then_inc(y_done, 1)
            in_pairs(pe, GROUPS, body)

        @block.vector
        def _(dve):
            V = nc.vector

            def add_out(g, q):
                t, half = q // 2, q % 2
                dve.wait_ge(y_done, g * YP + q + 1)
                if q == 0 and at_least(g, 1):
                    dve.wait_ge(y_added, g * YP)
                dst = acc[:, t, half * NB:(half + 1) * NB]
                V.tensor_tensor(dst, ps_y[q % 4][:, :], dst, ALU.add).then_inc(y_added, 1)

            def body(g, slot):
                for e in range(G4):
                    step, raw, pr = G4 * g + e, e % 2, e // 2
                    dve.wait_ge(h_in[raw], 16 * (2 * g + pr) + 16)
                    dve.wait_ge(g_in[pr], 16 * g + 16)
                    if at_least(step, 2):
                        dve.wait_ge(alo_ready, step - 1)
                    V.tensor_tensor(ps_a[raw][:, :].rearrange("p (c t) -> p c t", t=HALF_T), hid[:, raw, :].rearrange("p (c t) -> p c t", t=HALF_T),
                                    gate[:, pr, :, e % 2, :], ALU.mult).then_inc(gated, 1)
                    for q in range(e * YS, (e + 1) * YS):
                        if at_least(g, 1):
                            add_out(g - 1, q)
                    dve.wait_ge(ahi_ready, step + 1)
                    V.tensor_tensor(a_part[1][:, slot, e, :], ps_a[raw][:, :], a_part[0][:, slot, e, :].bitcast(F32), ALU.subtract).then_inc(alo_ready, 1)

            dve.wait_ge(acc_zero, 1)
            in_pairs(dve, GROUPS, body)
            for q in range(YP):
                add_out(GROUPS - 1, q)


def one2(view, n):
    return view[:, n, :] if isinstance(n, int) else view[:, bass.ds(n, 1), :].rearrange("p a n -> p (a n)")


def one_pair(view, n):
    part = view[:, n] if isinstance(n, int) else view[:, bass.ds(n, 1)].rearrange("p m c k t -> p (m c) k t")
    return part.rearrange("p c k t -> p c (k t)")


def final(nc, d, keep):
    with ExitStack() as ctx:
        sb = lambda n, s, t=F32: ctx.enter_context(nc.sbuf_tensor(n, s, t))
        sem = lambda n: ctx.enter_context(nc.semaphore(n))
        acc = keep["acc"]
        gate2, ln_g, ln_b = sb("gate2", [P, D]), sb("ln2_gain", [P, D]), sb("ln2_bias", [P, D])
        x1 = sb("x1", [P, TILES, D])
        stats, mv = sb("stats2", [P, TILES, 2, 6]), sb("mean_var2", [P, TILES, 2])
        rstd, power = sb("rstd2", [P, TILES, 2]), sb("power2", [P, 1])
        rows_in, x1_in, power_set = sem("final_rows_in"), sem("x1_in"), sem("power_set")
        var_ready, rstd_ready, out_ready, out_stored = sem("var2_ready"), sem("rstd2_ready"), sem("out_ready"), sem("out_stored")
        dve_chain = sem("dve_chain4")
        block = ctx.enter_context(nc.Block())

        @block.sync
        def _(sp):
            sp.dma_start(gate2[:, :], d["gate2_keep"]).then_inc(rows_in, 16)
            sp.dma_start(x1[:, :, :], d["x1_keep"].rearrange("t p n -> p t n")).then_inc(x1_in, 16)
            for t in range(TILES):
                sp.wait_ge(out_ready, t + 1)
                sp.dma_start(d["out"].rearrange("a (t p) n -> (a t) p n", p=P)[t], acc[:, t, :]).then_inc(out_stored, 16)
            sp.wait_ge(out_stored, 16 * TILES)

        @block.gpsimd
        def _(pool):
            nc.gpsimd.memset(power[:, :], -0.5).then_inc(power_set, 1)
            pool.wait_ge(power_set, 1)
            for t in range(TILES):
                pool.wait_ge(var_ready, t + 1)
                nc.gpsimd.tensor_tensor(rstd[:, t, 0:1], rstd[:, t, 1:2], power[:, :], ALU.pow).then_inc(rstd_ready, 1)

        @block.scalar
        def _(act):
            act.dma_start(ln_g[:, :], d["ln2_g"].to_broadcast([P, D])).then_inc(rows_in, 16)
            act.dma_start(ln_b[:, :], d["ln2_b"].to_broadcast([P, D])).then_inc(rows_in, 16)

        @block.vector
        def _(dve):
            V = nc.vector
            chain = Chain(dve, dve_chain)
            dve.wait_ge(rows_in, 48)
            dve.wait_ge(x1_in, 16)
            for t in range(TILES):
                y = acc[:, t, :]
                chain.link(V.tensor_tensor(y, y, gate2[:, :], ALU.mult))
                chain.link(V.scalar_tensor_tensor(y, x1[:, t, :], ALPHA, y, ALU.mult, ALU.add))
                V.bn_stats(stats[:, t, 0, :], acc[:, t, 0:NB])
                chain.link(V.bn_stats(stats[:, t, 1, :], acc[:, t, NB:D]))
                chain.link(V.bn_aggr(mv[:, t, :], stats[:, t, :, :]))
                V.tensor_scalar_add(rstd[:, t, 1:2], mv[:, t, 1:2], EPS).then_inc(var_ready, 1)
                chain.link(V.scalar_tensor_tensor(y, y, mv[:, t, 0:1], ln_g[:, :], ALU.subtract, ALU.mult))
                dve.wait_ge(rstd_ready, t + 1)
                V.scalar_tensor_tensor(y, y, rstd[:, t, 0:1], ln_b[:, :], ALU.mult, ALU.add).then_inc(out_ready, 1)


def build(nc, d):
    d["gate2_keep"] = nc.dram_tensor("gate2_keep", [P, D], F32, kind="Internal").ap()
    d["x1_keep"] = nc.dram_tensor("x1_keep", [TILES, P, D], F32, kind="Internal").ap()
    d["scores_keep"] = nc.dram_tensor("scores_keep", [TILES, P, NQ * KEYS], F32, kind="Internal").ap()
    d["hid_keep"] = nc.dram_tensor("hid_keep", [KEYS, P, SEQ], F32, kind="Internal").ap()
    d["gates_keep"] = nc.dram_tensor("gates_keep", [PIECES, P, KEYS * HALF_T], F32, kind="Internal").ap()
    keep = {}
    with ExitStack() as ctx:
        sb = lambda n, s, t=F32: ctx.enter_context(nc.sbuf_tensor(n, s, t))
        keep["h2T"] = keep["acc"] = sb("h2T_then_sums", [P, DC, SEQ])
        with nc.sbuf_tensor("const", [P, C_WIDTH], F32) as const:
            keep["const"] = const
            with nc.sbuf_tensor("mod", [P, 6, D], F32) as mod, nc.sbuf_tensor("pool_col", [P, PG], F32) as pool_col:
                keep["mod"], keep["pool_col"] = mod, pool_col
                modulation(nc, d, keep)
                mixing(nc, d, keep)
            with nc.sbuf_tensor("h_hi", [P, DC, SEQ], F32R) as h_hi, nc.sbuf_tensor("h_lo", [P, DC, SEQ], F32R) as h_lo:
                keep["h_hi"], keep["h_lo"] = h_hi, h_lo
                queries(nc, d, keep)
                routing(nc, d, keep)
        outputs(nc, d, keep)
        final(nc, d, keep)


_INS = ['x', 'c', 'w_ada', 'b_ada', 'w_in', 'attn_sinks', 'w_pool', 'pool_scale', 'w_out', 'ln1_g', 'ln1_b',
        'w_pq', 'peer_k1', 'peer_k2', 'peer_u', 'peer_v', 'ln2_g', 'ln2_b']


def shape_constants():
    import numpy as np
    k = np.zeros((P, C_WIDTH), np.float32)
    k[:, C_IDENT:C_IDENT + P] = np.eye(P)
    q, s = np.arange(P)[:, None], np.arange(2 * P)[None, :]
    rel = q + P - s
    band = (rel >= 0) & (rel < P)
    k[:, C_MASK:C_MASK + 2 * P] = np.where(band & (s >= P), 0.0, NEG)
    k[:, C_MASK + 2 * P:C_MASK + 4 * P] = np.where(band, 0.0, NEG)
    s, t = np.arange(P)[:, None], np.arange(P)[None, :]
    for g, w in enumerate(POOLS):
        own = (s <= t) & (t - s < w)
        prev = t + P - s < w
        first = np.where(own, 1.0 / np.minimum(t + 1, w), 0.0) - (s == t)
        for n, m in enumerate((first, own / w - (s == t), prev / w)):
            at = C_BAND + (3 * g + n) * P
            k[:, at:at + P] = m
    k[:, C_IOTA:C_IOTA + P] = np.arange(P)
    starts = np.array(ROW_START, np.float32)
    k[:, C_START:C_START + NTH] = starts[1:]
    k[:, C_DSTART:C_DSTART + NTH] = starts[1:] - starts[:-1]
    freqs = np.float32(10000.0) ** (-np.arange(HALF, dtype=np.float32) / np.float32(HALF))
    ang = np.arange(SEQ, dtype=np.float32)[:, None] * freqs[None, :]
    for at, f in ((C_COS, np.cos), (C_SIN, np.sin)):
        tab = f(ang).astype(np.float32).reshape(TILES, P, HALF).transpose(1, 0, 2)
        k[:, at:at + TILES * HALF] = tab.reshape(P, TILES * HALF)
    return k


def kernel(**inputs):
    import numpy as _np
    import concourse.bacc as _bacc
    from concourse import mybir as _mybir
    from concourse.bass_utils import run_bass_kernel_spmd as _run

    nc = _bacc.Bacc("TRN2", target_bir_lowering=False, num_devices=1)
    arrays, d = {}, {}
    for name in _INS:
        a = _np.ascontiguousarray(inputs[name])
        arrays[f"in_{name}_dram"] = a
        d[name] = nc.dram_tensor(f"in_{name}_dram", a.shape, _mybir.dt.from_np(a.dtype), kind="ExternalInput").ap()
    arrays["const_dram"] = shape_constants()
    d["const"] = nc.dram_tensor("const_dram", arrays["const_dram"].shape, F32, kind="ExternalInput").ap()
    d["out"] = nc.dram_tensor("out_0_dram", (1, SEQ, D), F32, kind="ExternalOutput").ap()
    build(nc, d)
    r = _run(nc, [arrays], core_ids=[0])
    return r.results[0]["out_0_dram"]
```

```python
from contextlib import ExitStack

import concourse.bass as bass
from concourse import mybir

ALU = mybir.AluOpType
ACT = mybir.ActivationFunctionType
AX = mybir.AxisListType
F32 = mybir.dt.float32
F32R = mybir.dt.float32r
BF16 = mybir.dt.bfloat16
U32 = mybir.dt.uint32

P = 128
D = 1024
DC = D // P
SEQ = 1024
TILES = SEQ // P
HD = 64
HALF = HD // 2
HEADS, KV_HEADS = 8, 2
QW, KVW = HEADS * HD, KV_HEADS * HD
POOLS = (2, 4, 8, 16)
PG = len(POOLS)
PW = D - QW
PEER_HEADS, KEYS, TOPK = 8, 128, 16
NQ = 2 * PEER_HEADS
EXPERTS = KEYS * KEYS
ALPHA = 2.0 ** 0.25
EPS = 1e-5
NEG = -1e30
LOWEST = -3.0e38
NB = 512

RECTS = ((0, 2, 16), (2, 8, 5), (8, 16, 1))
CAND = sum((a1 - a0) * w for a0, a1, w in RECTS)
ROW_START = [sum((min(a, a1) - a0) * w for a0, a1, w in RECTS if a > a0) for a in range(TOPK)]
NTH = TOPK - 1

HALF_T = 64
PIECES = SEQ // HALF_T

C_IDENT = 0
C_IOTA = C_IDENT + P
C_START = C_IOTA + P
C_DSTART = C_START + NTH
C_WIDTH = C_DSTART + NTH
M_MASK = 0
M_BAND = M_MASK + 4 * P
M_COS = M_BAND + PG * 3 * P
M_SIN = M_COS + TILES * HALF
M_WIDTH = M_SIN + TILES * HALF


class Chain:

    def __init__(self, eng, sem):
        self.eng, self.sem, self.n = eng, sem, 0

    def step(self, ins):
        ins.then_inc(self.sem, 1)
        self.n += 1

    def wait(self):
        self.eng.wait_ge(self.sem, self.n)

    def link(self, ins):
        self.step(ins)
        self.wait()

    def clear(self):
        self.wait()
        self.eng.sem_clear(self.sem)
        self.n = 0


def modulation(nc, d, keep):
    CH = 6 * D // NB
    RING = 3
    with ExitStack() as ctx:
        sb = lambda n, s, t=F32: ctx.enter_context(nc.sbuf_tensor(n, s, t))
        sem = lambda n: ctx.enter_context(nc.semaphore(n))
        c_col = sb("c_col", [P, DC])
        c_act = sb("c_act", [P, DC])
        c_rep = sb("c_rep", [P, DC, P])
        ones = sb("ones", [1, P])
        bias = sb("bias", [1, RING, NB])
        wada = sb("wada", [P, RING, DC, NB])
        pool_row = sb("pool_row", [PG, P])
        ps = [ctx.enter_context(nc.psum_tensor(f"ps_mod{i}", [P, NB], F32)) for i in range(2)]
        ps_turn = ctx.enter_context(nc.psum_tensor("ps_turn", [P, PG], F32))
        c_in, const_in, silu_done = sem("c_in"), sem("const_in"), sem("silu_done")
        ones_set, rep_ready = sem("ones_set"), sem("rep_ready")
        w_in = [sem(f"wada_in{i}") for i in range(RING)]
        mod_sum, mod_out = sem("mod_sum"), sem("mod_out")
        gate2_out, turned = sem("gate2_out"), sem("pool_turned")
        pool_ready, rows_in = sem("pool_ready"), sem("ada_rows_in")
        block = ctx.enter_context(nc.Block())
        w_view = d["w_ada"].rearrange("a (p j) n -> (a p) j n", j=DC)

        @block.sync
        def _(sp):
            sp.dma_start(c_col[:, :], d["c"].rearrange("a (p j) -> (a p) j", j=DC)).then_inc(c_in, 16)
            for n in range(CH):
                if n >= RING:
                    sp.wait_ge(mod_sum, n - RING + 1)
                sp.dma_start(wada[:, n % RING, :, :],
                             w_view[:, :, n * NB:(n + 1) * NB]).then_inc(w_in[n % RING], 16)
                sp.dma_start(bias[:, n % RING, :], d["b_ada"][:, n * NB:(n + 1) * NB]).then_inc(w_in[n % RING], 16)
                if n >= RING and n - RING < DC:
                    load_mix_weights(sp, d, keep, n - RING)
            sp.wait_ge(mod_out, CH)
            sp.dma_start(d["gate2_keep"], keep["mod"][:, 5, :]).then_inc(gate2_out, 16)
            sp.wait_ge(gate2_out, 16)

        @block.gpsimd
        def _(pool):
            nc.gpsimd.memset(ones[:, :], 1.0).then_inc(ones_set, 1)

        @block.scalar
        def _(act):
            act.dma_start(keep["const"][:, :], d["const"]).then_inc(const_in, 16)
            act.dma_start(keep["mix_const"][:, :], d["mix_const"]).then_inc(keep["mix_in"], 16)
            act.dma_start(pool_row[:, :], d["pool_scale"].rearrange("a (g p) -> (a g) p", p=P)).then_inc(rows_in, 16)
            act.wait_ge(c_in, 16)
            nc.scalar.activation(c_act[:, :], c_col[:, :], ACT.Silu).then_inc(silu_done, 1)

        @block.tensor
        def _(pe):
            pe.wait_ge(const_in, 16)
            pe.wait_ge(rows_in, 16)
            nc.tensor.transpose(ps_turn[:, 0:PG], pool_row[:, :], keep["const"][0:PG, 0:PG]).then_inc(turned, 1)
            pe.wait_ge(rep_ready, 1)
            pe.wait_ge(ones_set, 1)
            for n in range(CH):
                pe.wait_ge(w_in[n % RING], 32 * (n // RING + 1))
                if n >= 2:
                    pe.wait_ge(mod_out, n - 1)
                for j in range(DC):
                    nc.tensor.matmul(ps[n % 2][:, :], c_rep[:, j, :], wada[:, n % RING, j, :], start=(j == 0), stop=False)
                nc.tensor.matmul(ps[n % 2][:, :], ones[:, :], bias[:, n % RING, :],
                                 start=False, stop=True).then_inc(mod_sum, 1)

        @block.vector
        def _(dve):
            dve.wait_ge(silu_done, 1)
            for j in range(DC):
                last = nc.vector.tensor_copy(c_rep[:, j, :], c_act[:, j:j + 1].to_broadcast([P, P]))
            last.then_inc(rep_ready, 1)
            dve.wait_ge(turned, 1)
            nc.vector.tensor_copy(keep["pool_col"][:, :], ps_turn[:, :]).then_inc(pool_ready, 1)
            for n in range(CH):
                dve.wait_ge(mod_sum, n + 1)
                kind = n * NB // D
                one = 0.0 if kind in (0, 3) else 1.0
                at = (n * NB) % D
                nc.vector.tensor_scalar_add(keep["mod"][:, kind, at:at + NB], ps[n % 2][:, :], one).then_inc(mod_out, 1)


def load_mix_weights(sp, d, keep, j):
    for name in ("w_in", "w_out"):
        sp.dma_start(keep[name][:, j, :], d[name].rearrange("a (j p) n -> (a p) j n", p=P)[:, j, :]).then_inc(keep["mix_in"], 16)


def mixing(nc, d, keep):
    with ExitStack() as ctx:
        sb = lambda n, s, t=F32: ctx.enter_context(nc.sbuf_tensor(n, s, t))
        sem = lambda n: ctx.enter_context(nc.semaphore(n))
        ps = lambda n, w: ctx.enter_context(nc.psum_tensor(n, [P, w], F32))
        const, mix_const, mod, h2T = keep["const"], keep["mix_const"], keep["mod"], keep["h2T"]
        ident = const[:, C_IDENT:C_IDENT + P]
        w_in, w_out = keep["w_in"], keep["w_out"]
        w_pool = sb("w_pool", [P, PG, P])
        ln_g, ln_b = sb("ln1_gain", [P, D]), sb("ln1_bias", [P, D])
        sink = sb("sink", [P, HEADS])
        xt, xr = sb("x_tile", [P, D]), sb("x_residual", [P, D])
        h, hT = sb("h_tile", [P, D]), sb("hT", [P, DC, P])
        rot_a, rot_b = sb("rot_a", [P, 10 * HD]), sb("rot_b", [P, 10 * HD])
        qk = sb("qk", [P, 10 * HD])
        qT, kT = sb("qT", [P, 4, P]), sb("kT", [P, 2, P])
        v, pin = sb("v", [P, 2, KVW]), sb("pool_in", [P, 2, PW])
        s = sb("scores", [P, 2, 4, 2 * P])
        pT = sb("probsT", [P, 8, P])
        small = sb("small", [P, 5, HEADS])
        pooledT = rot_a[:, 0:PW]
        mixT = sb("mixT", [P, DC, P])
        y, h2 = sb("y", [P, D]), sb("h2", [P, D])
        stats, mv, rstd = sb("stats", [P, 2, 6]), sb("mean_var", [P, 2]), sb("rstd", [P, 2])
        power = sb("power", [P, 1])
        ps_t, ps_p, ps_s, ps_o = ps("ps_t", 2 * NB), ps("ps_p", 3 * NB), ps("ps_s", 2 * NB), ps("ps_o", NB)

        w_ready, x_in, xr_in, x1_out = sem("mix_rows_in"), sem("x_in"), sem("xr_in"), sem("x1_out")
        zeroed = sem("zeroed")
        h_ready, h_turned, hT_ready, proj_done = sem("h_ready"), sem("h_turned"), sem("hT_ready"), sem("proj_done")
        rope_done, qk_turned, qkT_ready, vp_ready = sem("rope_done"), sem("qk_turned"), sem("qkT_ready"), sem("vp_ready")
        scores_done, s_ready, negm_ready, exp_done = sem("scores_done"), sem("s_ready"), sem("negm_ready"), sem("exp_done")
        rden_ready, probs_ready, pT_done, pT_ready = sem("rden_ready"), sem("probs_ready"), sem("pT_done"), sem("pT_ready")
        pv_done, mixa_ready, pooled_done, pooledT_ready = sem("pv_done"), sem("mixa_ready"), sem("pooled_done"), sem("pooledT_ready")
        y_done, mixb_ready, out_done, out_taken, res_done = (
            sem("y_done"), sem("mixb_ready"), sem("out_done"), sem("out_taken"), sem("res_done"))
        var_ready, rstd_ready, x1_ready, h2_ready = sem("var_ready"), sem("rstd_ready"), sem("x1_ready"), sem("h2_ready")
        h2_turned, h2T_ready = sem("h2_turned"), sem("h2T_ready")
        dve_chain, pool_chain = sem("dve_chain1"), sem("pool_chain1")
        block = ctx.enter_context(nc.Block())
        x_view = d["x"].rearrange("a (t p) n -> (a t) p n", p=P)

        def over_tiles(eng, body):
            body(0)
            body(1)
            with eng.Fori(2, TILES - 1) as i:
                body(i)
            body(TILES - 1)

        first = lambda i: isinstance(i, int) and i == 0
        final_tile = lambda i: isinstance(i, int) and i == TILES - 1

        @block.sync
        def _(sp):
            sp.dma_start(xt[:, :], x_view[0]).then_inc(x_in, 16)

            def store_x1(i):
                sp.wait_ge(x1_ready, i + 1)
                sp.dma_start(d["x1_keep"][i], y[:, :]).then_inc(x1_out, 16)

            def body(i):
                if not final_tile(i):
                    sp.wait_ge(h_ready, i + 1)
                    sp.dma_start(xt[:, :], x_view[i + 1]).then_inc(x_in, 16)
                if not first(i):
                    sp.wait_ge(res_done, i)
                sp.dma_start(xr[:, :], x_view[i]).then_inc(xr_in, 16)
                if not first(i):
                    store_x1(i - 1)
            over_tiles(sp, body)
            store_x1(TILES - 1)
            sp.wait_ge(x1_out, 16 * TILES)

        @block.gpsimd
        def _(pool):
            nc.gpsimd.memset(kT[:, 0, :], 0.0).then_inc(zeroed, 1)
            nc.gpsimd.memset(v[:, 0, :], 0.0).then_inc(zeroed, 1)
            nc.gpsimd.memset(pin[:, 0, :], 0.0).then_inc(zeroed, 1)
            nc.gpsimd.memset(power[:, :], -0.5).then_inc(zeroed, 1)
            chain = Chain(pool, pool_chain)

            def make_h(i):
                pool.wait_ge(x_in, 16 * i + 16)
                if at_least(i, 1):
                    pool.wait_ge(h_turned, i)
                chain.link(nc.gpsimd.tensor_tensor(h[:, :], xt[:, :], mod[:, 1, :], ALU.mult))
                nc.gpsimd.tensor_tensor(h[:, :], h[:, :], mod[:, 0, :], ALU.add).then_inc(h_ready, 1)
                chain.clear()

            def make_h2(i):
                pool.wait_ge(var_ready, i + 1)
                nc.gpsimd.tensor_tensor(rstd[:, 0:1], rstd[:, 1:2], power[:, :], ALU.pow).then_inc(rstd_ready, 1)
                if at_least(i, 1):
                    pool.wait_ge(h2_turned, i)
                pool.wait_ge(x1_ready, i + 1)
                chain.link(nc.gpsimd.tensor_tensor(h2[:, :], y[:, :], mod[:, 4, :], ALU.mult))
                nc.gpsimd.tensor_tensor(h2[:, :], h2[:, :], mod[:, 3, :], ALU.add).then_inc(h2_ready, 1)
                chain.clear()

            def body(i):
                if not final_tile(i):
                    make_h(i + 1)
                if not first(i):
                    make_h2(i - 1)
            make_h(0)
            over_tiles(pool, body)
            make_h2(TILES - 1)

        @block.scalar
        def _(act):
            for dst, name in ((ln_g, "ln1_g"), (ln_b, "ln1_b")):
                act.dma_start(dst[:, :], d[name].to_broadcast([P, D])).then_inc(w_ready, 16)
            act.dma_start(sink[:, :], d["attn_sinks"].to_broadcast([P, HEADS])).then_inc(w_ready, 16)
            act.dma_start(w_pool[:, :, :], d["w_pool"].rearrange("a g p n -> (a p) g n")).then_inc(w_ready, 16)

            def take_hT(i):
                act.wait_ge(h_turned, i + 1)
                nc.scalar.activation(hT[:, :, :], ps_t[:, :].rearrange("p (j t) -> p j t", t=P), ACT.Copy).then_inc(hT_ready, 1)

            def take_values(i):
                act.wait_ge(proj_done, i + 1)
                nc.scalar.activation(pin[:, 1, :], ps_p[:, 2 * NB:3 * NB], ACT.Copy)
                act.wait_ge(rope_done, i + 1)
                nc.scalar.activation(v[:, 1, :], ps_p[:, QW + KVW:QW + 2 * KVW], ACT.Copy).then_inc(vp_ready, 1)

            def take_h2T(i):
                act.wait_ge(h2_turned, i + 1)
                nc.scalar.activation(h2T[:, :, bass.ds(i * P, P)], ps_t[:, :].rearrange("p (j t) -> p j t", t=P), ACT.Copy).then_inc(h2T_ready, 1)

            def body(i):
                act.wait_ge(qk_turned, i + 1)
                nc.scalar.activation(qT[:, :, :], ps_t[:, 0:4 * P].rearrange("p (j t) -> p j t", t=P), ACT.Copy)
                nc.scalar.activation(kT[:, 1, :], ps_t[:, 4 * P:5 * P], ACT.Copy).then_inc(qkT_ready, 1)
                act.wait_ge(pooled_done, i + 1)
                nc.scalar.activation(pooledT[:, :], ps_o[:, :], ACT.Copy).then_inc(pooledT_ready, 1)
                if not final_tile(i):
                    take_hT(i + 1)
                for r in range(2):
                    act.wait_ge(negm_ready, 2 * i + r + 1)
                    for n in range(4):
                        hd = 4 * r + n
                        nc.scalar.activation(s[:, r, n, :], s[:, r, n, :], ACT.Exp, bias=small[:, 1, hd:hd + 1],
                                             accum_out=small[:, 2, hd:hd + 1])
                    last = nc.scalar.activation(small[:, 3, 4 * r:4 * r + 4], small[:, 3, 4 * r:4 * r + 4], ACT.Exp)
                    last.then_inc(exp_done, 1)
                for r in range(2):
                    act.wait_ge(exp_done, 2 * i + r + 1)
                    act.wait_ge(rden_ready, 2 * i + r + 1)
                    for n in range(4):
                        hd = 4 * r + n
                        last = nc.scalar.activation(s[:, r, n, :], s[:, r, n, :], ACT.Copy, scale=small[:, 4, hd:hd + 1])
                    last.then_inc(probs_ready, 1)
                for r in range(2):
                    for f in range(2):
                        n = 4 * i + 2 * r + f
                        act.wait_ge(pT_done, n + 1)
                        if r or not first(i):
                            act.wait_ge(pv_done, n - 1)
                        nc.scalar.activation(pT[:, 4 * f:4 * f + 4, :], ps_t[:, f * NB:(f + 1) * NB].rearrange("p (j t) -> p j t", t=P),
                                             ACT.Copy).then_inc(pT_ready, 1)
                act.wait_ge(pv_done, 4 * i + 4)
                nc.scalar.activation(mixT[:, 0:4, :], ps_o[:, :].rearrange("p (j t) -> p j t", t=P), ACT.Copy).then_inc(mixa_ready, 1)
                if not first(i):
                    take_h2T(i - 1)
                if not final_tile(i):
                    nc.scalar.activation(kT[:, 0, :], kT[:, 1, :], ACT.Copy)
                    nc.scalar.activation(v[:, 0, :], v[:, 1, :], ACT.Copy)
                    nc.scalar.activation(pin[:, 0, :], pin[:, 1, :], ACT.Copy).then_inc(moved, 1)
                    act.wait_ge(moved, i + 1)
                    take_values(i + 1)
            moved = ctx.enter_context(nc.semaphore("block_moved"))
            take_hT(0)
            take_values(0)
            over_tiles(act, body)
            take_h2T(TILES - 1)

        @block.tensor
        def _(pe):
            pe.wait_ge(zeroed, 4)
            pe.wait_ge(keep["mix_in"], 16 * (1 + 2 * DC))
            pe.wait_ge(w_ready, 64)

            def turn_h(i):
                pe.wait_ge(h_ready, i + 1)
                if at_least(i, 1):
                    pe.wait_ge(qkT_ready, i)
                for j in range(DC):
                    last = nc.tensor.transpose(ps_t[:, j * P:(j + 1) * P], h[:, j * P:(j + 1) * P], ident)
                last.then_inc(h_turned, 1)

            def project(i):
                if at_least(i, 1):
                    pe.wait_ge(vp_ready, i)
                pe.wait_ge(hT_ready, i + 1)
                for at, src, width in ((0, 0, QW), (QW, QW, 2 * KVW), (2 * NB, QW + 2 * KVW, PW)):
                    for j in range(DC):
                        last = nc.tensor.matmul(ps_p[:, at:at + width], hT[:, j, :], w_in[:, j, src:src + width],
                                                start=(j == 0), stop=(j == DC - 1))
                last.then_inc(proj_done, 1)

            def turn_h2(i):
                pe.wait_ge(h2_ready, i + 1)
                if at_least(i, 1):
                    pe.wait_ge(h2T_ready, i)
                for j in range(DC):
                    last = nc.tensor.transpose(ps_t[:, j * P:(j + 1) * P], h2[:, j * P:(j + 1) * P], ident)
                last.then_inc(h2_turned, 1)

            def body(i):
                pe.wait_ge(rope_done, i + 1)
                if at_least(i, 2):
                    pe.wait_ge(h2T_ready, i - 1)
                elif i == 1:
                    pe.wait_ge(pT_ready, 4)
                for j in range(4):
                    nc.tensor.transpose(ps_t[:, j * P:(j + 1) * P], qk[:, j * P:(j + 1) * P], ident)
                nc.tensor.transpose(ps_t[:, 4 * P:5 * P], qk[:, QW:QW + KVW], ident).then_inc(qk_turned, 1)
                pe.wait_ge(vp_ready, i + 1)
                for g in range(PG):
                    own = M_BAND + (3 * g + (0 if first(i) else 1)) * P
                    prev = M_BAND + (3 * g + 2) * P
                    out = ps_o[:, g * P:(g + 1) * P]
                    nc.tensor.matmul(out, pin[:, 1, g * P:(g + 1) * P], mix_const[:, own:own + P], start=True, stop=False)
                    last = nc.tensor.matmul(out, pin[:, 0, g * P:(g + 1) * P], mix_const[:, prev:prev + P], start=False, stop=True)
                last.then_inc(pooled_done, 1)
                pe.wait_ge(qkT_ready, i + 1)
                if not final_tile(i):
                    turn_h(i + 1)
                if not first(i):
                    pe.wait_ge(out_taken, i)

                def score_round(r):
                    for n in range(4):
                        last = nc.tensor.matmul(ps_s[:, n * 2 * P:(n + 1) * 2 * P], qT[HD * r:HD * r + HD, n, :],
                                                kT[HD * r:HD * r + HD, :, :], start=True, stop=True)
                    last.then_inc(scores_done, 1)

                score_round(0)
                pe.wait_ge(pooledT_ready, i + 1)
                for g in range(PG):
                    last = nc.tensor.matmul(ps_o[:, g * P:(g + 1) * P], w_pool[:, g, :],
                                            pooledT[:, g * P:(g + 1) * P], start=True, stop=True)
                last.then_inc(y_done, 1)
                pe.wait_ge(s_ready, 2 * i + 1)
                score_round(1)
                if not final_tile(i):
                    project(i + 1)

                def turn_probs(r, f):
                    if f == 0:
                        pe.wait_ge(probs_ready, 2 * i + r + 1)
                    for n in range(4 * f, 4 * f + 4):
                        last = nc.tensor.transpose(ps_t[:, n * P:(n + 1) * P], s[:, r, n // 2, (n % 2) * P:(n % 2 + 1) * P], ident)
                    last.then_inc(pT_done, 1)

                def mix_values(r, f):
                    pe.wait_ge(pT_ready, 4 * i + 2 * r + f + 1)
                    for n in range(2 * f, 2 * f + 2):
                        hd = 4 * r + n
                        at = HD * (hd % 2)
                        out = ps_o[at:at + HD, (hd // 2) * P:(hd // 2 + 1) * P]
                        for k in range(2):
                            last = nc.tensor.matmul(out, v[:, k, r * HD:(r + 1) * HD], pT[:, 2 * n + k, :],
                                                    start=(k == 0), stop=(k == 1))
                    last.then_inc(pv_done, 1)

                turn_probs(0, 0)
                turn_probs(0, 1)
                pe.wait_ge(mixb_ready, i + 1)
                mix_values(0, 0)
                turn_probs(1, 0)
                mix_values(0, 1)
                turn_probs(1, 1)
                mix_values(1, 0)
                mix_values(1, 1)
                if not first(i):
                    turn_h2(i - 1)
                pe.wait_ge(mixa_ready, i + 1)
                for half in range(2):
                    for j in range(DC):
                        last = nc.tensor.matmul(ps_s[:, half * NB:(half + 1) * NB], mixT[:, j, :],
                                                w_out[:, j, half * NB:(half + 1) * NB], start=(j == 0), stop=(j == DC - 1))
                last.then_inc(out_done, 1)
            turn_h(0)
            project(0)
            over_tiles(pe, body)
            turn_h2(TILES - 1)

        @block.vector
        def _(dve):
            chain = Chain(dve, dve_chain)
            V = nc.vector
            dve.wait_ge(w_ready, 64)
            dve.wait_ge(keep["mix_in"], 16 * (1 + 2 * DC))

            def rope(i):
                dve.wait_ge(proj_done, i + 1)
                src = ps_p[:, 0:10 * HD].rearrange("p (n a c) -> p n a c", a=2, c=HALF)
                cos = mix_const[:, bass.ds(i * HALF + M_COS, HALF)]
                sin = mix_const[:, bass.ds(i * HALF + M_SIN, HALF)]
                ra = rot_a[:, :].rearrange("p (n a c) -> p n a c", a=2, c=HALF)
                rb = rot_b[:, :].rearrange("p (n a c) -> p n a c", a=2, c=HALF)
                qk4 = qk[:, :].rearrange("p (n a c) -> p n a c", a=2, c=HALF)
                for a in range(2):
                    V.tensor_tensor(ra[:, :, a, :], src[:, :, a, :], cos.unsqueeze(1).to_broadcast([P, 10, HALF]), ALU.mult)
                    last = V.tensor_tensor(rb[:, :, a, :], src[:, :, 1 - a, :], sin.unsqueeze(1).to_broadcast([P, 10, HALF]), ALU.mult)
                chain.link(last)
                for a, op in ((0, ALU.subtract), (1, ALU.add)):
                    by_pair = lambda t: t[:, 0:HEADS, a, :].rearrange("p (g j) c -> p g j c", g=2)
                    V.tensor_tensor(qk4[:, 0:HEADS, a, :].rearrange("p (j g) c -> p g j c", g=2), by_pair(ra), by_pair(rb), op)
                    last = V.tensor_tensor(qk4[:, HEADS:, a, :], ra[:, HEADS:, a, :], rb[:, HEADS:, a, :], op)
                last.then_inc(rope_done, 1)

            def scores_and_max(i, r):
                hs = slice(4 * r, 4 * r + 4)
                dve.wait_ge(scores_done, 2 * i + r + 1)
                mask = mix_const[:, M_MASK:M_MASK + 2 * P] if first(i) else mix_const[:, M_MASK + 2 * P:M_MASK + 4 * P]
                V.scalar_tensor_tensor(s[:, r, :, :], ps_s[:, :].rearrange("p (n k) -> p n k", n=4), HD ** -0.5,
                                       mask.unsqueeze(1).to_broadcast([P, 4, 2 * P]), ALU.mult, ALU.add).then_inc(s_ready, 1)
                dve.wait_ge(s_ready, 2 * i + r + 1)
                chain.link(V.tensor_reduce(small[:, 0, hs], s[:, r, :, :], AX.X, ALU.max))
                chain.link(V.tensor_tensor(small[:, 0, hs], small[:, 0, hs], sink[:, hs], ALU.max))
                V.tensor_tensor(small[:, 3, hs], sink[:, hs], small[:, 0, hs], ALU.subtract)
                V.tensor_scalar(small[:, 1, hs], small[:, 0, hs], -1.0, None, ALU.mult).then_inc(negm_ready, 1)

            def denominators(i, r):
                hs = slice(4 * r, 4 * r + 4)
                dve.wait_ge(exp_done, 2 * i + r + 1)
                chain.link(V.tensor_tensor(small[:, 0, hs], small[:, 2, hs], small[:, 3, hs], ALU.add))
                V.reciprocal(small[:, 4, hs], small[:, 0, hs]).then_inc(rden_ready, 1)

            def norm_stats(i):
                dve.wait_ge(res_done, i + 1)
                V.bn_stats(stats[:, 0, :], y[:, 0:NB])
                chain.link(V.bn_stats(stats[:, 1, :], y[:, NB:D]))
                chain.link(V.bn_aggr(mv[:, :], stats[:, :, :]))
                V.tensor_scalar_add(rstd[:, 1:2], mv[:, 1:2], EPS).then_inc(var_ready, 1)
                chain.step(V.scalar_tensor_tensor(y[:, :], y[:, :], mv[:, 0:1], ln_g[:, :], ALU.subtract, ALU.mult))

            def norm_apply(i):
                chain.wait()
                dve.wait_ge(rstd_ready, i + 1)
                V.scalar_tensor_tensor(y[:, :], y[:, :], rstd[:, 0:1], ln_b[:, :], ALU.mult, ALU.add).then_inc(x1_ready, 1)

            def residual(i):
                dve.wait_ge(out_done, i + 1)
                if at_least(i, 1):
                    dve.wait_ge(x1_out, 16 * i)
                V.tensor_tensor(y[:, :], ps_s[:, :], mod[:, 2, :], ALU.mult).then_inc(out_taken, 1)
                dve.wait_ge(out_taken, i + 1)
                dve.wait_ge(xr_in, 16 * i + 16)
                V.scalar_tensor_tensor(y[:, :], xr[:, :], ALPHA, y[:, :], ALU.mult, ALU.add).then_inc(res_done, 1)

            def body(i):
                scores_and_max(i, 0)
                scores_and_max(i, 1)
                dve.wait_ge(y_done, i + 1)
                V.tensor_tensor(mixT[:, 4:8, :], ps_o[:, :].rearrange("p (g t) -> p g t", g=PG),
                                keep["pool_col"][:, :].unsqueeze(2).to_broadcast([P, PG, P]), ALU.mult).then_inc(mixb_ready, 1)
                if not first(i):
                    norm_stats(i - 1)
                denominators(i, 0)
                denominators(i, 1)
                if not first(i):
                    norm_apply(i - 1)
                if not final_tile(i):
                    rope(i + 1)
                residual(i)
                chain.clear()
            rope(0)
            over_tiles(dve, body)
            norm_stats(TILES - 1)
            norm_apply(TILES - 1)


def in_pairs(eng, count, body, straight=1):
    for n in range(2 * straight):
        body(n, n % 2)
    with eng.Fori(straight, count // 2 - 1) as m:
        body(2 * m, 0)
        body(2 * m + 1, 1)
    body(count - 2, 0)
    body(count - 1, 1)


def at_least(n, k):
    return not isinstance(n, int) or n >= k


def one(view, n):
    if isinstance(n, int):
        return view[:, n]
    return view[:, bass.ds(n, 1)].rearrange("p m j n -> p (m j) n")


def queries(nc, d, keep):
    with ExitStack() as ctx:
        sb = lambda n, s, t=F32: ctx.enter_context(nc.sbuf_tensor(n, s, t))
        sem = lambda n: ctx.enter_context(nc.semaphore(n))
        ps = lambda n, w: ctx.enter_context(nc.psum_tensor(n, [P, w], F32))
        const, h2T, h_part = keep["const"], keep["h2T"], (keep["h_hi"], keep["h_lo"])
        ident = const[:, C_IDENT:C_IDENT + P]
        k_rows, keysT = sb("key_rows", [P, 2, P]), sb("keysT", [P, 2, P])
        w_raw = sb("wq_raw", [P, 2, DC, P])
        w_part = (sb("wq_hi", [P, 2, DC, P], F32R), sb("wq_lo", [P, 2, DC, P], F32R))
        qT = sb("queriesT", [P, 2, SEQ])
        score = sb("score_rows", [P, 2, TILES, P])
        ps_q = [ps(f"ps_q{e}", 2 * NB) for e in range(2)]
        ps_s = [ps(f"ps_s{e}", 2 * NB) for e in range(2)]
        keys_in, keys_turned, keysT_ready = sem("keys_in"), sem("keys_turned"), sem("keysT_ready")
        hi_ready, lo_ready = sem("h2_hi_ready"), sem("h2_lo_ready")
        w_in = [sem(f"wq_in{e}") for e in range(2)]
        whi_ready, wlo_ready = sem("wq_hi_ready"), sem("wq_lo_ready")
        q_done, qT_ready, s_done, s_ready = sem("q_done"), sem("qT_ready"), sem("s_done"), sem("s_rows_ready")
        stored = [sem(f"scores_stored{e}") for e in range(2)]
        block = ctx.enter_context(nc.Block())
        w_view = d["w_pq"].rearrange("a (j p) (m n) -> (a p) m j n", p=P, n=P)
        s_view = d["scores_keep"].rearrange("t p (m k) -> p m t k", k=KEYS)

        @block.sync
        def _(sp):
            def body(n, e):
                if at_least(n, 2):
                    sp.wait_ge(wlo_ready, n - 1)
                sp.dma_start(w_raw[:, e, :, :], one(w_view, n)).then_inc(w_in[e], 16)
                if not at_least(n, 1):
                    sp.dma_start(k_rows[:, 0, :], d["peer_k1"].rearrange("a k c -> (a k) c")).then_inc(keys_in, 16)
                    sp.dma_start(k_rows[:, 1, :], d["peer_k2"].rearrange("a k c -> (a k) c")).then_inc(keys_in, 16)
            in_pairs(sp, NQ, body)
            for e in range(2):
                u_view = d["peer_u"].rearrange("a (k1 k2) n -> (a k1) k2 n", k2=KEYS)
                sp.dma_start(keep["raw_rows"][:, e, :], one2(u_view, e)).then_inc(keep["u_in"][e], 16)

        @block.gpsimd
        def _(pool):
            def body(n, e):
                pool.wait_ge(s_ready, n + 1)
                pool.wait_ge(keys_in, 32)
                pool.dma_start(one(s_view, n), score[:, e, :, :]).then_inc(stored[e], 16)
            in_pairs(pool, NQ, body)
            for e in range(2):
                pool.wait_ge(stored[e], 16 * PEER_HEADS)

        @block.scalar
        def _(act):
            def w_hi(n, e):
                act.wait_ge(w_in[e], 8 * (n - e) + 16)
                if at_least(n, 2):
                    act.wait_ge(q_done, n - 1)
                nc.scalar.activation(w_part[0][:, e, :, :], w_raw[:, e, :, :], ACT.Copy).then_inc(whi_ready, 1)

            def body(n, e):
                if not isinstance(n, int) or n < NQ - 1:
                    w_hi(n + 1, 1 - e)
                if not at_least(n, 1):
                    act.wait_ge(keys_turned, 1)
                    nc.scalar.activation(keysT[:, :, :], ps_s[0][:, 0:2 * P].rearrange("p (a k) -> p a k", a=2), ACT.Copy).then_inc(keysT_ready, 1)
                act.wait_ge(q_done, n + 1)
                if at_least(n, 2):
                    act.wait_ge(s_done, n - 1)
                nc.scalar.activation(qT[:, e, :], ps_q[e][:, :], ACT.Copy).then_inc(qT_ready, 1)

            for j in range(DC):
                nc.scalar.activation(h_part[0][:, j, :], h2T[:, j, :], ACT.Copy).then_inc(hi_ready, 1)
                if j == 1:
                    w_hi(0, 0)
            in_pairs(act, NQ, body)

        @block.tensor
        def _(pe):
            def key_scores(n, e):
                pe.wait_ge(qT_ready, n + 1)
                if at_least(n, 2):
                    pe.wait_ge(s_ready, n - 1)
                for t in range(TILES):
                    last = nc.tensor.matmul(ps_s[e][:, t * P:(t + 1) * P], qT[:, e, t * P:(t + 1) * P], keysT[:, e, :], start=True, stop=True)
                last.then_inc(s_done, 1)

            def body(n, e):
                pe.wait_ge(whi_ready, n + 1)
                pe.wait_ge(wlo_ready, n + 1)
                if at_least(n, 2):
                    pe.wait_ge(qT_ready, n - 1)
                if not at_least(n, 1):
                    for j in range(DC):
                        pe.wait_ge(hi_ready, j + 1)
                        pe.wait_ge(lo_ready, j + 1)
                        for half in range(2):
                            for a, b in ((0, 0), (1, 0), (0, 1)):
                                last = nc.tensor.matmul(ps_q[e][:, half * NB:(half + 1) * NB], w_part[a][:, e, j, :],
                                                        h_part[b][:, j, half * NB:(half + 1) * NB],
                                                        start=(j + a + b == 0), stop=(j == DC - 1 and b == 1))
                    last.then_inc(q_done, 1)
                    pe.wait_ge(keys_in, 32)
                    for a in range(2):
                        last = nc.tensor.transpose(ps_s[0][:, a * P:(a + 1) * P], k_rows[:, a, :], ident)
                    last.then_inc(keys_turned, 1)
                    return
                for half in range(2):
                    k = 0
                    for a, b in ((0, 0), (1, 0), (0, 1)):
                        for j in range(DC):
                            last = nc.tensor.matmul(ps_q[e][:, half * NB:(half + 1) * NB], w_part[a][:, e, j, :],
                                                    h_part[b][:, j, half * NB:(half + 1) * NB], start=(k == 0), stop=(k == 3 * DC - 1))
                            k += 1
                last.then_inc(q_done, 1)
                if not at_least(n, 2):
                    pe.wait_ge(keysT_ready, 1)
                key_scores(n - 1, 1 - e)
            in_pairs(pe, NQ, body)
            key_scores(NQ - 1, 1)

        @block.vector
        def _(dve):
            V = nc.vector

            def w_lo(n, e):
                dve.wait_ge(whi_ready, n + 1)
                if at_least(n, 2):
                    dve.wait_ge(q_done, n - 1)
                V.tensor_tensor(w_part[1][:, e, :, :], w_raw[:, e, :, :], w_part[0][:, e, :, :].bitcast(F32), ALU.subtract).then_inc(wlo_ready, 1)

            def rows_out(n, e):
                dve.wait_ge(s_done, n + 1)
                if at_least(n, 2):
                    dve.wait_ge(stored[e], 8 * (n - e))
                V.tensor_copy(score[:, e, :, :], ps_s[e][:, :].rearrange("p (t k) -> p t k", k=P)).then_inc(s_ready, 1)

            def body(n, e):
                if not isinstance(n, int) or n < NQ - 1:
                    w_lo(n + 1, 1 - e)
                if at_least(n, 1):
                    rows_out(n - 1, 1 - e)

            for j in range(DC):
                dve.wait_ge(hi_ready, j + 1)
                V.tensor_tensor(h_part[1][:, j, :], h2T[:, j, :], h_part[0][:, j, :].bitcast(F32), ALU.subtract).then_inc(lo_ready, 1)
                if j == 1:
                    w_lo(0, 0)
            in_pairs(dve, NQ, body, straight=2)
            rows_out(NQ - 1, 1)


def routing(nc, d, keep):
    UNIT = 4
    FILLS = 2
    UNITS = P // UNIT
    TILE_STEPS = KEYS // TILES
    HEAD_STEPS = TILE_STEPS // 2 - 2
    LAST_STEPS = TILE_STEPS // 2
    CLOSE_STEPS = TILE_STEPS - HEAD_STEPS - LAST_STEPS
    with ExitStack() as ctx:
        sb = lambda n, s, t=F32: ctx.enter_context(nc.sbuf_tensor(n, s, t))
        sem = lambda n: ctx.enter_context(nc.semaphore(n))
        ps = lambda n, w: ctx.enter_context(nc.psum_tensor(n, [P, w], F32))
        const, h_part = keep["const"], (keep["h_hi"], keep["h_lo"])
        ident = const[:, C_IDENT:C_IDENT + P]
        iota = const[:, C_IOTA:C_IOTA + P]
        sc = sb("score_tile", [P, NQ, P])
        gates = [keep["h2T"][:, :, :].rearrange("p j n -> p (j n)").rearrange("p (k t) -> p k t", t=HALF_T),
                 sb("gates1", [P, KEYS, HALF_T])[:, :, :]]
        vals = sb("vals", [P, NQ, TOPK])
        idx_u = sb("idx_u", [P, NQ, TOPK], U32)
        idx = sb("idx", [P, NQ, TOPK], BF16)
        rest = sb("rest", [P, NQ, P])
        wide = sb("wide", [P, PEER_HEADS * TOPK * TOPK], BF16)
        cand = wide[:, 0:2 * PEER_HEADS * CAND].bitcast(F32).rearrange("p (h n) -> p h n", h=PEER_HEADS)
        cand_rest = rest[:, 0:PEER_HEADS, 0:CAND]
        top = sb("top", [P, PEER_HEADS, TOPK])
        pos_u = idx_u[:, 0:PEER_HEADS, :]
        pos = sb("pos", [P, PEER_HEADS, TOPK], BF16)
        col = sb("col", [P, PEER_HEADS, TOPK], BF16)
        starts = sb("starts", [P, 2 * NTH + TOPK], BF16)
        step1 = sb("step1", [P, PEER_HEADS, NTH], BF16)
        past = wide[:, :].rearrange("p (h k r) -> p h k r", h=PEER_HEADS, k=TOPK)
        prod = rest[:, PEER_HEADS:NQ, :].rearrange("p n k -> p (n k)").bitcast(BF16).rearrange(
            "p (h k r) -> p h k r", h=PEER_HEADS, k=TOPK)
        red = sb("red", [P, PEER_HEADS, TOPK])
        route = sb("route", [P, 3, P])
        stand = sb("stand", [P, 1])
        gsum = sb("gsum", [P, 2, PEER_HEADS])
        routeT = sb("routeT", [P, 3, P])
        gate_part = (sb("gate_hi", [P, P], F32R), sb("gate_lo", [P, P]))
        hot1 = sb("hot1", [P, 2, UNIT, P], F32R)
        hot2 = sb("hot2_gated", [P, 2, UNIT, 2, P], F32R)
        off = sb("key_offset", [P, 2, 2, UNIT, P], BF16)
        same = sb("same_key", [P, 2, UNIT, P], BF16)
        u_raw = keep["raw_rows"]
        uT = (sb("uT_hi", [P, 2, DC, P], F32R), sb("uT_lo", [P, 2, DC, P], F32R))
        hid = sb("hid", [P, 2, SEQ])
        ps_u, ps_g = ps("ps_u", 2 * NB), ps("ps_gate", 2 * NB)
        ps_h = [ps(f"ps_h{e}", 2 * NB) for e in range(2)]

        scores_in, s_used = sem("scores_in"), sem("s_used")
        top_done, exp_done, route_ready, route_turned, routeT_ready = (
            sem("top_done"), sem("gate_exp_done"), sem("route_ready"), sem("route_turned"), sem("routeT_ready"))
        off_ready, same_ready, lo_hot_ready = sem("off_ready"), sem("same_ready"), sem("lo_hot_ready")
        hot_ready, gate_done, gate_out = sem("hot_ready"), sem("gate_done"), sem("gate_out")
        stored = [sem("gates_stored0"), sem("gates_stored1")]
        starts_ready = sem("starts_ready")
        u_in = keep["u_in"]
        u_turned, uhi_ready, ulo_ready = sem("u_turned"), sem("uhi_ready"), sem("ulo_ready")
        hid_done, gelu_done = sem("hid_done"), sem("gelu_done")
        hid_stored = [sem(f"hid_stored{b}") for b in range(2)]
        dve_chain = sem("dve_chain2")
        block = ctx.enter_context(nc.Block())
        u_view = d["peer_u"].rearrange("a (k1 k2) n -> (a k1) k2 n", k2=KEYS)
        hid_view = d["hid_keep"].rearrange("k2 p t -> p k2 t")

        def over_rounds(eng, pair, end=None):
            for c in range(HEAD_STEPS // 2):
                pair(0, c, 2 * c, None, 0, 0)
            if end:
                end(0)

            def middle(i):
                for c in range(TILE_STEPS // 2):
                    pair(i, c, HEAD_STEPS + TILE_STEPS * (i - 1) + 2 * c, i - 1, UNITS // TILE_STEPS, 2 * c * (UNITS // TILE_STEPS))
            middle(1)
            with eng.Fori(2, TILES - 1) as i:
                middle(i)
            middle(TILES - 1)
            units = UNITS // LAST_STEPS
            for c in range((LAST_STEPS + CLOSE_STEPS) // 2):
                step = KEYS - LAST_STEPS - CLOSE_STEPS + 2 * c
                pair(TILES, c, step, TILES - 1, units if 2 * c < LAST_STEPS else 0, min(2 * c * units, UNITS))

        def has_next(step):
            return not isinstance(step, int) or step + 2 < KEYS

        def closes(i, c, e):
            return c == TILE_STEPS // 2 - 1 and e == 1

        def ahead(make, i, tile, unit):
            if unit < UNITS:
                make(tile, unit)
            elif not isinstance(i, int) or i < TILES:
                make(tile + 1, unit - UNITS)

        @block.sync
        def _(sp):
            def pair(i, c, step0, tile, units, unit0):
                for e in range(2):
                    step = step0 + e
                    if has_next(step):
                        sp.wait_ge(u_turned, step + 1)
                        sp.dma_start(u_raw[:, e, :], one2(u_view, step + 2)).then_inc(u_in[e], 16)
                    sp.wait_ge(gelu_done, step + 1)
                    sp.dma_start(one2(hid_view, step), hid[:, e, :]).then_inc(hid_stored[e], 16)
            over_rounds(sp, pair)
            sp.wait_ge(u_turned, KEYS)
            for e in range(2):
                load_v(sp, d, keep, e, e)
            for e in range(2):
                sp.wait_ge(hid_stored[e], 16 * KEYS // 2)
            for half in range(2):
                sp.wait_ge(stored[half], 16 * TILES)

        @block.gpsimd
        def _(pool):
            def load_scores(i):
                pool.dma_start(sc[:, :, :].rearrange("p n k -> p (n k)"), d["scores_keep"][i]).then_inc(scores_in, 16)

            def gate_unit(tile, unit):
                slot = unit % 2
                n = tile * UNITS + unit
                if at_least(n, 2):
                    pool.wait_ge(same_ready, n - 1)
                pool.wait_ge(routeT_ready, tile + 1)
                tok = slice(unit * UNIT, (unit + 1) * UNIT)
                for a in range(2):
                    last = nc.gpsimd.tensor_tensor(off[:, slot, a, :, :], iota.unsqueeze(1).to_broadcast([P, UNIT, P]),
                                                   routeT[:, a, tok].unsqueeze(2).to_broadcast([P, UNIT, P]), ALU.subtract)
                last.then_inc(off_ready, 1)

            def pair(i, c, step0, tile, units, unit0):
                if c == 2 and not (isinstance(i, int) and i >= TILES - 1):
                    pool.wait_ge(s_used, i + 1)
                    pool.wait_ge(scores_in, 16 * i + 16)
                    load_scores(i + 1)
                for k in range(2 * units):
                    gate_unit(tile, unit0 + k)
            load_scores(0)
            over_rounds(pool, pair)

        @block.scalar
        def _(act):
            def u_hi(e, step):
                act.wait_ge(u_turned, step + 1)
                nc.scalar.activation(uT[0][:, e, :, :], ps_u[:, :].rearrange("p (j k) -> p j k", k=P), ACT.Copy).then_inc(uhi_ready, 1)

            def lo_rows(tile, unit):
                slot = unit % 2
                act.wait_ge(same_ready, tile * UNITS + unit + 1)
                for t in range(UNIT):
                    tok = slice(unit * UNIT + t, unit * UNIT + t + 1)
                    last = nc.scalar.activation(hot2[:, slot, t, 1, :], same[:, slot, t, :], ACT.Copy, scale=gate_part[1][:, tok])
                last.then_inc(lo_hot_ready, 1)

            def pair(i, c, step0, tile, units, unit0):
                if tile is not None and isinstance(tile, int) and tile + c == 0:
                    lo_rows(0, 0)
                    lo_rows(0, 1)
                for e in range(2):
                    step = step0 + e
                    unit = unit0 + e * units
                    closing = closes(i, c, e)
                    early = 0 if closing else max(units - 1, 0)
                    for k in range(early):
                        ahead(lo_rows, i, tile, unit + k + 2)
                    if closing:
                        take_routes(i)
                    act.wait_ge(hid_done, step + 1)
                    if at_least(step, 2):
                        act.wait_ge(hid_stored[e], 8 * (step - e))
                    nc.scalar.activation(hid[:, e, :], ps_h[e][:, :], ACT.Gelu).then_inc(gelu_done, 1)
                    if has_next(step):
                        u_hi(e, step + 2)
                    for k in range(early, units):
                        ahead(lo_rows, i, tile, unit + k + 2)
                    done = unit + units
                    if units and done % (UNITS // 2) == 0:
                        half = done // (UNITS // 2) - 1
                        act.wait_ge(gate_out, FILLS * (tile * UNITS + done))
                        act.dma_start(d["gates_keep"][2 * tile + half], gates[half].rearrange("p k t -> p (k t)")).then_inc(stored[half], 16)
                if c == (1 if tile is None else 3) and not (isinstance(i, int) and i == TILES):
                    act.wait_ge(top_done, i + 1)
                    nc.scalar.activation(red[:, :, :], red[:, :, :], ACT.Exp).then_inc(exp_done, 1)

            def take_routes(i):
                act.wait_ge(route_turned, i + 1)
                nc.scalar.activation(routeT[:, :, :], ps_g[:, 0:3 * P].rearrange("p (n t) -> p n t", t=P), ACT.Copy).then_inc(routeT_ready, 1)

            for e in range(2):
                u_hi(e, e)
            over_rounds(act, pair, take_routes)

        @block.tensor
        def _(pe):
            def turn(e, step):
                pe.wait_ge(u_in[e], 8 * (step - e) + 16)
                if at_least(step, 1):
                    pe.wait_ge(ulo_ready, step)
                for j in range(DC):
                    last = nc.tensor.transpose(ps_u[:, j * P:(j + 1) * P], u_raw[:, e, j * P:(j + 1) * P], ident)
                last.then_inc(u_turned, 1)

            def hidden(e, step, quarter):
                half = quarter // 2
                if quarter == 0:
                    pe.wait_ge(ulo_ready, step + 1)
                    if at_least(step, 2):
                        pe.wait_ge(gelu_done, step - 1)
                products = [(a, b, j) for a, b in ((0, 0), (0, 1), (1, 0)) for j in range(DC)]
                for n in range(quarter % 2 * len(products) // 2, (quarter % 2 + 1) * len(products) // 2):
                    a, b, j = products[n]
                    last = nc.tensor.matmul(ps_h[e][:, half * NB:(half + 1) * NB], uT[a][:, e, j, :],
                                            h_part[b][:, j, half * NB:(half + 1) * NB],
                                            start=(n == 0), stop=(n == len(products) - 1))
                if quarter == 3:
                    last.then_inc(hid_done, 1)

            def gate_unit(tile, unit):
                slot = unit % 2
                n = tile * UNITS + unit
                pe.wait_ge(hot_ready, n + 1)
                pe.wait_ge(lo_hot_ready, n + 1)
                for t in range(UNIT):
                    if t % (UNIT // FILLS) == 0 and at_least(n, 1):
                        pe.wait_ge(gate_out, FILLS * (n - 1) + t // (UNIT // FILLS) + 1)
                    sums = ps_g[:, 2 * P * t:2 * P * (t + 1)]
                    last = nc.tensor.matmul(sums, hot1[:, slot, t, :], hot2[:, slot, t, :, :].rearrange("p a k -> p (a k)"),
                                            start=True, stop=True)
                    if (t + 1) % (UNIT // FILLS) == 0:
                        last.then_inc(gate_done, 1)

            def pair(i, c, step0, tile, units, unit0):
                for e in range(2):
                    for quarter in range(4):
                        hidden(e, step0 + e, quarter)
                        if quarter == 3 and has_next(step0 + e):
                            turn(e, step0 + e + 2)
                        if quarter == 2 and closes(i, c, e):
                            turn_routes(i)
                        if quarter == 3 and closes(i, c, e):
                            pe.wait_ge(routeT_ready, i + 1)
                        for k in range(units * quarter // 4, units * (quarter + 1) // 4):
                            gate_unit(tile, unit0 + e * units + k)

            def turn_routes(i):
                pe.wait_ge(route_ready, i + 1)
                if at_least(i, 1):
                    pe.wait_ge(gate_out, (i * UNITS - 1) * FILLS)
                for n in range(3):
                    last = nc.tensor.transpose(ps_g[:, n * P:(n + 1) * P], route[:, n, :], ident)
                last.then_inc(route_turned, 1)

            for e in range(2):
                turn(e, e)
            over_rounds(pe, pair, turn_routes)

        @block.vector
        def _(dve):
            V = nc.vector
            chain = Chain(dve, dve_chain)
            V.tensor_copy(starts[:, 0:2 * NTH], const[:, C_START:C_START + 2 * NTH]).then_inc(starts_ready, 1)
            V.tensor_copy(starts[:, 2 * NTH:2 * NTH + TOPK], const[:, C_IOTA:C_IOTA + TOPK]).then_inc(starts_ready, 1)
            dve.wait_ge(starts_ready, 2)
            th = starts[:, 0:NTH].unsqueeze(1).to_broadcast([P, P, NTH])
            dth = starts[:, NTH:2 * NTH].unsqueeze(1).to_broadcast([P, P, NTH])
            cols = starts[:, 2 * NTH:].unsqueeze(1).to_broadcast([P, P, TOPK])
            heads4 = [P, PEER_HEADS, TOPK, TOPK]
            pair_vals = vals[:, :, :].rearrange("p (h a) k -> p h a k", a=2)
            pidx = idx[:, :, :].rearrange("p (h a) k -> p h a k", a=2)
            flat = lambda t: t.rearrange("p h k -> p (h k)")
            deep = past[:, :, :, 0:NTH].rearrange("p h k r -> p (h k) r")
            pdeep = prod[:, :, :, 0:NTH]
            by_rank = lambda n: route[:, n, :].rearrange("p (h k) -> p h k", h=PEER_HEADS)
            r1, r2, rg = by_rank(0), by_rank(1), by_rank(2)
            ranks = [P, PEER_HEADS, TOPK]

            def first_max(i):
                dve.wait_ge(scores_in, 16 * i + 16)
                V.memset(stand[:, :], 0.0)
                for n in range(NQ):
                    last = V.max(vals[:, n, 0:8], sc[:, n, :])
                chain.step(last)

            def first_keys(i):
                chain.wait()
                for n in range(NQ // 2):
                    V.max_index(idx_u[:, n, 0:8], vals[:, n, 0:8], sc[:, n, :])
                    last = V.match_replace(rest[:, n, :], vals[:, n, 0:8], sc[:, n, :], LOWEST)
                chain.step(last)

            def more_first_keys(i):
                for n in range(NQ // 2, NQ):
                    V.max_index(idx_u[:, n, 0:8], vals[:, n, 0:8], sc[:, n, :])
                    last = V.match_replace(rest[:, n, :], vals[:, n, 0:8], sc[:, n, :], LOWEST)
                chain.step(last)

            def second_max(i):
                chain.wait()
                V.memset(stand[:, :], 0.0).then_inc(s_used, 1)
                for n in range(NQ):
                    last = V.max(vals[:, n, 8:16], rest[:, n, :])
                chain.step(last)

            def second_keys(i):
                chain.wait()
                for n in range(NQ):
                    last = V.max_index(idx_u[:, n, 8:16], vals[:, n, 8:16], rest[:, n, :])
                chain.step(last)

            def candidates(i):
                at = 0
                for a0, a1, w in RECTS:
                    m = (a1 - a0) * w
                    shape = [P, PEER_HEADS, a1 - a0, w]
                    last = V.tensor_tensor(cand[:, :, at:at + m].rearrange("p h (a b) -> p h a b", b=w),
                                           pair_vals[:, :, 0, a0:a1].unsqueeze(3).to_broadcast(shape),
                                           pair_vals[:, :, 1, 0:w].unsqueeze(2).to_broadcast(shape), ALU.add)
                    at += m
                chain.link(last)
                V.tensor_copy(idx[:, :, :], idx_u[:, :, :])
                for n in range(PEER_HEADS):
                    last = V.max(top[:, n, 0:8], cand[:, n, :])
                chain.step(last)

            def first_tops(i):
                chain.wait()
                for n in range(PEER_HEADS):
                    V.max_index(pos_u[:, n, 0:8], top[:, n, 0:8], cand[:, n, :])
                    last = V.match_replace(cand_rest[:, n, :], top[:, n, 0:8], cand[:, n, :], LOWEST)
                chain.link(last)
                for n in range(PEER_HEADS):
                    last = V.max(top[:, n, 8:16], cand_rest[:, n, :])
                chain.step(last)

            def tops(i):
                chain.wait()
                for n in range(PEER_HEADS):
                    last = V.max_index(pos_u[:, n, 8:16], top[:, n, 8:16], cand_rest[:, n, :])
                V.tensor_tensor(red[:, :, :], top[:, :, :], top[:, :, 0:1].to_broadcast(ranks), ALU.subtract).then_inc(top_done, 1)
                dve.wait_ge(top_done, i + 1)
                V.tensor_tensor(step1[:, :, :], pidx[:, :, 0, 1:TOPK], pidx[:, :, 0, 0:NTH], ALU.subtract)
                chain.step(V.tensor_copy(pos[:, :, :], pos_u[:, :, :]))

            def past_rows(i):
                chain.wait()
                chain.link(V.tensor_tensor(deep, flat(pos[:, :, :]).unsqueeze(2).to_broadcast([P, P, NTH]), th, ALU.is_ge))
                chain.step(V.tensor_tensor(pdeep, past[:, :, :, 0:NTH], step1[:, :, :].unsqueeze(2).to_broadcast([P, PEER_HEADS, TOPK, NTH]), ALU.mult))

            def rows(i):
                chain.wait()
                chain.link(V.tensor_reduce(r1, pdeep, AX.X, ALU.add))
                chain.step(V.tensor_tensor(pdeep.rearrange("p h k r -> p (h k) r"), deep, dth, ALU.mult))

            def row_starts(i):
                dve.wait_ge(exp_done, i + 1)
                V.tensor_reduce(gsum[:, 0, :], red[:, :, :], AX.X, ALU.add)
                chain.link(V.tensor_tensor(r1, r1, pidx[:, :, 0, 0:1].to_broadcast(ranks), ALU.add))
                V.reciprocal(gsum[:, 1, :], gsum[:, 0, :])
                chain.link(V.tensor_reduce(r2, pdeep, AX.X, ALU.add))
                V.tensor_tensor(rg, red[:, :, :], gsum[:, 1, :].unsqueeze(2).to_broadcast(ranks), ALU.mult)

            def columns(i):
                chain.link(V.tensor_tensor(col[:, :, :], pos[:, :, :], r2, ALU.subtract))
                chain.step(V.tensor_tensor(past[:, :, :, :].rearrange("p h k r -> p (h k) r"),
                                           flat(col[:, :, :]).unsqueeze(2).to_broadcast([P, P, TOPK]), cols, ALU.is_equal))

            def column_keys(i):
                chain.wait()
                chain.step(V.tensor_tensor(prod[:, :, :, :], past[:, :, :, :], pidx[:, :, 1, :].unsqueeze(2).to_broadcast(heads4), ALU.mult))

            def route_out(i):
                chain.wait()
                V.tensor_reduce(r2, prod[:, :, :, :], AX.X, ALU.add).then_inc(route_ready, 1)
                chain.clear()

            gate_scalar = (gate_part[0][:, :].bitcast(F32), gate_part[1][:, :])
            parts = (first_max, first_keys, more_first_keys, second_max, second_keys, candidates, first_tops, tops,
                     past_rows, rows, row_starts, columns, column_keys, route_out)

            def u_lo(e, step):
                dve.wait_ge(uhi_ready, step + 1)
                V.tensor_tensor(uT[1][:, e, :, :], ps_u[:, :].rearrange("p (j k) -> p j k", k=P), uT[0][:, e, :, :].bitcast(F32), ALU.subtract).then_inc(ulo_ready, 1)

            def hot_rows(tile, unit):
                slot = unit % 2
                n = tile * UNITS + unit
                dve.wait_ge(off_ready, n + 1)
                if at_least(n, 2):
                    dve.wait_ge(gate_done, FILLS * (n - 1))
                V.tensor_scalar(hot1[:, slot, :, :], off[:, slot, 0, :, :], 0.0, None, ALU.is_equal)
                V.tensor_scalar(same[:, slot, :, :], off[:, slot, 1, :, :], 0.0, None, ALU.is_equal).then_inc(same_ready, 1)
                dve.wait_ge(same_ready, n + 1)
                for t in range(UNIT):
                    tok = slice(unit * UNIT + t, unit * UNIT + t + 1)
                    last = V.tensor_scalar(hot2[:, slot, t, 0, :], same[:, slot, t, :], gate_scalar[0][:, tok], None, ALU.mult)
                last.then_inc(hot_ready, 1)

            def take_gates(tile, unit):
                half, n = unit // (UNITS // 2), tile * UNITS + unit
                if unit % (UNITS // 2) == 0 and at_least(tile, 1):
                    dve.wait_ge(stored[half], 16 * tile)
                for f in range(FILLS):
                    dve.wait_ge(gate_done, FILLS * n + f + 1)
                    at = (unit * UNIT + f * UNIT // FILLS) % HALF_T
                    sums = ps_g[:, f * NB:(f + 1) * NB].rearrange("p (t a k) -> p k t a", a=2, k=KEYS)
                    V.tensor_reduce(gates[half][:, :, at:at + UNIT // FILLS], sums, AX.X, ALU.add).then_inc(gate_out, 1)

            def pair(i, c, step0, tile, units, unit0):
                for e in range(2):
                    unit = unit0 + e * units
                    if tile is not None and isinstance(tile, int) and tile + c + e == 0:
                        hot_rows(0, 0)
                        hot_rows(0, 1)
                    if tile is None:
                        parts_here = parts[3 * (2 * c + e):3 * (2 * c + e) + 3]
                    elif not isinstance(i, int) or i < TILES:
                        parts_here = parts[2 * c + e:2 * c + e + 1]
                    else:
                        parts_here = ()
                    for part in parts_here:
                        part(i)
                    for k in range(max(units - 1, 0)):
                        take_gates(tile, unit + k)
                        if closes(i, c, e) and k == 0:
                            gate_parts(i)
                        ahead(hot_rows, i, tile, unit + k + 2)
                    if has_next(step0 + e):
                        u_lo(e, step0 + e + 2)
                    for k in range(max(units - 1, 0), units):
                        take_gates(tile, unit + k)
                        if closes(i, c, e) and k == 0:
                            gate_parts(i)
                        ahead(hot_rows, i, tile, unit + k + 2)

            def gate_parts(i):
                dve.wait_ge(routeT_ready, i + 1)
                chain.link(V.tensor_copy(gate_part[0][:, :], routeT[:, 2, :]))
                chain.link(V.tensor_tensor(gate_part[1][:, :], routeT[:, 2, :], gate_scalar[0], ALU.subtract))
                chain.clear()

            for e in range(2):
                u_lo(e, e)
            over_rounds(dve, pair, gate_parts)


def load_v(sp, d, keep, step, e):
    v_view = d["peer_v"].rearrange("a (k1 k2) n -> (a k1) k2 n", k2=KEYS)
    sp.dma_start(keep["raw_rows"][:, e, :], one2(v_view, step)).then_inc(keep["v_in"][e], 16)


def outputs(nc, d, keep):
    G4 = 4
    GROUPS = KEYS // G4
    with ExitStack() as ctx:
        sb = lambda n, s, t=F32: ctx.enter_context(nc.sbuf_tensor(n, s, t))
        sem = lambda n: ctx.enter_context(nc.semaphore(n))
        ps = lambda n, w: ctx.enter_context(nc.psum_tensor(n, [P, w], F32))
        acc = keep["acc"]
        v_raw, v_in = keep["raw_rows"], keep["v_in"]
        hid = sb("hid_back", [P, 2, SEQ])
        gate = sb("gate", [P, 2, PIECES, 2, HALF_T])
        a_part = (sb("act_hi", [P, 2, G4, SEQ], F32R), sb("act_lo", [P, 2, G4, SEQ], F32R))
        v_part = (sb("v_hi", [P, 2, G4, D], F32R), sb("v_lo", [P, 2, G4, D], F32R))
        ps_a = [ps(f"ps_a{e}", 2 * NB) for e in range(2)]
        ps_y = [ps(f"ps_y{b}", NB) for b in range(4)]
        h_in = [sem(f"hid_in{b}") for b in range(2)]
        g_in = [sem(f"gate_in{b}") for b in range(2)]
        vhi_ready, vlo_ready = sem("vhi_ready"), sem("vlo_ready")
        gated, ahi_ready, alo_ready = sem("gated"), sem("ahi_ready"), sem("alo_ready")
        y_done, y_added = sem("y_done2"), sem("y_added")
        gate2, ln_g, ln_b = sb("gate2", [P, D]), sb("ln2_gain", [P, D]), sb("ln2_bias", [P, D])
        stats, mv = sb("stats2", [P, TILES, 2, 6]), sb("mean_var2", [P, TILES, 2])
        rstd, power = sb("rstd2", [P, TILES, 2]), sb("power2", [P, 1])
        rows_in, power_set = sem("final_rows_in"), sem("power_set")
        x1_in = [sem(f"x1_in{k}") for k in range(TILES // 2)]
        y_gated, x1_scaled, var_ready, rstd_ready = sem("y_gated"), sem("x1_scaled"), sem("var2_ready"), sem("rstd2_ready")
        centred, scaled, out_ready, out_stored = sem("centred"), sem("scaled"), sem("out_ready"), sem("out_stored")
        dve_chain = sem("dve_chain4")
        block = ctx.enter_context(nc.Block())
        g_view = d["gates_keep"].rearrange("c p (m k t) -> p m c k t", k=2, t=HALF_T)
        hid_view = d["hid_keep"].rearrange("k2 p t -> p k2 t")
        YP = 2 * TILES
        BESIDE = (0, YP // 4, YP // 2, 3 * YP // 4, YP - 2, YP)
        LAST = (GROUPS - 1) * YP
        x1_rows = (gate[:, 0].rearrange("p c k t -> p (c k t)").rearrange("p (t n) -> p t n", n=D), hid[:, :, :],
                   gate[:, 1].rearrange("p c k t -> p (c k t)").rearrange("p (t n) -> p t n", n=D), v_raw[:, :, :])

        @block.sync
        def _(sp):
            def body(g, slot):
                for e in range(G4):
                    step, raw, pr = G4 * g + e, e % 2, e // 2
                    if at_least(step, 2):
                        sp.wait_ge(gated, step - 1)
                    sp.dma_start(hid[:, raw, :], one2(hid_view, step)).then_inc(h_in[raw], 16)
                    if e % 2 == 0:
                        if at_least(g, 1):
                            sp.wait_ge(gated, G4 * (g - 1) + e + 2)
                        sp.dma_start(gate[:, pr, :, :, :].rearrange("p c k t -> p c (k t)"),
                                     one_pair(g_view, 2 * g + pr)).then_inc(g_in[pr], 16)
                    if at_least(step, 2):
                        sp.wait_ge(vlo_ready, step - 1)
                        load_v(sp, d, keep, step, raw)
            in_pairs(sp, GROUPS, body)
            for dst, src in ((gate2, d["gate2_keep"]), (ln_g, d["ln2_g"].to_broadcast([P, D])), (ln_b, d["ln2_b"].to_broadcast([P, D]))):
                sp.dma_start(dst[:, :], src).then_inc(rows_in, 16)
            for k in range(TILES // 2):
                sp.wait_ge(*((gated, KEYS - 2), (gated, KEYS), (gated, KEYS), (vlo_ready, KEYS))[k])
                sp.dma_start(x1_rows[k], d["x1_keep"].rearrange("t p n -> p t n")[:, 2 * k:2 * k + 2]).then_inc(x1_in[k], 16)
            for t in range(TILES):
                sp.wait_ge(out_ready, t + 1)
                sp.dma_start(d["out"].rearrange("a (t p) n -> (a t) p n", p=P)[t], acc[:, t, :]).then_inc(out_stored, 16)
            sp.wait_ge(out_stored, 16 * TILES)

        @block.gpsimd
        def _(pool):
            def body(g, slot):
                for e in range(G4):
                    step = G4 * g + e
                    pool.wait_ge(vhi_ready, step + 1)
                    nc.gpsimd.tensor_tensor(v_part[1][:, slot, e, :], v_raw[:, e % 2, :], v_part[0][:, slot, e, :].bitcast(F32), ALU.subtract).then_inc(vlo_ready, 1)
            in_pairs(pool, GROUPS, body)
            nc.gpsimd.memset(power[:, :], -0.5).then_inc(power_set, 1)
            pool.wait_ge(power_set, 1)
            pool.wait_ge(rows_in, 48)
            for n in range(TILES + 2):
                if n < TILES:
                    pool.wait_ge(y_added, LAST + 2 * n + 2)
                    nc.gpsimd.tensor_tensor(acc[:, n, :], acc[:, n, :], gate2[:, :], ALU.mult).then_inc(y_gated, 1)
                if 1 <= n < TILES + 1:
                    pool.wait_ge(var_ready, n)
                    nc.gpsimd.tensor_tensor(rstd[:, n - 1, 0:1], rstd[:, n - 1, 1:2], power[:, :], ALU.pow).then_inc(rstd_ready, 1)
                if n >= 2:
                    t = n - 2
                    pool.wait_ge(scaled, t + 1)
                    nc.gpsimd.tensor_tensor(acc[:, t, :], acc[:, t, :], ln_b[:, :], ALU.add).then_inc(out_ready, 1)

        @block.scalar
        def _(act):
            def body(g, slot):
                for e in range(G4):
                    step, raw = G4 * g + e, e % 2
                    act.wait_ge(v_in[raw], 16 * (2 * g + e // 2) + 16)
                    if at_least(g, 2) and e == 0:
                        act.wait_ge(y_done, (g - 1) * YP)
                    nc.scalar.activation(v_part[0][:, slot, e, :], v_raw[:, raw, :], ACT.Copy).then_inc(vhi_ready, 1)
                    act.wait_ge(gated, step + 1)
                    nc.scalar.activation(a_part[0][:, slot, e, :], ps_a[raw][:, :], ACT.Copy).then_inc(ahi_ready, 1)
            in_pairs(act, GROUPS, body)
            act.wait_ge(alo_ready, KEYS)
            for n in range(TILES + 1):
                if n < TILES:
                    act.wait_ge(x1_in[n // 2], 16)
                    if n >= 2:
                        act.wait_ge(centred, n - 1)
                    nc.scalar.activation(ps_a[n % 2][:, :], x1_rows[n // 2][:, n % 2, :], ACT.Copy, scale=ALPHA).then_inc(x1_scaled, 1)
                if n:
                    t = n - 1
                    act.wait_ge(rstd_ready, t + 1)
                    act.wait_ge(centred, t + 1)
                    nc.scalar.activation(acc[:, t, :], acc[:, t, :], ACT.Copy, scale=rstd[:, t, 0:1]).then_inc(scaled, 1)

        @block.tensor
        def _(pe):
            def products(slot, q, e):
                t, half = q // 2, q % 2
                for n, (a, b) in enumerate(((0, 0), (0, 1), (1, 0))):
                    last = nc.tensor.matmul(ps_y[q % 4][:, :], a_part[a][:, slot, e, t * P:(t + 1) * P],
                                            v_part[b][:, slot, e, half * NB:(half + 1) * NB],
                                            start=(e == 0 and n == 0), stop=(e == G4 - 1 and n == 2))
                if e == G4 - 1:
                    last.then_inc(y_done, 1)

            def body(g, slot):
                ahead = 0
                if isinstance(g, int) and g == 0:
                    for e in range(G4):
                        pe.wait_ge(alo_ready, e + 1)
                        pe.wait_ge(vlo_ready, e + 1)
                        for q in range(4):
                            products(slot, q, e)
                    ahead = 2
                else:
                    pe.wait_ge(alo_ready, G4 * g + G4)
                    pe.wait_ge(vlo_ready, G4 * g + G4)
                for t in range(ahead, TILES):
                    pe.wait_ge(y_added, g * YP + 2 * t - 2)
                    for half in range(2):
                        for e in range(G4):
                            products(slot, 2 * t + half, e)
            in_pairs(pe, GROUPS, body)

        @block.vector
        def _(dve):
            V = nc.vector

            def add_out(g, q):
                t, half = q // 2, q % 2
                dve.wait_ge(y_done, g * YP + q + 1)
                if q == 0 and at_least(g, 1):
                    dve.wait_ge(y_added, g * YP)
                dst = acc[:, t, half * NB:(half + 1) * NB]
                if at_least(g, 1):
                    V.tensor_tensor(dst, ps_y[q % 4][:, :], dst, ALU.add).then_inc(y_added, 1)
                else:
                    V.tensor_copy(dst, ps_y[q % 4][:, :]).then_inc(y_added, 1)

            def body(g, slot):
                for e in range(G4):
                    step, raw, pr = G4 * g + e, e % 2, e // 2
                    dve.wait_ge(h_in[raw], 16 * (2 * g + pr) + 16)
                    dve.wait_ge(g_in[pr], 16 * g + 16)
                    if at_least(step, 2):
                        dve.wait_ge(alo_ready, step - 1)
                    V.tensor_tensor(ps_a[raw][:, :].rearrange("p (c t) -> p c t", t=HALF_T), hid[:, raw, :].rearrange("p (c t) -> p c t", t=HALF_T),
                                    gate[:, pr, :, e % 2, :], ALU.mult).then_inc(gated, 1)
                    for q in range(BESIDE[e], BESIDE[e + 1]):
                        if at_least(g, 1):
                            add_out(g - 1, q)
                    dve.wait_ge(ahi_ready, step + 1)
                    V.tensor_tensor(a_part[1][:, slot, e, :], ps_a[raw][:, :], a_part[0][:, slot, e, :].bitcast(F32), ALU.subtract).then_inc(alo_ready, 1)

                for q in range(BESIDE[G4], YP):
                    if at_least(g, 1):
                        add_out(g - 1, q)

            chain = Chain(dve, dve_chain)

            def norm(t):
                z = ps_a[t % 2]
                dve.wait_ge(x1_scaled, t + 1)
                dve.wait_ge(y_gated, t + 1)
                chain.link(V.tensor_tensor(z[:, :], z[:, :], acc[:, t, :], ALU.add))
                V.bn_stats(stats[:, t, 0, :], z[:, 0:NB])
                chain.link(V.bn_stats(stats[:, t, 1, :], z[:, NB:D]))
                chain.link(V.bn_aggr(mv[:, t, :], stats[:, t, :, :]))
                V.tensor_scalar_add(rstd[:, t, 1:2], mv[:, t, 1:2], EPS).then_inc(var_ready, 1)
                V.scalar_tensor_tensor(acc[:, t, :], z[:, :], mv[:, t, 0:1], ln_g[:, :], ALU.subtract, ALU.mult).then_inc(centred, 1)

            in_pairs(dve, GROUPS, body)
            dve.wait_ge(rows_in, 48)
            for t in range(TILES):
                add_out(GROUPS - 1, 2 * t)
                add_out(GROUPS - 1, 2 * t + 1)
                if t:
                    norm(t - 1)
            norm(TILES - 1)


def one2(view, n):
    return view[:, n, :] if isinstance(n, int) else view[:, bass.ds(n, 1), :].rearrange("p a n -> p (a n)")


def one_pair(view, n):
    part = view[:, n] if isinstance(n, int) else view[:, bass.ds(n, 1)].rearrange("p m c k t -> p (m c) k t")
    return part.rearrange("p c k t -> p c (k t)")


def build(nc, d):
    d["gate2_keep"] = nc.dram_tensor("gate2_keep", [P, D], F32, kind="Internal").ap()
    d["x1_keep"] = nc.dram_tensor("x1_keep", [TILES, P, D], F32, kind="Internal").ap()
    d["scores_keep"] = nc.dram_tensor("scores_keep", [TILES, P, NQ * KEYS], F32, kind="Internal").ap()
    d["hid_keep"] = nc.dram_tensor("hid_keep", [KEYS, P, SEQ], F32, kind="Internal").ap()
    d["gates_keep"] = nc.dram_tensor("gates_keep", [PIECES, P, KEYS * HALF_T], F32, kind="Internal").ap()
    keep = {}
    with ExitStack() as ctx:
        sb = lambda n, s, t=F32: ctx.enter_context(nc.sbuf_tensor(n, s, t))
        keep["h2T"] = keep["acc"] = sb("h2T_then_sums", [P, DC, SEQ])
        with nc.sbuf_tensor("const", [P, C_WIDTH], F32) as const:
            keep["const"] = const
            with ExitStack() as mix:
                msb = lambda n, s: mix.enter_context(nc.sbuf_tensor(n, s, F32))
                keep["mod"], keep["pool_col"] = msb("mod", [P, 6, D]), msb("pool_col", [P, PG])
                keep["w_in"], keep["w_out"] = msb("w_in", [P, DC, QW + 2 * KVW + PW]), msb("w_out", [P, DC, D])
                keep["mix_const"] = msb("mix_const", [P, M_WIDTH])
                keep["mix_in"] = mix.enter_context(nc.semaphore("mix_weights_in"))
                modulation(nc, d, keep)
                mixing(nc, d, keep)
            with nc.sbuf_tensor("raw_rows", [P, 2, D], F32) as raw_rows:
                keep["raw_rows"] = raw_rows
                keep["u_in"] = [ctx.enter_context(nc.semaphore(f"u_in{b}")) for b in range(2)]
                keep["v_in"] = [ctx.enter_context(nc.semaphore(f"v_in{b}")) for b in range(2)]
                with nc.sbuf_tensor("h_hi", [P, DC, SEQ], F32R) as h_hi, nc.sbuf_tensor("h_lo", [P, DC, SEQ], F32R) as h_lo:
                    keep["h_hi"], keep["h_lo"] = h_hi, h_lo
                    queries(nc, d, keep)
                    routing(nc, d, keep)
                outputs(nc, d, keep)


_INS = ['x', 'c', 'w_ada', 'b_ada', 'w_in', 'attn_sinks', 'w_pool', 'pool_scale', 'w_out', 'ln1_g', 'ln1_b',
        'w_pq', 'peer_k1', 'peer_k2', 'peer_u', 'peer_v', 'ln2_g', 'ln2_b']


def shape_constants():
    import numpy as np
    k, m = np.zeros((P, C_WIDTH), np.float32), np.zeros((P, M_WIDTH), np.float32)
    k[:, C_IDENT:C_IDENT + P] = np.eye(P)
    q, s = np.arange(P)[:, None], np.arange(2 * P)[None, :]
    rel = q + P - s
    band = (rel >= 0) & (rel < P)
    m[:, M_MASK:M_MASK + 2 * P] = np.where(band & (s >= P), 0.0, NEG)
    m[:, M_MASK + 2 * P:M_MASK + 4 * P] = np.where(band, 0.0, NEG)
    s, t = np.arange(P)[:, None], np.arange(P)[None, :]
    for g, w in enumerate(POOLS):
        own = (s <= t) & (t - s < w)
        prev = t + P - s < w
        first = np.where(own, 1.0 / np.minimum(t + 1, w), 0.0) - (s == t)
        for n, band_of in enumerate((first, own / w - (s == t), prev / w)):
            at = M_BAND + (3 * g + n) * P
            m[:, at:at + P] = band_of
    k[:, C_IOTA:C_IOTA + P] = np.arange(P)
    starts = np.array(ROW_START, np.float32)
    k[:, C_START:C_START + NTH] = starts[1:]
    k[:, C_DSTART:C_DSTART + NTH] = starts[1:] - starts[:-1]
    freqs = np.float32(10000.0) ** (-np.arange(HALF, dtype=np.float32) / np.float32(HALF))
    ang = np.arange(SEQ, dtype=np.float32)[:, None] * freqs[None, :]
    for at, f in ((M_COS, np.cos), (M_SIN, np.sin)):
        tab = f(ang).astype(np.float32).reshape(TILES, P, HALF).transpose(1, 0, 2)
        m[:, at:at + TILES * HALF] = tab.reshape(P, TILES * HALF)
    return {"const": k, "mix_const": m}


def kernel(**inputs):
    import numpy as _np
    import concourse.bacc as _bacc
    from concourse import mybir as _mybir
    from concourse.bass_utils import run_bass_kernel_spmd as _run

    nc = _bacc.Bacc("TRN2", target_bir_lowering=False, num_devices=1)
    arrays, d = {}, {}
    for name in _INS:
        a = _np.ascontiguousarray(inputs[name])
        arrays[f"in_{name}_dram"] = a
        d[name] = nc.dram_tensor(f"in_{name}_dram", a.shape, _mybir.dt.from_np(a.dtype), kind="ExternalInput").ap()
    for name, a in shape_constants().items():
        arrays[f"{name}_dram"] = a
        d[name] = nc.dram_tensor(f"{name}_dram", a.shape, F32, kind="ExternalInput").ap()
    d["out"] = nc.dram_tensor("out_0_dram", (1, SEQ, D), F32, kind="ExternalOutput").ap()
    build(nc, d)
    r = _run(nc, [arrays], core_ids=[0])
    return r.results[0]["out_0_dram"]
```
